# Optimizing a Trainium2 kernel written in Bass

```python
import math
import jax, jax.numpy as jnp
from jax import lax
import numpy as np

"""One inference step of a hybrid decoder trunk (post-LN DeepNorm, DEPTH layers).

Each layer has three sub-layers, each followed by x <- LayerNorm(ALPHA * x + f(x)):
  1. parallel head-group mixer: one combined input projection whose columns are split among
     a Griffin RG-LRU group (gelu gate branch + causal conv4 + RG-LRU, D_REC channels, 8 heads)
     and a Conformer convolution group (GLU -> causal depthwise conv31 -> LayerNorm -> swish,
     D_CONV channels); the two outputs are concatenated into one output projection.
  2. cross-attention (4 heads) into 256 memory tokens.
  3. DeepSeek-V3 style MoE: sigmoid, group-limited top-8 of 64 SwiGLU experts + 1 shared expert.

Inputs:
  x_prompt (BATCH, SEQ, D_MODEL), x_sample (DEC_BATCH, DEC_SEQ, D_MODEL), mem_prompt (BATCH, N_MEM, D_MODEL)
  state_rglru_h (DEPTH, DEC_BATCH, D_REC)             RG-LRU hidden state
  state_rglru_conv (DEPTH, DEC_BATCH, 3, D_REC)        last 3 inputs of the width-4 conv
  state_dwconv (DEPTH, DEC_BATCH, 30, D_CONV)          last 30 GLU outputs for the width-31 conv
  cache_mem_k / cache_mem_v (DEPTH, DEC_BATCH, N_MEM, XA_HEADS, XA_HEAD_DIM)  memory keys / values
  followed by the per-layer weights (leading DEPTH axis).
Output tuple:
  (y_prompt (BATCH, SEQ, D_MODEL), y_sample (DEC_BATCH, DEC_SEQ, D_MODEL),
   new_rglru_h_prompt (DEPTH, BATCH, D_REC), new_rglru_conv_prompt (DEPTH, BATCH, 3, D_REC),
   new_dwconv_prompt (DEPTH, BATCH, 30, D_CONV),
   new_mem_k_prompt (DEPTH, BATCH, N_MEM, XA_HEADS, XA_HEAD_DIM), new_mem_v_prompt (same),
   new_rglru_h_sample (DEPTH, DEC_BATCH, D_REC), new_rglru_conv_sample (DEPTH, DEC_BATCH, 3, D_REC),
   new_dwconv_sample (DEPTH, DEC_BATCH, 30, D_CONV))
"""

D_MODEL = 1024
BATCH = 1
SEQ = 512
DEPTH = 1
DEC_BATCH = 8
DEC_SEQ = 1
PAST_LEN = 4096
PAGE_SIZE = 128

D_MIX = D_MODEL
D_REC = D_MIX // 2
D_CONV = D_MIX - D_REC
REC_HEADS = 8
REC_HEAD_DIM = D_REC // REC_HEADS
REC_CONV_W = 4
RG_C = 8.0
CONF_CONV_W = 31
N_MEM = 256
XA_HEADS = 4
XA_HEAD_DIM = D_MODEL // XA_HEADS
N_EXPERTS = 64
TOP_K = 8
N_GROUPS = 8
TOPK_GROUPS = 4
D_EXPERT = D_MODEL // 4
D_SHARED = D_EXPERT
ROUTED_SCALE = 2.5
EXPERT_BLOCK = 128
LN_EPS = 1e-5
ALPHA = (2 * DEPTH) ** 0.25
BETA = (8 * DEPTH) ** -0.25

kernel_name = 'hymba_griffin_conformer_moe_decoder_step'

def layer_norm(x, g, b):
    xf = x.astype(jnp.float32)
    mu = jnp.mean(xf, axis=-1, keepdims=True)
    var = jnp.mean(jnp.square(xf - mu), axis=-1, keepdims=True)
    return ((xf - mu) * lax.rsqrt(var + LN_EPS) * g.astype(jnp.float32) + b.astype(jnp.float32)).astype(x.dtype)

def causal_dwconv(u, buf, w, b):
    ext = jnp.concatenate([buf.astype(u.dtype), u], axis=1)
    y = lax.conv_general_dilated(ext, w[:, None, :].astype(u.dtype), window_strides=(1,), padding='VALID',
                                 dimension_numbers=('NWC', 'WIO', 'NWC'), feature_group_count=u.shape[-1])
    return y + b.astype(u.dtype), ext[:, ext.shape[1] - (w.shape[0] - 1):]

def block_diag(u, w, b):
    n, l, _ = u.shape
    uh = u.reshape(n, l, REC_HEADS, REC_HEAD_DIM)
    return jnp.einsum('nlhi,hij->nlhj', uh, w.astype(u.dtype)).reshape(n, l, -1) + b.astype(u.dtype)

def rglru(u, h0, w_a, b_a, w_x, b_x, lam):
    uf = u.astype(jnp.float32)
    r = jax.nn.sigmoid(block_diag(uf, w_a.astype(jnp.float32), b_a.astype(jnp.float32)))
    i = jax.nn.sigmoid(block_diag(uf, w_x.astype(jnp.float32), b_x.astype(jnp.float32)))
    log_a = -RG_C * r * jax.nn.softplus(-lam.astype(jnp.float32))
    a = jnp.exp(log_a)
    bterm = jnp.sqrt(-jnp.expm1(2.0 * log_a)) * (i * uf)
    bterm = bterm.at[:, 0].add(a[:, 0] * h0.astype(jnp.float32))

    def combine(left, right):
        a1, b1 = left
        a2, b2 = right
        return a1 * a2, a2 * b1 + b2

    _, h = lax.associative_scan(combine, (a, bterm), axis=1)
    return h, h[:, -1]

def cross_attn(x, k, v, w_q, w_o):
    n, l, _ = x.shape
    q = (x @ w_q).reshape(n, l, XA_HEADS, XA_HEAD_DIM)
    s = jnp.einsum('nlhd,nmhd->nhlm', q, k.astype(x.dtype)).astype(jnp.float32) * (XA_HEAD_DIM ** -0.5)
    p = jax.nn.softmax(s, axis=-1).astype(x.dtype)
    o = jnp.einsum('nhlm,nmhd->nlhd', p, v.astype(x.dtype)).reshape(n, l, XA_HEADS * XA_HEAD_DIM)
    return o @ w_o

def swiglu(x, w1, w3, w2):
    return (jax.nn.silu(x @ w1) * (x @ w3)) @ w2

def routed_experts(xf, idx, gates, w1_e, w3_e, w2_e):
    t, d = xf.shape
    n_assign = t * TOP_K
    flat_e = idx.reshape(-1)
    order = jnp.argsort(flat_e, stable=True)
    e_sorted = flat_e[order]
    tok_sorted = (order // TOP_K).astype(jnp.int32)
    gate_sorted = gates.reshape(-1)[order]
    counts = jnp.bincount(flat_e, length=N_EXPERTS)
    padded = (counts + EXPERT_BLOCK - 1) // EXPERT_BLOCK * EXPERT_BLOCK
    pad_end = jnp.cumsum(padded)
    pad_start = pad_end - padded
    start = jnp.cumsum(counts) - counts
    dest = pad_start[e_sorted] + jnp.arange(n_assign, dtype=jnp.int32) - start[e_sorted]
    n_blocks = (n_assign + N_EXPERTS * (EXPERT_BLOCK - 1) + EXPERT_BLOCK - 1) // EXPERT_BLOCK
    n_rows = n_blocks * EXPERT_BLOCK
    slot_tok = jnp.full((n_rows,), t, jnp.int32).at[dest].set(tok_sorted)
    slot_gate = jnp.zeros((n_rows,), jnp.float32).at[dest].set(gate_sorted)
    block_e = jnp.minimum(jnp.searchsorted(pad_end, jnp.arange(n_blocks, dtype=jnp.int32) * EXPERT_BLOCK, side='right'),
                          N_EXPERTS - 1)
    xpad = jnp.concatenate([xf, jnp.zeros((1, d), xf.dtype)], axis=0)

    def run_block(args):
        e, toks, g = args
        xb = xpad[toks]
        hb = jax.nn.silu(xb @ w1_e[e]) * (xb @ w3_e[e])
        return (hb @ w2_e[e]) * g[:, None].astype(xb.dtype)

    yb = lax.map(run_block, (block_e, slot_tok.reshape(n_blocks, EXPERT_BLOCK), slot_gate.reshape(n_blocks, EXPERT_BLOCK)))
    out = jnp.zeros((t + 1, d), xf.dtype).at[slot_tok].add(yb.reshape(n_rows, d))
    return out[:t]

def moe(x, w_router, router_bias, w1_e, w3_e, w2_e, w1_s, w3_s, w2_s):
    n, l, d = x.shape
    xf = x.reshape(n * l, d)
    t = xf.shape[0]
    scores = jax.nn.sigmoid(xf.astype(jnp.float32) @ w_router.astype(jnp.float32))
    biased = scores + router_bias.astype(jnp.float32)
    grp = biased.reshape(t, N_GROUPS, N_EXPERTS // N_GROUPS)
    grp_score = jnp.sum(lax.top_k(grp, 2)[0], axis=-1)
    _, top_g = lax.top_k(grp_score, TOPK_GROUPS)
    gmask = jnp.any(top_g[:, :, None] == jnp.arange(N_GROUPS)[None, None, :], axis=1)
    emask = jnp.repeat(gmask, N_EXPERTS // N_GROUPS, axis=1)
    _, idx = lax.top_k(jnp.where(emask, biased, -jnp.inf), TOP_K)
    w_sel = jnp.take_along_axis(scores, idx, axis=1)
    gates = w_sel / jnp.sum(w_sel, axis=-1, keepdims=True) * ROUTED_SCALE
    y = swiglu(xf, w1_s, w3_s, w2_s) + routed_experts(xf, idx, gates, w1_e, w3_e, w2_e)
    return y.reshape(n, l, d)

def decoder_layer(x, mem_k, mem_v, h0, buf_a, buf_b, p):
    z = x @ p['w_in'] + p['b_in']
    g, u, v, gg = jnp.split(z, [D_REC, 2 * D_REC, 2 * D_REC + D_CONV], axis=-1)
    u_c, new_buf_a = causal_dwconv(u, buf_a, p['w_conv_a'], p['b_conv_a'])
    h, h_last = rglru(u_c, h0, p['w_rg_a'], p['b_rg_a'], p['w_rg_x'], p['b_rg_x'], p['rg_lambda'])
    y_a = jax.nn.gelu(g) * h.astype(x.dtype)
    glu = v * jax.nn.sigmoid(gg)
    c, new_buf_b = causal_dwconv(glu, buf_b, p['w_conv_b'], p['b_conv_b'])
    y_b = jax.nn.silu(layer_norm(c, p['ln_c_g'], p['ln_c_b']))
    mix = jnp.concatenate([y_a, y_b], axis=-1) @ p['w_out']
    x = layer_norm(ALPHA * x + mix, p['ln1_g'], p['ln1_b'])
    x = layer_norm(ALPHA * x + cross_attn(x, mem_k, mem_v, p['w_q'], p['w_o']), p['ln2_g'], p['ln2_b'])
    f = moe(x, p['w_router'], p['router_bias'], p['w1_e'], p['w3_e'], p['w2_e'], p['w1_s'], p['w3_s'], p['w2_s'])
    x = layer_norm(ALPHA * x + f, p['ln3_g'], p['ln3_b'])
    return x, h_last.astype(h0.dtype), new_buf_a, new_buf_b

def setup_inputs(seed: int = 0) -> dict:
    key = jax.random.key(seed)
    ks = iter(jax.random.split(key, 48))

    def nrm(shape, scale):
        return jax.random.normal(next(ks), shape, jnp.float32) * scale

    def gain(shape):
        return 1.0 + nrm(shape, 0.02)

    u_a = jax.random.uniform(next(ks), (DEPTH, D_REC), jnp.float32, minval=0.9, maxval=0.999)
    a_base = u_a ** (1.0 / RG_C)
    rg_lambda = jnp.log(a_base) - jnp.log1p(-a_base)
    return {
        'x_prompt': nrm((BATCH, SEQ, D_MODEL), 1.0),
        'x_sample': nrm((DEC_BATCH, DEC_SEQ, D_MODEL), 1.0),
        'mem_prompt': nrm((BATCH, N_MEM, D_MODEL), 1.0),
        'state_rglru_h': nrm((DEPTH, DEC_BATCH, D_REC), 0.5),
        'state_rglru_conv': nrm((DEPTH, DEC_BATCH, REC_CONV_W - 1, D_REC), 1.0),
        'state_dwconv': nrm((DEPTH, DEC_BATCH, CONF_CONV_W - 1, D_CONV), 0.5),
        'cache_mem_k': nrm((DEPTH, DEC_BATCH, N_MEM, XA_HEADS, XA_HEAD_DIM), 1.0),
        'cache_mem_v': nrm((DEPTH, DEC_BATCH, N_MEM, XA_HEADS, XA_HEAD_DIM), BETA),
        'w_in': nrm((DEPTH, D_MODEL, 2 * D_REC + 2 * D_CONV), D_MODEL ** -0.5),
        'b_in': nrm((DEPTH, 2 * D_REC + 2 * D_CONV), 0.02),
        'w_conv_a': nrm((DEPTH, REC_CONV_W, D_REC), REC_CONV_W ** -0.5),
        'b_conv_a': nrm((DEPTH, D_REC), 0.02),
        'w_rg_a': nrm((DEPTH, REC_HEADS, REC_HEAD_DIM, REC_HEAD_DIM), REC_HEAD_DIM ** -0.5),
        'b_rg_a': nrm((DEPTH, D_REC), 0.02),
        'w_rg_x': nrm((DEPTH, REC_HEADS, REC_HEAD_DIM, REC_HEAD_DIM), REC_HEAD_DIM ** -0.5),
        'b_rg_x': nrm((DEPTH, D_REC), 0.02),
        'rg_lambda': rg_lambda,
        'w_conv_b': nrm((DEPTH, CONF_CONV_W, D_CONV), CONF_CONV_W ** -0.5),
        'b_conv_b': nrm((DEPTH, D_CONV), 0.02),
        'ln_c_g': gain((DEPTH, D_CONV)),
        'ln_c_b': nrm((DEPTH, D_CONV), 0.02),
        'w_out': nrm((DEPTH, D_MIX, D_MODEL), BETA * D_MIX ** -0.5),
        'ln1_g': gain((DEPTH, D_MODEL)),
        'ln1_b': nrm((DEPTH, D_MODEL), 0.02),
        'w_q': nrm((DEPTH, D_MODEL, XA_HEADS * XA_HEAD_DIM), D_MODEL ** -0.5),
        'w_k': nrm((DEPTH, D_MODEL, XA_HEADS * XA_HEAD_DIM), D_MODEL ** -0.5),
        'w_v': nrm((DEPTH, D_MODEL, XA_HEADS * XA_HEAD_DIM), BETA * D_MODEL ** -0.5),
        'w_o': nrm((DEPTH, XA_HEADS * XA_HEAD_DIM, D_MODEL), BETA * (XA_HEADS * XA_HEAD_DIM) ** -0.5),
        'ln2_g': gain((DEPTH, D_MODEL)),
        'ln2_b': nrm((DEPTH, D_MODEL), 0.02),
        'w_router': nrm((DEPTH, D_MODEL, N_EXPERTS), D_MODEL ** -0.5),
        'router_bias': nrm((DEPTH, N_EXPERTS), 0.01),
        'w1_e': nrm((DEPTH, N_EXPERTS, D_MODEL, D_EXPERT), D_MODEL ** -0.5),
        'w3_e': nrm((DEPTH, N_EXPERTS, D_MODEL, D_EXPERT), D_MODEL ** -0.5),
        'w2_e': nrm((DEPTH, N_EXPERTS, D_EXPERT, D_MODEL), BETA * D_EXPERT ** -0.5),
        'w1_s': nrm((DEPTH, D_MODEL, D_SHARED), D_MODEL ** -0.5),
        'w3_s': nrm((DEPTH, D_MODEL, D_SHARED), D_MODEL ** -0.5),
        'w2_s': nrm((DEPTH, D_SHARED, D_MODEL), BETA * D_SHARED ** -0.5),
        'ln3_g': gain((DEPTH, D_MODEL)),
        'ln3_b': nrm((DEPTH, D_MODEL), 0.02),
    }

def reference(x_prompt, x_sample, mem_prompt, state_rglru_h, state_rglru_conv, state_dwconv, cache_mem_k, cache_mem_v,
              w_in, b_in, w_conv_a, b_conv_a, w_rg_a, b_rg_a, w_rg_x, b_rg_x, rg_lambda, w_conv_b, b_conv_b,
              ln_c_g, ln_c_b, w_out, ln1_g, ln1_b, w_q, w_k, w_v, w_o, ln2_g, ln2_b, w_router, router_bias,
              w1_e, w3_e, w2_e, w1_s, w3_s, w2_s, ln3_g, ln3_b):
    n_p = x_prompt.shape[0]
    n_mem = mem_prompt.shape[1]
    yp, ys = x_prompt, x_sample
    hp_l, cap_l, cbp_l, mk_l, mv_l = [], [], [], [], []
    hs_l, cas_l, cbs_l = [], [], []
    for l in range(DEPTH):
        p = dict(w_in=w_in[l], b_in=b_in[l], w_conv_a=w_conv_a[l], b_conv_a=b_conv_a[l], w_rg_a=w_rg_a[l],
                 b_rg_a=b_rg_a[l], w_rg_x=w_rg_x[l], b_rg_x=b_rg_x[l], rg_lambda=rg_lambda[l],
                 w_conv_b=w_conv_b[l], b_conv_b=b_conv_b[l], ln_c_g=ln_c_g[l], ln_c_b=ln_c_b[l],
                 w_out=w_out[l], ln1_g=ln1_g[l], ln1_b=ln1_b[l], w_q=w_q[l], w_o=w_o[l],
                 ln2_g=ln2_g[l], ln2_b=ln2_b[l], w_router=w_router[l], router_bias=router_bias[l],
                 w1_e=w1_e[l], w3_e=w3_e[l], w2_e=w2_e[l], w1_s=w1_s[l], w3_s=w3_s[l], w2_s=w2_s[l],
                 ln3_g=ln3_g[l], ln3_b=ln3_b[l])
        mk_p = (mem_prompt @ w_k[l]).reshape(n_p, n_mem, XA_HEADS, XA_HEAD_DIM)
        mv_p = (mem_prompt @ w_v[l]).reshape(n_p, n_mem, XA_HEADS, XA_HEAD_DIM)
        h0_p = jnp.zeros((n_p, D_REC), x_prompt.dtype)
        bufa_p = jnp.zeros((n_p, REC_CONV_W - 1, D_REC), x_prompt.dtype)
        bufb_p = jnp.zeros((n_p, CONF_CONV_W - 1, D_CONV), x_prompt.dtype)
        yp, hp, cap, cbp = decoder_layer(yp, mk_p, mv_p, h0_p, bufa_p, bufb_p, p)
        ys, hs, cas, cbs = decoder_layer(ys, cache_mem_k[l], cache_mem_v[l], state_rglru_h[l],
                                         state_rglru_conv[l], state_dwconv[l], p)
        hp_l.append(hp); cap_l.append(cap); cbp_l.append(cbp); mk_l.append(mk_p); mv_l.append(mv_p)
        hs_l.append(hs); cas_l.append(cas); cbs_l.append(cbs)
    return (yp, ys, jnp.stack(hp_l), jnp.stack(cap_l), jnp.stack(cbp_l), jnp.stack(mk_l), jnp.stack(mv_l),
            jnp.stack(hs_l), jnp.stack(cas_l), jnp.stack(cbs_l))


_drawn_inputs = setup_inputs


def setup_inputs(seed=0):
    import zlib

    import numpy as np

    out = dict(_drawn_inputs(seed))
    spreads = {}
    factors = {'b_rg_a': 7.859, 'b_rg_x': 5.248, 'ln_c_b': 3.501, 'ln3_g': 2.892, 'ln3_b': 2.73}
    for name, (base, spread) in spreads.items():
        noise = np.random.default_rng([zlib.crc32(name.encode()), seed]).standard_normal(out[name].shape)
        drawn = base * np.exp(spread * noise) if base else spread * noise
        out[name] = __import__('jax').numpy.asarray(drawn.astype(out[name].dtype))
    for name, factor in factors.items():
        out[name] = (out[name] * factor).astype(out[name].dtype)
    return out
```

```python
from contextlib import ExitStack
import math

import concourse.bass as bass
from concourse import mybir

ALU = mybir.AluOpType
ACT = mybir.ActivationFunctionType
AX = mybir.AxisListType
F32 = mybir.dt.float32
I32 = mybir.dt.int32
U32 = mybir.dt.uint32

P = 128
D = 1024
KC = D // P
SEQ, NS = 512, 8
T = SEQ + NS
HALF = T // 2
RC = 4
TT = 5
N_MEM, XH, XD = 256, 4, 256
E, FE, TOPK = 64, 256, 8
WA, WB = 4, 31
ALPHA = 2.0 ** 0.25
EPS = 1e-5
RG_C = 8.0
ROUTED_SCALE = 2.5
EP = E + 2
NROW = T * TOPK
FAR = 100000.0
ROUNDS = (T + P - 1) // P

PAR_SPEC = [("b_in", 16), ("w_conv_a", 16), ("b_conv_a", 4), ("b_rg_a", 4), ("b_rg_x", 4), ("rg_lambda", 4),
            ("b_conv_b", 4), ("ln_c_g", 4), ("ln_c_b", 4), ("ln1_g", 8), ("ln1_b", 8), ("ln2_g", 8), ("ln2_b", 8)]
PAR_AT = {}
_row = 0
for _n, _k in PAR_SPEC:
    PAR_AT[_n] = _row
    _row += _k
NPAR = _row

GROUPS = [("par", "V"), ("st", "V"), ("cb", "V")]
GROUPS += [(f"x{c}", "AV"[c % 2]) for c in range(KC)]
GROUPS += [(f"zv{c}", "A") for c in range(RC)] + [(f"zs{c}", "A") for c in range(RC)]
GROUPS += [(f"zu{c}", "A") for c in range(RC)] + [(f"zg{c}", "A") for c in range(RC)]
GROUPS += [("mt0", "A"), ("mt1", "A"), ("v0", "A"), ("v1", "A")]
GROUPS += [("tails", "V")]
GROUPS += [(f"ra{c}", "A") for c in range(RC)] + [(f"ri{c}", "A") for c in range(RC)]
GROUPS += [("k0", "A"), ("k1", "A"), ("kt0", "A"), ("kt1", "A")]
GROUPS += [("hlast", "V"), ("cmean", "V"), ("cvar", "A")]
GROUPS += [(f"wo{c}", "V") for c in range(KC)] + [("mean1", "V"), ("var1", "A")]
GROUPS += [(f"q{c}", "A") for c in range(KC)] + [("qs", "A")]
GROUPS += [("sc0", "A"), ("qb0", "V"), ("qb1", "V"), ("sc1", "A"), ("pt0", "A"), ("qb2", "V"), ("qb3", "V"),
           ("sc2", "A"), ("pt1", "A"), ("qb4", "V"), ("qb5", "V"), ("sc3", "A"), ("pt2", "A"), ("qb6", "V"),
           ("qb7", "V"), ("pt3", "A")]
GROUPS += [(f"o{c}", "A") for c in range(KC)] + [("ssT", "A"), ("spT", "A"), ("os", "A")]
GROUPS += [(f"xo{c}", "V") for c in range(KC)] + [("mean2", "V"), ("var2", "A")]
GROUPS += [("rt", "A")] + [(f"x2{t}", "A") for t in range(TT)]
GROUPS += [("h1a", "A"), ("h3a", "V"), ("h1b", "A"), ("h3b", "V"), ("rank", "V"), ("count", "V")]
GROUPS += [(f"so{t}", "V") for t in range(TT)]
GID = {name: g for g, (name, _) in enumerate(GROUPS)}

A0, A1, A2, A3, A4 = 0, 4160, 8320, 12480, 16640
A_SIZE = A4 + 2080


def width(t):
    return P if t < TT - 1 else NS


def decoder_step(nc: bass.Bass, ins, outs):
    I = ins
    (o_yp, o_ys, o_hp, o_cap, o_cbp, o_mk, o_mv, o_hs, o_cas, o_cbs) = outs

    with ExitStack() as ctx:
        def sb(name, shape, dt=F32):
            return ctx.enter_context(nc.sbuf_tensor(name, shape, dt))

        def sem(name):
            return ctx.enter_context(nc.semaphore(name))

        x2_rows = nc.dram_tensor("x2_rows", [T, D], F32)
        y_rows = nc.dram_tensor("y_rows", [NROW, D], F32)

        arena = sb("arena", [P, 3 * 8192])
        act_mem = sb("act_mem", [P, A_SIZE])
        kv_mem = sb("kv_mem", [P, 4096])
        mk_mem = sb("mk_mem", [P, 2048])
        ident = sb("ident", [P, P])
        mean_d = sb("mean_d", [P, P])
        mean_c = sb("mean_c", [P, P])
        ones = sb("ones", [P, P])
        par = sb("par", [P, NPAR])
        wcb = sb("wcb", [P, WB * RC])
        gate_w = sb("gate_w", [P, 2, RC, P])
        rstd = sb("rstd", [P, T])
        tail = sb("tail", [38, 2, 512])
        h0t = sb("h0t", [P, RC, NS])
        c8 = sb("c8", [P, 8, RC])
        eps_t = sb("eps_t", [P, 1])
        small = sb("small", [P, 44])
        psum = ctx.enter_context(nc.psum_tensor("psum", [P, 4, D], F32))

        def rows(at, k):
            return act_mem[:, at:at + k * T].rearrange("p (k t) -> p k t", k=k)

        def halves(ap):
            return ap.rearrange("p (h t) -> p h t", h=2)

        def col(name, c):
            return par[:, PAR_AT[name] + c:PAR_AT[name] + c + 1]

        xT = rows(A0, KC)
        gT, uT = rows(A1, RC), rows(A1 + RC * T, RC)
        gluT, rT = rows(A2, RC), rows(A2 + RC * T, RC)
        cT, ucT = rows(A3, RC), rows(A3 + RC * T, RC)
        thT = rows(A4, RC)
        x_tok = act_mem[:, A3:A3 + TT * D].rearrange("p (t n) -> p t n", t=TT)
        raw_par = act_mem[0:P, A1:A1 + P]
        raw_wcb = act_mem[0:P, A1 + P:A1 + 2 * P]
        cbT = act_mem[:, A4 + 960:A4 + 1920].rearrange("p (c n) -> p c n", c=RC)
        caT = act_mem[:, A4 + 1920:A4 + 1920 + 96].rearrange("p (c n) -> p c n", c=RC)
        cprod = act_mem[:, A4:A4 + 240].rearrange("p (b j) -> p b j", b=NS)
        csum = act_mem[:, A4 + 240:A4 + 248]
        sq = rows(A1, KC)
        sq_c = rows(A2, RC)
        st_cb = mk_mem[0:120, 0:1024].rearrange("p (r n) -> p r n", r=2)
        st_ca = mk_mem[0:24, 1024:1536]
        st_h = mk_mem[0:NS, 1536:2048]
        mem_tok = mk_mem[:, :].rearrange("p (m n) -> p m n", m=2)
        memT = kv_mem[:, 0:2048].rearrange("p (k m) -> p k m", k=KC)
        keyT = memT
        v_tok = kv_mem[:, 2048:4096].rearrange("p (m n) -> p m n", m=2)
        k_tok = mem_tok
        qT = rows(A2, KC)
        prT = rows(A1, KC)
        oT = rows(A3, KC)
        probs = act_mem[:, A4:A4 + 2048].rearrange("p (b h m) -> p b h m", b=2, h=XH)
        q_s = mk_mem[0:NS, 0:1024]
        junk = mk_mem[:, 1024:1280]
        ss = mk_mem[:, 1280:1344].rearrange("p (m n) -> p m n", m=2)
        sp = mk_mem[0:32, 1344:1600]
        spT = mk_mem[:, 1600:1664].rearrange("p (m n) -> p m n", m=2)
        base = act_mem[:, A1:A1 + TT * D].rearrange("p (t n) -> p t n", t=TT)
        ys = act_mem[:, 9280:9280 + 2048].rearrange("p (b n) -> p b n", b=2)
        silu = act_mem[:, 11328:11328 + 512].rearrange("p (b n) -> p b n", b=2)
        hid = act_mem[:, 11840:11840 + 512].rearrange("p (b n) -> p b n", b=2)
        sh1 = rows(A3, 2)
        shT = rows(A3 + 2 * T, 2)
        onehot = act_mem[:, 14560:14560 + 2 * TT * P].rearrange("p (b t s) -> p b t s", b=2, t=TT)
        hidT = act_mem[:, 15840:15840 + 512].rearrange("p (b k s) -> p b k s", b=2, k=2)
        xg = act_mem[:, 0:2048].rearrange("p (b n) -> p b n", b=2)
        xgT = act_mem[:, 2048:4096].rearrange("p (b k s) -> p b k s", b=2, k=KC)
        place = act_mem[:, A4:A4 + TT * EP].rearrange("p (t e) -> p t e", t=TT)
        table = act_mem[:, A4 + 330:A4 + 330 + 2 * TT * EP].rearrange("p (t e c) -> p t e c", t=TT, e=EP)
        NB = 4
        idx_m = act_mem[:, A4 + 994:A4 + 994 + NB]
        gate_s = act_mem[:, A4 + 998:A4 + 998 + NB]
        idx_y = sb("idx_y", [P, NB], U32)
        idx_x = sb("idx_x", [P, NB], U32)
        over = sb("over", [P, 1], I32)
        ln3g, ln3b = kv_mem[:, 0:1024], kv_mem[:, 1024:2048]
        R = [kv_mem[:, 2048 + 320 * n:2368 + 320 * n].rearrange("p (t e) -> p t e", t=TT) for n in range(6)]
        rbias = mk_mem[:, 0:64]
        rmax = mk_mem[:, 64:64 + 320].rearrange("p (t g j) -> p t g j", t=TT, g=8)
        gscore = mk_mem[:, 384:424].rearrange("p (t g) -> p t g", t=TT)
        grank = mk_mem[:, 424:464].rearrange("p (t g) -> p t g", t=TT)
        top8 = mk_mem[:, 464:504].rearrange("p (t g) -> p t g", t=TT)
        gsum = mk_mem[:, 504:509]
        row8 = mk_mem[:, 509:514]
        rmask = mk_mem[:, 514:519]
        wsum = mk_mem[:, 520:584]
        tri8 = mk_mem[:, 584:648].rearrange("p (g j) -> p g j", g=8)
        pair = mk_mem[:, 648:968].rearrange("p (t g j) -> p t g j", t=TT, g=8)
        pair2 = mk_mem[:, 968:1288].rearrange("p (t g j) -> p t g j", t=TT, g=8)
        cmax = mk_mem[:, 1288:1289]
        tri = gate_w[:, 0, 0, :]
        slots = gate_w[:, 0, 1, :]
        slots_r = gate_w[:, 0, 2, :]
        wr = gate_w[:, 1, :, :].rearrange("p c n -> p (c n)").rearrange("p (k e) -> p k e", k=KC)
        rounds_t = small[:, 38:38 + ROUNDS - 1]
        st6 = sb("st6", [P, 2, 6])
        y_in = [arena[:, 8192 * n:8192 * n + 8192].rearrange("p (j n) -> p j n", j=TOPK) for n in range(3)]

        def wslot(n):
            return arena[:, 8192 * n:8192 * n + 8192].rearrange("p (k n) -> p k n", k=KC)

        def cache(n, b):
            return arena[:, 8192 * n + 2048 * b:8192 * n + 2048 * b + 2048].rearrange("p (m n) -> p m n", m=2)

        def ew(n):
            at = 6144 * n
            return (arena[:, at:at + 4096].rearrange("p (w k n) -> p k w n", w=2, k=KC),
                    arena[:, at + 4096:at + 6144].rearrange("p (k n) -> p k n", k=2))

        w1s = arena[:, 16384:18432].rearrange("p (k n) -> p k n", k=KC)
        w3s = arena[:, 18432:20480].rearrange("p (k n) -> p k n", k=KC)
        w2s = arena[:, 20480:22528].rearrange("p (k n) -> p k n", k=2)

        s_full = sem("s_full")
        s_emA = sem("s_emA")
        s_emV = sem("s_emV")
        s_par = sem("s_par")
        s_wcbl = sem("s_wcbl")
        s_state = sem("s_state")
        s_x = sem("s_x")
        s_gw = sem("s_gw")
        s_mem = sem("s_mem")
        s_load = [sem(f"s_load{n}") for n in range(12)]
        s_out = sem("s_out")
        s_tailout = sem("s_tailout")
        s_stateout = sem("s_stateout")
        s_kout = sem("s_kout")
        s_const = sem("s_const")
        s_gwz = sem("s_gwz")
        s_late = sem("s_late")
        s_v = sem("s_v")
        s_glu = sem("s_glu")
        s_uc = sem("s_uc")
        s_convb = sem("s_convb")
        s_c8 = sem("s_c8")
        s_tanh = sem("s_tanh")
        s_srt = sem("s_srt")
        s_root = sem("s_root")
        s_h = sem("s_h")
        s_ya = sem("s_ya")
        s_sub = sem("s_sub")
        s_sq = sem("s_sq")
        s_nrm = sem("s_nrm")
        s_ln = sem("s_ln")
        s_smax = sem("s_smax")
        s_prob = sem("s_prob")
        s_ssum = sem("s_ssum")
        s_x2out = sem("s_x2out")
        s_rt = sem("s_rt")
        s_wr = sem("s_wr")
        s_c8e = sem("s_c8e")
        s_late2 = sem("s_late2")
        s_rz = sem("s_rz")
        s_done = sem("s_done")
        s_lnw = sem("s_lnw")
        s_sel = sem("s_sel")
        s_table = sem("s_table")
        s_over = sem("s_over")
        s_rowv = sem("s_rowv")
        s_abs = sem("s_abs")

        s_w = [sem(f"s_w{n}") for n in range(4)]
        m_oh = sem("m_oh")
        m_ip = sem("m_ip")
        m_idx0 = sem("m_idx0")
        m_idx = sem("m_idx")
        m_iv = sem("m_iv")
        m_g = [sem(f"m_g{n}") for n in range(2)]
        m_xt = sem("m_xt")
        m_xc = sem("m_xc")
        m_h = sem("m_h")
        m_sl = sem("m_sl")
        m_hd = sem("m_hd")
        m_ht = sem("m_ht")
        m_hc = sem("m_hc")
        m_y = sem("m_y")
        m_ya = sem("m_ya")
        m_yv = sem("m_yv")
        m_s = [sem(f"m_s{n}") for n in range(2)]
        m_z = sem("m_z")
        m_go = sem("m_go")
        f_sem = {n: sem("f_" + n) for n in ("w", "oh", "ip", "iv", "idx", "g", "xt", "xc", "h", "sl", "hd", "ht",
                                            "hc", "y", "ya", "yv", "s", "it")}
        s_yin = [sem(f"s_yin{n}") for n in range(3)]
        s_fin = sem("s_fin")
        s_sd = sem("s_sd")
        s_var = sem("s_var")
        s_res = sem("s_res")

        def emptied(eng, g):
            who = GROUPS[g][1]
            n = sum(1 for _, w in GROUPS[:g + 1] if w == who)
            eng.wait_ge(s_emA if who == "A" else s_emV, n)

        def wait_out(eng, name):
            emptied(eng, GID[name])

        def wait_full(eng, name):
            eng.wait_ge(s_full, GID[name] + 1)

        def bank(name):
            return psum[:, GID[name] % 4, :]

        def two(ap):
            return ap.rearrange("p (h n) -> p h n", h=2)[:, :, 0:HALF]

        block = ctx.enter_context(nc.Block())

        @block.sync
        def _(sp):
            at = 0
            for name, k in PAR_SPEC:
                a = I[name][0]
                src = a.rearrange("j (c p) -> (j c) p", p=P) if name == "w_conv_a" else a.rearrange("(c p) -> c p", p=P)
                sp.dma_start(raw_par[at:at + k, :], src).then_inc(s_par, 16)
                at += k
            for t in range(4):
                sp.dma_start(x_tok[:, t, :], I["x_prompt"][0, t * P:(t + 1) * P, :]).then_inc(s_x, 16)
            sp.dma_start(x_tok[0:NS, 4, :], I["x_sample"][:, 0, :]).then_inc(s_x, 16)
            w_in = I["w_in"][0].rearrange("(k p) n -> p k n", p=P)
            for k in range(0, KC, 2):
                sp.dma_start(wslot(0)[:, k:k + 2, :], w_in[:, k:k + 2, 1024:2048]).then_inc(s_load[0], 16)
            sp.dma_start(wslot(1), w_in[:, :, 0:1024]).then_inc(s_load[1], 16)

            def big(n, src):
                sp.dma_start(wslot(n % 3), src.rearrange("(k p) n -> p k n", p=P)).then_inc(s_load[n], 16)

            def big_cache(n, src, b0):
                for b in range(4):
                    sp.dma_start(cache(n % 3, b), src[0, b0 + b].rearrange("(p m) h d -> p m (h d)", m=2)).then_inc(
                        s_load[n], 16)

            big(2, I["w_v"][0])
            wait_out(sp, "cb")
            sp.dma_start(mem_tok, I["mem_prompt"][0].rearrange("(m p) n -> p m n", p=P)).then_inc(s_mem, 16)
            wait_full(sp, "zs3")
            big(3, I["w_k"][0])
            wait_full(sp, "zg3")
            big(4, I["w_out"][0])
            wait_full(sp, "v1")
            big(5, I["w_q"][0])
            for m in range(2):
                wait_out(sp, f"v{m}")
                sp.dma_start(o_mv[0, 0, m * P:(m + 1) * P].rearrange("m h d -> m (h d)"), v_tok[:, m, :]).then_inc(s_out, 16)
            wait_full(sp, "ri3")
            sp.dma_start(wr, I["w_router"][0].rearrange("(k p) e -> p k e", p=P)).then_inc(s_wr, 16)
            wait_full(sp, "k1")
            big_cache(6, I["cache_mem_k"], 0)
            wait_out(sp, "tails")
            sp.dma_start(o_cap[0, 0], tail[0:3, 0, :]).then_inc(s_tailout, 16)
            sp.dma_start(o_cas[0, :, 2, :], tail[3:11, 0, :]).then_inc(s_tailout, 16)
            sp.dma_start(o_cbp[0, 0], tail[0:30, 1, :]).then_inc(s_tailout, 16)
            sp.dma_start(o_cbs[0, :, 29, :], tail[30:38, 1, :]).then_inc(s_tailout, 16)
            for m in range(2):
                wait_out(sp, f"k{m}")
                sp.dma_start(o_mk[0, 0, m * P:(m + 1) * P].rearrange("m h d -> m (h d)"), k_tok[:, m, :]).then_inc(s_kout, 16)
            wait_out(sp, "hlast")
            sp.dma_start(o_hp[0], tail[0:1, 0, :]).then_inc(s_out, 16)
            sp.dma_start(o_hs[0], tail[1:9, 0, :]).then_inc(s_out, 16)
            wait_full(sp, "wo7")
            big_cache(7, I["cache_mem_k"], 4)
            wait_full(sp, "q7")
            big(8, I["w_o"][0])
            wait_out(sp, "qb3")
            big_cache(9, I["cache_mem_v"], 0)
            wait_out(sp, "qb7")
            big_cache(10, I["cache_mem_v"], 4)
            wait_full(sp, "xo7")
            sp.dma_start(w1s, I["w1_s"][0].rearrange("(k p) n -> p k n", p=P)).then_inc(s_load[11], 16)
            sp.dma_start(w3s, I["w3_s"][0].rearrange("(k p) n -> p k n", p=P)).then_inc(s_load[11], 16)
            sp.dma_start(w2s, I["w2_s"][0].rearrange("(k p) n -> p k n", p=P)).then_inc(s_load[11], 16)

            def expert(n, e, s):
                wu, wd = ew(n)
                sp.dma_start(wu[:, :, 0, :], I["w1_e"][0, e].rearrange("(p k) n -> p k n", k=KC)).then_inc(s, 16)
                sp.dma_start(wu[:, :, 1, :], I["w3_e"][0, e].rearrange("(p k) n -> p k n", k=KC)).then_inc(s, 16)
                sp.dma_start(wd, I["w2_e"][0, e].rearrange("(p k) n -> p k n", k=2)).then_inc(s, 16)

            expert(0, 0, s_w[0])
            expert(1, 1, s_w[1])
            wait_out(sp, "rank")
            sp.dma_start(ln3g, I["ln3_g"][0].rearrange("(a n) -> a n", a=1).broadcast_to([P, D])).then_inc(s_lnw, 16)
            sp.dma_start(ln3b, I["ln3_b"][0].rearrange("(a n) -> a n", a=1).broadcast_to([P, D])).then_inc(s_lnw, 16)
            wait_full(sp, "so4")
            expert(2, 2, s_w[2])
            expert(3, 3, s_w[3])
            with sp.Fori(0, E // 4 - 1) as i:
                for n in range(4):
                    sp.wait_ge(m_y, 4 * i + (n + 1))
                    expert(n, 4 * i + (n + 4), s_w[n])

            sp.wait_ge(s_over, 1)
            sp.wait_ge(m_y, E)
            n_max = sp.value_load(over[0:1, 0:1], min_val=0, max_val=T)
            with sp.If(n_max > P):
                with sp.Fori(1, E * (ROUNDS - 1) + 1) as i:
                    sp.wait_ge(f_sem["it"], i)
                    expert(0, (i - 1) % E, f_sem["w"])

            for p in range(2):
                sp.wait_ge(m_s[p], 16 * (E // 2))
            sp.wait_ge(s_done, 1)
            for t in range(TT):
                w = width(t)
                if t >= 3:
                    sp.wait_ge(s_rowv, t - 2)
                sp.dma_start(y_in[t % 3][0:w], y_rows[t * D:t * D + w * TOPK, :].rearrange("(p j) n -> p j n", j=TOPK)).then_inc(
                    s_yin[t % 3], 16)
            for t in range(TT):
                w = width(t)
                sp.wait_ge(s_res, t + 1)
                dst = o_yp[0, t * P:(t + 1) * P, :] if t < 4 else o_ys[:, 0, :]
                sp.dma_start(dst, base[0:w, t, :]).then_inc(s_out, 16)
            sp.wait_ge(s_out, 16 * (2 + 2 + TT))
            sp.wait_ge(s_tailout, 16 * 4)
            sp.wait_ge(s_stateout, 16 * 2)
            sp.wait_ge(s_kout, 16 * 2)

        @block.gpsimd
        def _(gp):
            gp.memset(ident[:, :], 0.0).then_inc(s_const, 1)
            gp.memset(mean_d[:, :], 1.0 / D).then_inc(s_const, 1)
            gp.memset(mean_c[:, :], 1.0 / 512).then_inc(s_const, 1)
            gp.memset(ones[:, :], 1.0).then_inc(s_const, 1)
            gp.memset(eps_t[:, :], EPS).then_inc(s_const, 1)
            gp.memset(gate_w[:, :, :, :], 0.0).then_inc(s_gwz, 1)
            gp.wait_ge(s_const, 5)
            gp.affine_select(out=ident[:, :], in_=ident[:, :], compare_op=ALU.not_equal, fill=1.0, base=0,
                             pattern=[[-1, P]], channel_multiplier=1).then_inc(s_const, 1)
            gp.wait_ge(s_gwz, 1)
            for m, name in enumerate(("w_rg_a", "w_rg_x")):
                for q in range(2):
                    gp.dma_start(gate_w[64 * q:64 * q + 64, m, :, 64 * q:64 * q + 64],
                                 I[name][0].rearrange("(c q) i j -> q i c j", q=2)[q]).then_inc(s_gw, 16)
            gp.dma_start(o_cas[0, :, 0:WA - 2, :], I["state_rglru_conv"][0, :, 1:WA - 1, :]).then_inc(s_stateout, 16)
            gp.dma_start(o_cbs[0, :, 0:WB - 2, :], I["state_dwconv"][0, :, 1:WB - 1, :]).then_inc(s_stateout, 16)
            wait_full(gp, "ri3")
            gp.memset(tri, 1.0).then_inc(s_late, 1)
            gp.iota(slots, pattern=[[1, P]], base=0, channel_multiplier=0, allow_small_or_imprecise_dtypes=True).then_inc(s_late, 1)
            gp.wait_ge(s_late, 2)
            gp.affine_select(out=tri, in_=tri, compare_op=ALU.is_gt, fill=0.0, base=0, pattern=[[1, P]],
                             channel_multiplier=-1).then_inc(s_late, 1)
            wait_out(gp, "os")
            wait_full(gp, "os")
            gp.memset(rmask, 1.0).then_inc(s_late, 1)
            gp.memset(tri8, 1.0).then_inc(s_late, 1)
            gp.iota(row8, pattern=[[TOPK * P, TT]], base=0, channel_multiplier=TOPK,
                    allow_small_or_imprecise_dtypes=True).then_inc(s_late, 1)
            gp.wait_ge(s_late, 6)
            gp.affine_select(out=rmask[:, 4:5], in_=rmask[:, 4:5], compare_op=ALU.is_gt, fill=0.0, base=NS,
                             pattern=[[0, 1]], channel_multiplier=-1).then_inc(s_late, 1)
            gp.affine_select(out=tri8, in_=tri8, compare_op=ALU.is_gt, fill=0.0, base=0, pattern=[[1, 8], [-1, 8]],
                             channel_multiplier=0).then_inc(s_late, 1)
            gp.dma_start(rbias, I["router_bias"][0].rearrange("(a n) -> a n", a=1).broadcast_to([P, E])).then_inc(s_rt, 16)
            wait_full(gp, "h3b")
            gp.iota(rounds_t, pattern=[[P, ROUNDS - 1]], base=P, channel_multiplier=0,
                    allow_small_or_imprecise_dtypes=True).then_inc(s_late, 1)
            gp.memset(xg[:, :, :], 0.0).then_inc(m_z, 1)
            gp.wait_ge(m_z, 1)
            gp.wait_ge(s_x2out, 16 * TT)

            last_x = gp.to_reg(T - 1)
            last_y = gp.to_reg(NROW - 1)

            def gather(n, b, s):
                gp.indirect_dma_start(
                    out=xg[:, b, :], out_offset=None, in_=x2_rows[:, :],
                    in_offset=bass.IndirectOffsetOnAxis(ap=idx_x[:, n:n + 1], axis=0),
                    bounds_check=last_x, oob_is_err=False).then_inc(s, 16)

            def scatter(n, b, s):
                gp.indirect_dma_start(
                    out=y_rows[:, :], out_offset=bass.IndirectOffsetOnAxis(ap=idx_y[:, n:n + 1], axis=0),
                    in_=ys[:, b, :], in_offset=None,
                    bounds_check=last_y, oob_is_err=False).then_inc(s, 16)

            def g_step(e, n):
                gp.wait_ge(s_x2out, 16 * TT)
                if isinstance(e, int) and e < 2:
                    gp.wait_ge(m_idx0, e + 1)
                else:
                    gp.wait_ge(m_idx, e - 1)
                    gp.wait_ge(m_xt, e - 1)
                    gp.sem_inc(m_go, 1)
                gather(n, n % 2, m_g[n % 2])

            def s_step(e, n):
                gp.wait_ge(s_table, 1)
                gp.wait_ge(m_ya, e + 1)
                gp.wait_ge(m_yv, e + 1)
                scatter(n, n % 2, m_s[n % 2])

            g_step(0, 0)
            g_step(1, 1)

            def step(e, k):
                g_step(e + 1, (k + 1) % 4)
                s_step(e - 1, (k - 1) % 4)

            with gp.Fori(0, E // 4 - 1) as i:
                for k in range(1, 5):
                    step(4 * i + k, k)
            for e in range(E - 3, E):
                step(e, e % 4)
            s_step(E - 1, 3)

            gp.wait_ge(s_over, 1)
            n_max = gp.value_load(over[0:1, 0:1], min_val=0, max_val=T)
            with gp.If(n_max > P):
                gp.wait_ge(m_g[0], 16 * (E // 2 + 1))
                gp.wait_ge(m_g[1], 16 * (E // 2))
                gp.wait_ge(m_s[0], 16 * (E // 2))
                gp.wait_ge(m_s[1], 16 * (E // 2))
                gp.sem_inc(f_sem["it"], 1)
                with gp.Fori(1, E * (ROUNDS - 1) + 1) as i:
                    gp.wait_ge(s_x2out, 16 * TT)
                    gp.wait_ge(f_sem["idx"], i)
                    gather(0, 0, f_sem["g"])
                    gp.wait_ge(s_table, 1)
                    gp.wait_ge(f_sem["ya"], i)
                    gp.wait_ge(f_sem["yv"], i)
                    scatter(0, 0, f_sem["s"])
                    gp.wait_ge(f_sem["s"], 16 * i)
                    gp.sem_inc(f_sem["it"], 1)
            gp.sem_inc(s_done, 1)

        @block.tensor
        def _(pe):
            def open_group(name):
                g = GID[name]
                if g >= 4:
                    emptied(pe, g - 4)
                return bank(name)

            def mm(out, lhsT, rhs, first, last):
                return pe.matmul(out, lhsT, rhs, start=first, stop=last)

            def wide(name, w, act, ks, before=None):
                ps = open_group(name)
                for n, k in enumerate(ks):
                    if before is not None:
                        before(k)
                    for h in range(2):
                        last = mm(ps[:, 512 * h:512 * h + HALF], w(k), act(k)[:, HALF * h:HALF * h + HALF],
                                  n == 0, n == len(ks) - 1)
                last.then_inc(s_full, 1)

            def turn(out, in_, n=P):
                return pe.transpose(out, in_, ident[0:n, 0:n])

            pe.wait_ge(s_const, 6)
            pe.wait_ge(s_par, 16 * len(PAR_SPEC))
            pe.wait_ge(s_wcbl, 16)
            ps = open_group("par")
            turn(ps[:, 0:NPAR], raw_par[0:NPAR, :], NPAR)
            turn(ps[:, 512:512 + WB * RC], raw_wcb[0:WB * RC, :], WB * RC).then_inc(s_full, 1)
            pe.wait_ge(s_state, 16 * 4)
            ps = open_group("st")
            for c in range(RC):
                turn(ps[:, NS * c:NS * c + NS], st_h[:, c * P:(c + 1) * P], NS)
            for c in range(RC):
                last = turn(ps[:, 32 + 24 * c:32 + 24 * c + 24], st_ca[:, c * P:(c + 1) * P], 24)
            last.then_inc(s_full, 1)
            ps = open_group("cb")
            for c in range(RC):
                for r in range(2):
                    at = 512 * (c // 2) + 240 * (c % 2) + 120 * r
                    last = turn(ps[:, at:at + 120], st_cb[:, r, c * P:(c + 1) * P], 120)
            last.then_inc(s_full, 1)
            pe.wait_ge(s_x, 16 * TT)
            for c in range(KC):
                ps = open_group(f"x{c}")
                for t in range(TT):
                    w = width(t)
                    last = turn(ps[:, t * P:t * P + w], x_tok[0:w, t, c * P:(c + 1) * P], w)
                last.then_inc(s_full, 1)
            wait_out(pe, "x6")
            wait_out(pe, "x7")
            pe.wait_ge(s_load[0], 16 * 4)
            for j in range(2 * RC):
                name = ("zv", "zs")[j // RC] + str(j % RC)
                wide(name, lambda k: wslot(0)[:, k, j * P:(j + 1) * P], lambda k: xT[:, k, :], range(KC))
            pe.wait_ge(s_load[1], 16)
            for j in range(2 * RC):
                name = ("zu", "zg")[j // RC] + str(j % RC)
                at = (j + RC) % (2 * RC)
                wide(name, lambda k: wslot(1)[:, k, at * P:(at + 1) * P], lambda k: xT[:, k, :], range(KC))
            pe.wait_ge(s_mem, 16)
            for g in range(2):
                ps = open_group(f"mt{g}")
                for c in range(4):
                    for m in range(2):
                        last = turn(ps[:, 256 * c + P * m:256 * c + P * m + P], mem_tok[:, m, (4 * g + c) * P:(4 * g + c + 1) * P])
                last.then_inc(s_full, 1)

            def memory(names, w, s):
                pe.wait_ge(s, 16)
                for m, name in enumerate(names):
                    ps = open_group(name)
                    for k in range(KC):
                        for n in range(2):
                            last = mm(ps[:, 512 * n:512 * n + 512], memT[:, k, m * P:(m + 1) * P],
                                      w[:, k, 512 * n:512 * n + 512], k == 0, k == KC - 1)
                    last.then_inc(s_full, 1)

            wait_out(pe, "mt1")
            memory(("v0", "v1"), wslot(2), s_load[2])
            wait_out(pe, "zu3")
            pe.wait_ge(s_glu, RC)
            ps = open_group("tails")
            for c in range(RC):
                turn(ps[0:11, c * P:(c + 1) * P], uT[:, c, T - 11:T])
            for c in range(RC):
                last = turn(ps[0:38, 512 + c * P:512 + (c + 1) * P], gluT[:, c, T - 38:T])
            last.then_inc(s_full, 1)
            pe.wait_ge(s_gw, 16 * 4)
            pe.wait_ge(s_uc, 1)
            for m, name in enumerate(("ra", "ri")):
                for c in range(RC):
                    wide(f"{name}{c}", lambda k: gate_w[:, m, c, :], lambda k: ucT[:, c, :], range(1))
            memory(("k0", "k1"), wslot(0), s_load[3])
            wait_out(pe, "k1")
            for g in range(2):
                ps = open_group(f"kt{g}")
                for c in range(4):
                    for m in range(2):
                        last = turn(ps[:, 256 * c + P * m:256 * c + P * m + P], k_tok[:, m, (4 * g + c) * P:(4 * g + c + 1) * P])
                last.then_inc(s_full, 1)
            pe.wait_ge(s_h, RC)
            ps = open_group("hlast")
            for c in range(RC):
                last = turn(ps[0:9, c * P:(c + 1) * P], ucT[:, c, SEQ - 1:T])
            last.then_inc(s_full, 1)

            norm_at = [0]

            def norm_stats(mean, var, w, x, sqs, n):
                wide(mean, lambda k: w[:, :], lambda k: x[:, k, :], range(n))
                wide(var, lambda k: w[:, :], lambda k: sqs[:, k, :], range(n),
                     before=lambda k: pe.wait_ge(s_sq, norm_at[0] + k + 1))
                norm_at[0] += n

            pe.wait_ge(s_convb, 1)
            norm_stats("cmean", "cvar", mean_c, cT, sq_c, RC)
            pe.wait_ge(s_load[4], 16)
            pe.wait_ge(s_ya, RC)
            pe.wait_ge(s_ln, RC)
            for j in range(KC):
                wide(f"wo{j}", lambda k: wslot(1)[:, k, j * P:(j + 1) * P],
                     lambda k: gT[:, k, :] if k < RC else cT[:, k - RC, :], range(KC))
            wait_out(pe, "wo7")
            norm_stats("mean1", "var1", mean_d, xT, sq, KC)
            pe.wait_ge(s_load[5], 16)
            pe.wait_ge(s_ln, RC + KC)
            for j in range(KC):
                wide(f"q{j}", lambda k: wslot(2)[:, k, j * P:(j + 1) * P], lambda k: xT[:, k, :], range(KC))
            wait_out(pe, "q7")
            ps = open_group("qs")
            for c in range(KC):
                last = turn(ps[0:NS, c * P:(c + 1) * P], qT[:, c, SEQ:T])
            last.then_inc(s_full, 1)
            wait_out(pe, "qs")

            def spread(b):
                ps = open_group(f"qb{b}")
                for n in range(2):
                    last = mm(ps[:, 512 * n:512 * n + 512], ident[0:NS, b:b + 1].to_broadcast([NS, P]),
                              q_s[:, 512 * n:512 * n + 512], True, True)
                last.then_inc(s_full, 1)

            def scores(t):
                ps = open_group(f"sc{t}")
                for h in range(XH):
                    for d in range(2):
                        last = mm(ps[:, XD * h:XD * h + XD], qT[:, 2 * h + d, t * P:(t + 1) * P], keyT[:, 2 * h + d, :],
                                  d == 0, d == 1)
                last.then_inc(s_full, 1)

            def turn_probs(t):
                pe.wait_ge(s_prob, t + 1)
                ps = open_group(f"pt{t}")
                for h in range(XH):
                    for m in range(2):
                        at = (2 * h + m) * P
                        last = turn(ps[:, at:at + P], probs[:, t % 2, h, m * P:(m + 1) * P])
                last.then_inc(s_full, 1)

            for name, _ in GROUPS[GID["sc0"]:GID["pt3"] + 1]:
                {"sc": scores, "qb": spread, "pt": turn_probs}[name[0:2]](int(name[2]))
            wait_out(pe, "pt3")
            for j in range(KC):
                ps = open_group(f"o{j}")
                for m in range(2):
                    last = mm(ps[:, 0:SEQ], v_tok[:, m, j * P:(j + 1) * P], prT[:, 2 * (j // 2) + m, 0:SEQ], m == 0, m == 1)
                last.then_inc(s_full, 1)
            wait_out(pe, "qb7")
            ps = open_group("ssT")
            for m in range(2):
                last = turn(ps[0:32, m * P:(m + 1) * P], ss[:, m, :])
            last.then_inc(s_full, 1)
            pe.wait_ge(s_prob, 5)
            ps = open_group("spT")
            for m in range(2):
                last = turn(ps[:, 32 * m:32 * m + 32], sp[:, m * P:(m + 1) * P], 32)
            last.then_inc(s_full, 1)
            wait_out(pe, "spT")
            ps = open_group("os")
            for b in range(NS):
                if b % 4 == 0:
                    pe.wait_ge(s_load[9 + b // 4], 16 * 4)
                vc = cache(b // 4, b % 4)
                for j in range(KC):
                    for m in range(2):
                        c = 4 * b + j // 2
                        last = mm(ps[:, 8 * b + j:8 * b + j + 1], vc[:, m, j * P:(j + 1) * P], spT[:, m, c:c + 1], m == 0, m == 1)
            last.then_inc(s_full, 1)
            wait_out(pe, "os")
            pe.wait_ge(s_load[8], 16)
            for j in range(KC):
                wide(f"xo{j}", lambda k: wslot(2)[:, k, j * P:(j + 1) * P], lambda k: oT[:, k, :], range(KC))
            wait_out(pe, "xo7")
            norm_stats("mean2", "var2", mean_d, xT, sq, KC)
            pe.wait_ge(s_ln, RC + 2 * KC)
            pe.wait_ge(s_wr, 16)
            ps = open_group("rt")
            for t in range(TT):
                w = width(t)
                for k in range(KC):
                    last = mm(ps[0:w, E * t:E * t + E], xT[:, k, t * P:t * P + w], wr[:, k, :], k == 0, k == KC - 1)
            last.then_inc(s_full, 1)
            for t in range(TT):
                w = width(t)
                ps = open_group(f"x2{t}")
                for k in range(KC):
                    last = turn(ps[0:w, k * P:(k + 1) * P], xT[:, k, t * P:t * P + w])
                last.then_inc(s_full, 1)
            pe.wait_ge(s_load[11], 16 * 3)
            for j in range(2):
                for name, w in (("h1", w1s), ("h3", w3s)):
                    wide(name + "ab"[j], lambda k: w[:, k, j * P:(j + 1) * P], lambda k: xT[:, k, :], range(KC))
            pe.wait_ge(s_late, 8)
            pe.wait_ge(s_sel, 1)
            ps = open_group("rank")
            sel = R[2]
            for t in range(TT):
                for u in range(t + 1):
                    last = mm(ps[:, E * t:E * t + E], tri if u == t else ones[:, :], sel[:, u, :], u == 0, u == t)
            last.then_inc(s_full, 1)
            ps = open_group("count")
            for t in range(TT):
                last = mm(ps[:, 0:E], ones[:, :], sel[:, t, :], t == 0, t == TT - 1)
            last.then_inc(s_full, 1)
            wait_out(pe, "h3b")
            for t in range(TT):
                w = width(t)
                ps = open_group(f"so{t}")
                for k in range(2):
                    for n in range(2):
                        last = mm(ps[0:w, 512 * n:512 * n + 512], shT[:, k, t * P:t * P + w], w2s[:, k, 512 * n:512 * n + 512],
                                  k == 0, k == 1)
                last.then_inc(s_full, 1)

            emptied(pe, GID["so4"])
            pe.wait_ge(s_table, 1)

            def find(n, e):
                for t in range(TT):
                    last = mm(psum[:, 3, 0:2], onehot[:, n % 2, t, :], table[:, t, e, :], t == 0, t == TT - 1)
                return last

            def turn_rows(b):
                for k in range(KC):
                    last = turn(psum[:, 1, k * P:(k + 1) * P], xg[:, b, k:D:KC])
                return last

            def up(b, part):
                wu, _ = ew(part)
                for k in range(KC):
                    last = mm(psum[:, 2, 0:512].rearrange("p (w n) -> p w n", w=2), xgT[:, b, k, :], wu[:, k, :, :], k == 0, k == KC - 1)
                return last

            def turn_hidden(b):
                for k in range(2):
                    last = turn(psum[:, 2, 512 + k * P:512 + (k + 1) * P], hid[:, b, k:FE:2])
                return last

            def down(b, part):
                _, wd = ew(part)
                for n in range(2):
                    for k in range(2):
                        last = mm(psum[:, 0, 512 * n:512 * n + 512], hidT[:, b, k, :], wd[:, k, 512 * n:512 * n + 512], k == 0, k == 1)
                return last

            def a_step(e, n):
                pe.wait_ge(m_oh, e + 1)
                if isinstance(e, int) and e < 3:
                    if e > 0:
                        pe.wait_ge(m_idx0, e)
                else:
                    pe.wait_ge(m_idx, e - 2)
                find(n, e).then_inc(m_ip, 1)

            def b_step(e, n, gath):
                pe.wait_ge(m_g[n % 2], gath)
                if not (isinstance(e, int) and e == 0):
                    pe.wait_ge(m_xc, e)
                turn_rows(n % 2).then_inc(m_xt, 1)

            def c_step(e, n, wait_w):
                pe.wait_ge(m_xc, e + 1)
                pe.wait_ge(s_w[n], wait_w)
                if not (isinstance(e, int) and e == 0):
                    pe.wait_ge(m_hd, e)
                up(n % 2, n).then_inc(m_h, 1)

            def d_step(e, n):
                pe.wait_ge(m_hd, e + 1)
                if not (isinstance(e, int) and e == 0):
                    pe.wait_ge(m_hc, e)
                turn_hidden(n % 2).then_inc(m_ht, 1)

            def y_step(e, n):
                pe.wait_ge(m_hc, e + 1)
                if not (isinstance(e, int) and e == 0):
                    pe.wait_ge(m_ya, e)
                    pe.wait_ge(m_yv, e)
                down(n % 2, n).then_inc(m_y, 1)

            a_step(0, 0)
            a_step(1, 1)
            b_step(0, 0, 16)
            c_step(0, 0, 48)
            a_step(2, 2)
            b_step(1, 1, 16)
            d_step(0, 0)

            def step(e, k, i):
                c_step(e, k % 4, 48 * i + 48 * (1 + k // 4))
                y_step(e - 1, (k - 1) % 4)
                if not (isinstance(e, int) and e + 2 >= EP):
                    a_step(e + 2, (k + 2) % 4)
                b_step(e + 1, (k + 1) % 4, 16 * (2 * i + (k + 1) // 2 + 1))
                d_step(e, k % 4)

            with pe.Fori(0, E // 4 - 1) as i:
                for k in range(1, 5):
                    step(4 * i + k, k, i)
            for k in range(1, 4):
                step(E - 4 + k, k, E // 4 - 1)
            y_step(E - 1, 3)

            pe.wait_ge(s_over, 1)
            n_max = pe.value_load(over[0:1, 0:1], min_val=0, max_val=T)
            with pe.If(n_max > P):
                pe.wait_ge(m_ya, E)
                pe.wait_ge(m_yv, E)
                pe.wait_ge(m_xc, E + 1)
                with pe.Fori(0, E * (ROUNDS - 1)) as i:
                    pe.wait_ge(f_sem["oh"], i + 1)
                    find(0, i % E).then_inc(f_sem["ip"], 1)
                    pe.wait_ge(f_sem["g"], 16 * i + 16)
                    turn_rows(0).then_inc(f_sem["xt"], 1)
                    pe.wait_ge(f_sem["xc"], i + 1)
                    pe.wait_ge(f_sem["w"], 48 * i + 48)
                    up(0, 0).then_inc(f_sem["h"], 1)
                    pe.wait_ge(f_sem["hd"], i + 1)
                    turn_hidden(0).then_inc(f_sem["ht"], 1)
                    pe.wait_ge(f_sem["hc"], i + 1)
                    down(0, 0).then_inc(f_sem["y"], 1)

        @block.scalar
        def _(act):
            act.dma_start(raw_wcb[0:WB * RC, :], I["w_conv_b"][0].rearrange("j (c p) -> (j c) p", p=P)).then_inc(s_wcbl, 16)
            act.dma_start(st_h, I["state_rglru_h"][0]).then_inc(s_state, 16)
            act.dma_start(st_ca, I["state_rglru_conv"][0].rearrange("b j n -> (b j) n")).then_inc(s_state, 16)
            for r in range(2):
                act.dma_start(st_cb[:, r, :], I["state_dwconv"][0, 4 * r:4 * r + 4].rearrange("b j n -> (b j) n")).then_inc(s_state, 16)

            def empty(name, out, func=ACT.Copy, **kw):
                wait_full(act, name)
                act.activation(out, two(bank(name)), func, **kw).then_inc(s_emA, 1)

            for c in range(0, KC, 2):
                wait_full(act, f"x{c}")
                act.activation(xT[:, c, :], bank(f"x{c}")[:, 0:T], ACT.Copy).then_inc(s_emA, 1)
            wait_out(act, "par")
            act.activation(c8[:, 0, :], par[:, PAR_AT["rg_lambda"]:PAR_AT["rg_lambda"] + RC], ACT.Abs).then_inc(s_abs, 1)
            act.wait_ge(s_abs, 1)
            act.activation(c8[:, 1, :], c8[:, 0, :], ACT.Exp, scale=-1.0).then_inc(s_c8e, 1)
            for c in range(RC):
                empty(f"zv{c}", halves(gluT[:, c, :]), ACT.Identity, bias=col("b_in", 8 + c))
            for c in range(RC):
                empty(f"zs{c}", halves(rT[:, c, :]), ACT.Sigmoid, bias=col("b_in", 12 + c))
            for c in range(RC):
                empty(f"zu{c}", halves(uT[:, c, :]), ACT.Identity, bias=col("b_in", 4 + c))
            for c in range(RC):
                empty(f"zg{c}", halves(gT[:, c, :]), ACT.Gelu_apprx_tanh, bias=col("b_in", c))
            for g in range(2):
                wait_full(act, f"mt{g}")
                act.activation(memT[:, 4 * g:4 * g + 4, :], bank(f"mt{g}").rearrange("p (c m) -> p c m", c=4), ACT.Copy).then_inc(s_emA, 1)
            for m in range(2):
                wait_full(act, f"v{m}")
                act.activation(v_tok[:, m, :], bank(f"v{m}"), ACT.Copy).then_inc(s_emA, 1)
            act.wait_ge(s_glu, RC)
            for c in range(RC):
                empty(f"ra{c}", halves(rT[:, c, :]), ACT.Sigmoid, bias=col("b_rg_a", c))
            wait_full(act, "tails")
            act.wait_ge(s_uc, 1)
            for c in range(RC):
                empty(f"ri{c}", halves(uT[:, c, :]), ACT.Sigmoid, bias=col("b_rg_x", c))
            for m in range(2):
                wait_full(act, f"k{m}")
                act.activation(k_tok[:, m, :], bank(f"k{m}"), ACT.Copy).then_inc(s_emA, 1)
            for g in range(2):
                wait_full(act, f"kt{g}")
                act.activation(keyT[:, 4 * g:4 * g + 4, :], bank(f"kt{g}").rearrange("p (c m) -> p c m", c=4), ACT.Copy).then_inc(s_emA, 1)
            act.wait_ge(s_c8, 1)
            act.wait_ge(s_convb, 1)
            wait_out(act, "ra3")
            for c in range(RC):
                act.activation(thT[:, c, :], rT[:, c, :], ACT.Tanh, scale=c8[:, 7, c:c + 1]).then_inc(s_tanh, 1)
            for c in range(RC):
                act.wait_ge(s_srt, c + 1)
                act.activation(thT[:, c, :], thT[:, c, :], ACT.Sqrt, scale=-2.0).then_inc(s_root, 1)

            norm_at = [0]

            def norm(var, x, sqs, n, g, b, func):
                for k in range(n):
                    act.wait_ge(s_sub, norm_at[0] + k + 1)
                    act.activation(sqs[:, k, :], x[:, k, :], ACT.Square).then_inc(s_sq, 1)
                empty(var, halves(rstd[:, :]), ACT.Sqrt, bias=eps_t[:, 0:1])
                for k in range(n):
                    act.wait_ge(s_nrm, norm_at[0] + k + 1)
                    act.activation(x[:, k, :], x[:, k, :], func, bias=col(b, k), scale=col(g, k)).then_inc(s_ln, 1)
                norm_at[0] += n

            norm("cvar", cT, sq_c, RC, "ln_c_g", "ln_c_b", ACT.Silu)
            wait_full(act, "wo7")
            norm("var1", xT, sq, KC, "ln1_g", "ln1_b", ACT.Identity)
            for c in range(KC):
                empty(f"q{c}", halves(qT[:, c, :]))
            act.wait_ge(s_kout, 16 * 2)
            wait_full(act, "qs")
            act.activation(q_s, bank("qs")[0:NS, :], ACT.Copy).then_inc(s_emA, 1)

            def softmax_exp(t):
                act.wait_ge(s_smax, t + 1)
                if t >= 2:
                    wait_full(act, f"pt{t - 2}")
                for h in range(XH):
                    last = act.activation(probs[:, t % 2, h, :], bank(f"sc{t}")[:, XD * h:XD * h + XD], ACT.Exp,
                                          bias=small[:, 4 + h:5 + h] if t % 2 == 0 else small[:, 12 + h:13 + h],
                                          scale=XD ** -0.5,
                                          accum_out=small[:, 16 + 4 * (t % 2) + h:17 + 4 * (t % 2) + h])
                    if h < XH - 1:
                        last.then_inc(s_ssum, 1)
                last.then_inc(s_emA, 1)

            def take_probs(t):
                wait_full(act, f"pt{t}")
                act.activation(prT[:, :, t * P:(t + 1) * P], bank(f"pt{t}").rearrange("p (k n) -> p k n", k=KC), ACT.Copy).then_inc(s_emA, 1)

            for name, who in GROUPS[GID["sc0"]:GID["pt3"] + 1]:
                if who == "A":
                    {"sc": softmax_exp, "pt": take_probs}[name[0:2]](int(name[2]))
            wait_full(act, "wo7")
            for j in range(KC):
                wait_full(act, f"o{j}")
                act.activation(oT[:, j, 0:SEQ], bank(f"o{j}")[:, 0:SEQ], ACT.Copy).then_inc(s_emA, 1)
            act.wait_ge(s_smax, 5)
            act.activation(sp, bank("ssT")[0:32, 0:N_MEM], ACT.Exp, bias=small[0:32, 25:26], scale=XD ** -0.5,
                           accum_out=small[0:32, 26:27]).then_inc(s_emA, 1)
            wait_full(act, "spT")
            act.activation(spT, bank("spT")[:, 0:64].rearrange("p (m n) -> p m n", m=2), ACT.Copy).then_inc(s_emA, 1)
            wait_full(act, "os")
            act.activation(oT[:, :, SEQ:T], bank("os")[:, 0:64].rearrange("p (b j) -> p j b", j=KC), ACT.Copy).then_inc(s_emA, 1)
            norm("var2", xT, sq, KC, "ln2_g", "ln2_b", ACT.Identity)
            act.wait_ge(s_rz, 1)
            wait_full(act, "rt")
            act.activation(R[0][:, 0:4, :], bank("rt")[:, 0:4 * E].rearrange("p (t e) -> p t e", t=4), ACT.Sigmoid).then_inc(s_ssum, 1)
            act.activation(R[0][0:NS, 4, :], bank("rt")[0:NS, 4 * E:5 * E], ACT.Sigmoid).then_inc(s_emA, 1)
            for t in range(TT):
                w = width(t)
                wait_full(act, f"x2{t}")
                act.activation(base[0:w, t, :], bank(f"x2{t}")[0:w, :], ACT.Copy).then_inc(s_emA, 1)
                emptied(act, GID[f"x2{t}"])
                act.dma_start(x2_rows[t * P:t * P + w, :], base[0:w, t, :]).then_inc(s_x2out, 16)
            for j in range(2):
                empty("h1" + "ab"[j], halves(sh1[:, j, :]), ACT.Silu)

            def xc(b):
                return act.activation(xgT[:, b, :, :], psum[:, 1, :].rearrange("p (k s) -> p k s", k=KC), ACT.Copy)

            def sl(b):
                return act.activation(silu[:, b, :], psum[:, 2, 0:FE], ACT.Silu)

            def yh(b, n):
                return act.activation(ys[:, b, 0:512], psum[:, 0, 0:512], ACT.Copy, scale=gate_s[:, n:n + 1])

            def b_step(e, n):
                act.wait_ge(m_xt, e + 1)
                if not (isinstance(e, int) and e < 2):
                    act.wait_ge(m_h, e - 1)
                xc(n % 2).then_inc(m_xc, 1)

            def c_step(e, n):
                act.wait_ge(m_h, e + 1)
                if not (isinstance(e, int) and e < 2):
                    act.wait_ge(m_hd, e - 1)
                sl(n % 2).then_inc(m_sl, 1)

            def y_step(e, n, sc):
                act.wait_ge(m_y, e + 1)
                if sc is not None:
                    act.wait_ge(m_s[n % 2], sc)
                yh(n % 2, n).then_inc(m_ya, 1)

            b_step(0, 0)
            c_step(0, 0)
            b_step(1, 1)

            def step(e, k, i, sc):
                c_step(e, k % 4)
                y_step(e - 1, (k - 1) % 4, sc)
                b_step(e + 1, (k + 1) % 4)

            for k in range(1, 5):
                step(k, k, 0, None if k <= 2 else 16 * ((k - 1) // 2))
            with act.Fori(1, E // 4 - 1) as i:
                for k in range(1, 5):
                    step(4 * i + k, k, i, 32 * i + 16 * ((k - 1) // 2))
            for k in range(1, 4):
                step(E - 4 + k, k, 0, 16 * ((E - 4 + k - 1) // 2))
            y_step(E - 1, 3, 16 * ((E - 1) // 2))

            act.wait_ge(s_over, 1)
            n_max = act.value_load(over[0:1, 0:1], min_val=0, max_val=T)
            with act.If(n_max > P):
                act.wait_ge(m_s[0], 16 * (E // 2))
                with act.Fori(0, E * (ROUNDS - 1)) as i:
                    act.wait_ge(f_sem["xt"], i + 1)
                    xc(0).then_inc(f_sem["xc"], 1)
                    act.wait_ge(f_sem["h"], i + 1)
                    sl(0).then_inc(f_sem["sl"], 1)
                    act.wait_ge(f_sem["y"], i + 1)
                    yh(0, 0).then_inc(f_sem["ya"], 1)

            for t in range(TT):
                w = width(t)
                act.wait_ge(s_var, t + 1)
                act.activation(small[0:w, 36:37], small[0:w, 35:36], ACT.Sqrt, bias=eps_t[0:w, 0:1]).then_inc(s_sd, 1)

        @block.vector
        def _(dve):
            count = [0]

            def chain(ins):
                count[0] += 1
                ins.then_inc(s_v, 1)
                return count[0]

            def link(ins):
                dve.wait_ge(s_v, chain(ins))

            wait_full(dve, "par")
            link(dve.tensor_copy(par[:, :], bank("par")[:, 0:NPAR]))
            dve.tensor_copy(wcb[:, :], bank("par")[:, 512:512 + WB * RC]).then_inc(s_emV, 1)
            wait_full(dve, "st")
            link(dve.tensor_copy(h0t[:, :, :], bank("st")[:, 0:32].rearrange("p (c b) -> p c b", c=RC)))
            dve.tensor_copy(caT, bank("st")[:, 32:128].rearrange("p (c b) -> p c b", c=RC)).then_inc(s_emV, 1)
            wait_full(dve, "cb")
            chain(dve.tensor_copy(cbT[:, 0:2, :], bank("cb")[:, 0:480].rearrange("p (c b) -> p c b", c=2)))
            dve.tensor_copy(cbT[:, 2:4, :], bank("cb")[:, 512:992].rearrange("p (c b) -> p c b", c=2)).then_inc(s_emV, 1)
            for c in range(1, KC, 2):
                wait_full(dve, f"x{c}")
                dve.tensor_copy(xT[:, c, :], bank(f"x{c}")[:, 0:T]).then_inc(s_emV, 1)

            lam = par[:, PAR_AT["rg_lambda"]:PAR_AT["rg_lambda"] + RC]
            dve.wait_ge(s_c8e, 1)
            y, s, s2, acc = c8[:, 1, :], c8[:, 2, :], c8[:, 3, :], c8[:, 4, :]
            link(dve.tensor_scalar(s, y, 2.0, None, ALU.add))
            link(dve.reciprocal(s2, s))
            link(dve.tensor_tensor(s, y, s2, ALU.mult))
            link(dve.tensor_tensor(s2, s, s, ALU.mult))
            terms = 9
            link(dve.tensor_scalar(acc, s2, 1.0 / (2 * terms + 1), 1.0 / (2 * terms - 1), ALU.mult, ALU.add))
            for n in range(terms - 2, -1, -1):
                link(dve.tensor_tensor(acc, acc, s2, ALU.mult))
                link(dve.tensor_scalar(acc, acc, 1.0 / (2 * n + 1), None, ALU.add))
            link(dve.tensor_tensor(acc, acc, s, ALU.mult))
            link(dve.tensor_scalar(c8[:, 5, :], lam, -1.0, 0.0, ALU.mult, ALU.max))
            link(dve.scalar_tensor_tensor(c8[:, 6, :], acc, 2.0, c8[:, 5, :], ALU.mult, ALU.add))
            dve.tensor_scalar(c8[:, 7, :], c8[:, 6, :], -RG_C / 2, None, ALU.mult).then_inc(s_c8, 1)

            def mult_add(out, in0, w, in1):
                return dve.scalar_tensor_tensor(out, in0, w, in1, ALU.mult, ALU.add)

            def conv_sample(x, state, out, taps, wtap, wrow, bias, c):
                link(dve.tensor_scalar(out[:, c, SEQ:T], x[:, c, SEQ:T], wtap(taps - 1), bias, ALU.mult, ALU.add))
                pr = cprod[:, :, 0:taps - 1]
                link(dve.tensor_tensor(pr, state[:, c, :].rearrange("p (b j) -> p b j", b=NS), wrow, ALU.mult))
                link(dve.tensor_reduce(csum, pr, AX.X, ALU.add))
                return dve.tensor_tensor(out[:, c, SEQ:T], out[:, c, SEQ:T], csum, ALU.add)

            def conv_prompt(x, out, taps, wtap, bias, chunks):
                done = {}
                for c in chunks:
                    done[c] = chain(dve.tensor_scalar(out[:, c, 0:SEQ], x[:, c, 0:SEQ], wtap(c, taps - 1), bias(c),
                                                      ALU.mult, ALU.add))
                for s in range(1, taps):
                    for c in chunks:
                        dve.wait_ge(s_v, done[c])
                        done[c] = chain(mult_add(out[:, c, s:SEQ], x[:, c, 0:SEQ - s], wtap(c, taps - 1 - s),
                                                 out[:, c, s:SEQ]))
                dve.wait_ge(s_v, count[0])

            def wb_tap(c, j):
                return wcb[:, j * RC + c:j * RC + c + 1]

            def wa_tap(c, j):
                return col("w_conv_a", j * RC + c)

            def wb_row(c):
                return wcb[:, c:(WB - 1) * RC:RC].unsqueeze(1).broadcast_to([P, NS, WB - 1])

            def wa_row(c):
                a = PAR_AT["w_conv_a"]
                return par[:, a + c:a + (WA - 1) * RC:RC].unsqueeze(1).broadcast_to([P, NS, WA - 1])

            wait_out(dve, "cb")
            for c in range(RC):
                wait_out(dve, f"zs{c}")
                dve.tensor_tensor(gluT[:, c, :], gluT[:, c, :], rT[:, c, :], ALU.mult).then_inc(s_glu, 1)
            dve.wait_ge(s_glu, RC)
            for c in range(RC):
                link(conv_sample(gluT, cbT, cT, WB, lambda j: wb_tap(c, j), wb_row(c), col("b_conv_b", c), c))
            conv_prompt(gluT, cT, WB, wb_tap, lambda c: col("b_conv_b", c), range(0, 2))
            for c in range(RC):
                wait_out(dve, f"zu{c}")
            for c in range(RC):
                link(conv_sample(uT, caT, ucT, WA, lambda j: wa_tap(c, j), wa_row(c), col("b_conv_a", c), c))
            conv_prompt(uT, ucT, WA, wa_tap, lambda c: col("b_conv_a", c), range(RC))
            dve.tensor_copy(csum[:, 0:1], csum[:, 0:1]).then_inc(s_uc, 1)
            wait_full(dve, "tails")
            chain(dve.tensor_copy(tail[0:11, 0, :], bank("tails")[0:11, 0:512]))
            dve.tensor_copy(tail[0:38, 1, :], bank("tails")[0:38, 512:1024]).then_inc(s_emV, 1)
            conv_prompt(gluT, cT, WB, wb_tap, lambda c: col("b_conv_b", c), range(2, 4))
            dve.tensor_copy(csum[:, 0:1], csum[:, 0:1]).then_inc(s_convb, 1)

            for c in range(RC):
                wait_out(dve, f"ri{c}")
                th, a, b, d = thT[:, c, :], rT[:, c, :], uT[:, c, :], ucT[:, c, :]
                link(dve.tensor_tensor(b, b, d, ALU.mult))
                dve.wait_ge(s_tanh, c + 1)
                link(dve.tensor_scalar(d, th, -1.0, 1.0, ALU.mult, ALU.add))
                link(dve.reciprocal(d, d))
                link(dve.scalar_tensor_tensor(a, th, 1.0, d, ALU.add, ALU.mult))
                link(dve.tensor_tensor(th, th, d, ALU.mult))
                dve.scalar_tensor_tensor(th, a, 1.0, th, ALU.add, ALU.mult).then_inc(s_srt, 1)
            for c in range(RC):
                th, a, b, h = thT[:, c, :], rT[:, c, :], uT[:, c, :], ucT[:, c, :]
                dve.wait_ge(s_root, c + 1)
                link(dve.tensor_tensor(b, b, th, ALU.mult))
                link(dve.tensor_tensor_scan(h[:, 0:SEQ], a[:, 0:SEQ], b[:, 0:SEQ], 0.0, ALU.mult, ALU.add))
                link(dve.tensor_tensor(h[:, SEQ:T], a[:, SEQ:T], h0t[:, c, :], ALU.mult))
                dve.tensor_tensor(h[:, SEQ:T], h[:, SEQ:T], b[:, SEQ:T], ALU.add).then_inc(s_h, 1)
                dve.wait_ge(s_h, c + 1)
                wait_out(dve, f"zg{c}")
                dve.tensor_tensor(gT[:, c, :], gT[:, c, :], h, ALU.mult).then_inc(s_ya, 1)
            wait_full(dve, "hlast")
            dve.wait_ge(s_tailout, 16 * 4)
            dve.tensor_copy(tail[0:9, 0, :], bank("hlast")[0:9, 0:512]).then_inc(s_emV, 1)

            norm_at = [0]

            def norm(mean, var, x, n):
                wait_full(dve, mean)
                for k in range(n):
                    ins = dve.tensor_tensor(halves(x[:, k, :]), halves(x[:, k, :]), two(bank(mean)), ALU.subtract)
                    if k < n - 1:
                        ins.then_inc(s_sub, 1)
                    else:
                        ins.then_inc(s_emV, 1)
                        emptied(dve, GID[mean])
                        dve.sem_inc(s_sub, 1)
                wait_out(dve, var)
                link(dve.reciprocal(rstd[:, :], rstd[:, :]))
                for k in range(n):
                    dve.tensor_tensor(x[:, k, :], x[:, k, :], rstd[:, :], ALU.mult).then_inc(s_nrm, 1)
                norm_at[0] += n

            def residual(name, k):
                wait_full(dve, name)
                dve.scalar_tensor_tensor(halves(xT[:, k, :]), halves(xT[:, k, :]), ALPHA, two(bank(name)),
                                         ALU.mult, ALU.add).then_inc(s_emV, 1)

            norm("cmean", "cvar", cT, RC)
            for k in range(KC):
                residual(f"wo{k}", k)
            norm("mean1", "var1", xT, KC)

            def softmax(t):
                o = 8 * (t % 2)
                so = 16 + 4 * (t % 2)
                wait_full(dve, f"sc{t}")
                link(dve.tensor_reduce(small[:, o:o + 4], bank(f"sc{t}").rearrange("p (h m) -> p h m", h=XH), AX.X, ALU.max))
                dve.tensor_scalar(small[:, o + 4:o + 8], small[:, o:o + 4], -XD ** -0.5, None, ALU.mult).then_inc(s_smax, 1)
                wait_out(dve, f"sc{t}")
                dve.wait_ge(s_ssum, (XH - 1) * (t + 1))
                link(dve.reciprocal(small[:, 27:31], small[:, so:so + 4]))
                for h in range(XH):
                    pr = probs[:, t % 2, h, :]
                    ins = dve.tensor_scalar(pr, pr, small[:, 27 + h:28 + h], None, ALU.mult)
                    if h < XH - 1:
                        chain(ins)
                ins.then_inc(s_prob, 1)

            def sample_scores(b):
                if b % 4 == 0:
                    dve.wait_ge(s_load[6 + b // 4], 16 * 4)
                kc = cache((b // 4), b % 4)
                wait_full(dve, f"qb{b}")
                for m in range(2):
                    for h in range(XH):
                        ins = dve.tensor_tensor_reduce(junk, kc[:, m, XD * h:XD * h + XD], bank(f"qb{b}")[:, XD * h:XD * h + XD],
                                                       1.0, 0.0, ALU.mult, ALU.add, ss[:, m, 4 * b + h:4 * b + h + 1])
                        if (m, h) != (1, XH - 1):
                            link(ins)
                ins.then_inc(s_emV, 1)
                wait_out(dve, f"qb{b}")

            for name, _ in GROUPS[GID["sc0"]:GID["pt3"] + 1]:
                if name[0:2] in ("sc", "qb"):
                    {"sc": softmax, "qb": sample_scores}[name[0:2]](int(name[2]))
            wait_full(dve, "ssT")
            link(dve.tensor_reduce(small[0:32, 24:25], bank("ssT")[0:32, 0:N_MEM], AX.X, ALU.max))
            dve.tensor_scalar(small[0:32, 25:26], small[0:32, 24:25], -XD ** -0.5, None, ALU.mult).then_inc(s_smax, 1)
            wait_out(dve, "ssT")
            link(dve.reciprocal(small[0:32, 31:32], small[0:32, 26:27]))
            dve.tensor_scalar(sp, sp, small[0:32, 31:32], None, ALU.mult).then_inc(s_prob, 1)
            for k in range(KC):
                residual(f"xo{k}", k)
            norm("mean2", "var2", xT, KC)

            dve.memset(R[0], 0.0).then_inc(s_rz, 1)
            dve.memset(place, -1.0).then_inc(s_late2, 1)
            dve.memset(table, 0.0).then_inc(s_late2, 1)
            dve.wait_ge(s_late2, 2)
            dve.wait_ge(s_rt, 16)
            dve.wait_ge(s_late, 8)
            wait_out(dve, "rt")
            dve.wait_ge(s_ssum, (XH - 1) * 4 + 1)
            score, biased, sel, tmp, left = R[0], R[1], R[2], R[3], R[4]
            link(dve.tensor_tensor(biased, score, rbias.unsqueeze(1).broadcast_to([P, TT, E]), ALU.add))
            for t in range(TT):
                for g in range(8):
                    n = chain(dve.max(rmax[:, t, g, :], biased[:, t, 8 * g:8 * g + 8]))
            dve.wait_ge(s_v, n)
            link(dve.tensor_tensor(gscore, rmax[:, :, :, 0], rmax[:, :, :, 1], ALU.add))
            mine = gscore.unsqueeze(3).broadcast_to([P, TT, 8, 8])
            other = gscore.unsqueeze(2).broadcast_to([P, TT, 8, 8])
            link(dve.tensor_tensor(pair, other, mine, ALU.is_equal))
            link(dve.tensor_tensor(pair, pair, tri8.unsqueeze(1).broadcast_to([P, TT, 8, 8]), ALU.mult))
            link(dve.tensor_tensor(pair2, other, mine, ALU.is_gt))
            link(dve.tensor_tensor(pair, pair, pair2, ALU.add))
            link(dve.tensor_reduce(grank, pair, AX.X, ALU.add))
            link(dve.tensor_scalar(grank, grank, 4.0, None, ALU.is_lt))
            gm = grank.unsqueeze(3).broadcast_to([P, TT, 8, 8])
            b4 = biased.rearrange("p t (g j) -> p t g j", g=8)
            t4 = tmp.rearrange("p t (g j) -> p t g j", g=8)
            link(dve.tensor_tensor(t4, b4, gm, ALU.mult))
            link(dve.tensor_scalar(grank, grank, 1.0, 1e30, ALU.subtract, ALU.mult))
            link(dve.tensor_tensor(t4, t4, gm, ALU.add))
            for t in range(TT):
                n = chain(dve.max(top8[:, t, :], tmp[:, t, :]))
            dve.wait_ge(s_v, n)
            for t in range(TT):
                n = chain(dve.match_replace(left[:, t, :], top8[:, t, :], tmp[:, t, :], -2e30))
            dve.wait_ge(s_v, n)
            link(dve.tensor_scalar(sel, left, -2e30, None, ALU.is_equal))
            dve.tensor_tensor(sel, sel, rmask.unsqueeze(2).broadcast_to([P, TT, E]), ALU.mult).then_inc(s_sel, 1)
            dve.wait_ge(s_sel, 1)
            link(dve.tensor_tensor(tmp, score, sel, ALU.mult))
            link(dve.tensor_reduce(gsum, tmp, AX.X, ALU.add))
            link(dve.tensor_scalar(gsum, gsum, 1e-30, None, ALU.max))
            link(dve.reciprocal(gsum, gsum))
            link(dve.tensor_scalar(gsum, gsum, ROUTED_SCALE, None, ALU.mult))
            link(dve.tensor_tensor(table[:, :, 0:E, 1], tmp, gsum.unsqueeze(2).broadcast_to([P, TT, E]), ALU.mult))
            link(dve.memset(wsum, 1.0))
            for t in range(TT):
                n = chain(dve.tensor_tensor_scan(left[:, t, :], wsum, sel[:, t, :], 0.0, ALU.mult, ALU.add))
            dve.wait_ge(s_v, n)
            link(dve.tensor_tensor(table[:, :, 0:E, 0], left, row8.unsqueeze(2).broadcast_to([P, TT, E]), ALU.add))

            def gated(name, j):
                wait_full(dve, name)
                wait_out(dve, "h1" + name[2])
                dve.tensor_tensor(halves(shT[:, j, :]), halves(sh1[:, j, :]), two(bank(name)), ALU.mult).then_inc(s_emV, 1)

            gated("h3a", 0)
            gated("h3b", 1)
            wait_full(dve, "rank")
            link(dve.scalar_tensor_tensor(place[:, :, 0:E], bank("rank")[:, 0:TT * E].rearrange("p (t e) -> p t e", t=TT),
                                          1.0, sel, ALU.add, ALU.mult))
            dve.tensor_scalar(place[:, :, 0:E], place[:, :, 0:E], 1.0, None, ALU.subtract).then_inc(s_emV, 1)
            wait_full(dve, "count")
            dve.tensor_reduce(cmax, bank("count")[:, 0:E], AX.X, ALU.max).then_inc(s_emV, 1)
            wait_out(dve, "count")
            dve.tensor_copy(over[:, :], cmax).then_inc(s_over, 1)
            wait_out(dve, "rank")
            dve.sem_inc(s_table, 1)
            for t in range(TT):
                w = width(t)
                wait_full(dve, f"so{t}")
                wait_out(dve, f"x2{t}")
                dve.wait_ge(s_x2out, 16 * TT)
                dve.scalar_tensor_tensor(base[0:w, t, :], base[0:w, t, :], ALPHA, bank(f"so{t}")[0:w, :],
                                         ALU.mult, ALU.add).then_inc(s_emV, 1)

            def oh(n, e, numbers):
                return dve.tensor_tensor(onehot[:, n % 2, :, :], place[:, :, bass.ds(e, 1)].broadcast_to([P, TT, P]),
                                         numbers.unsqueeze(1).broadcast_to([P, TT, P]), ALU.is_equal)

            def indices(n, s, base_count):
                m = idx_m[:, n:n + 1]
                dve.tensor_scalar(m, psum[:, 3, 0:1], 0.0, FAR, ALU.is_equal, ALU.mult).then_inc(s, 1)
                dve.tensor_copy(gate_s[:, n:n + 1], psum[:, 3, 1:2]).then_inc(s, 1)
                dve.wait_ge(s, base_count + 2)
                dve.scalar_tensor_tensor(idx_y[:, n:n + 1], psum[:, 3, 0:1], -1.0, m, ALU.add, ALU.add).then_inc(s, 1)
                dve.wait_ge(s, base_count + 3)
                return dve.tensor_scalar(idx_x[:, n:n + 1], idx_y[:, n:n + 1], 3, None, ALU.logical_shift_right)

            def hd(b):
                return dve.tensor_tensor(hid[:, b, :], silu[:, b, :], psum[:, 2, FE:2 * FE], ALU.mult)

            def hc(b):
                return dve.tensor_copy(hidT[:, b, :, :], psum[:, 2, 512:768].rearrange("p (k s) -> p k s", k=2))

            def yh(b, n):
                return dve.tensor_scalar(ys[:, b, 512:1024], psum[:, 0, 512:1024], gate_s[:, n:n + 1], None, ALU.mult)

            def oh_step(e, n):
                if not (isinstance(e, int) and e < 2):
                    dve.wait_ge(m_ip, e - 1)
                oh(n, e, slots).then_inc(m_oh, 1)

            def i_step(e, n, sc):
                dve.wait_ge(m_ip, e + 1)
                if sc is not None:
                    dve.wait_ge(m_s[n % 2], sc)
                indices(n, m_iv, 3 * e).then_inc(m_idx0 if isinstance(e, int) and e < 2 else m_idx, 1)

            def c_step(e, n):
                dve.wait_ge(m_sl, e + 1)
                if not (isinstance(e, int) and e < 2):
                    dve.wait_ge(m_ht, e - 1)
                hd(n % 2).then_inc(m_hd, 1)

            def d_step(e, n):
                dve.wait_ge(m_ht, e + 1)
                if not (isinstance(e, int) and e < 2):
                    dve.wait_ge(m_y, e - 1)
                hc(n % 2).then_inc(m_hc, 1)

            def y_step(e, n, sc):
                dve.wait_ge(m_y, e + 1)
                if sc is not None:
                    dve.wait_ge(m_s[n % 2], sc)
                yh(n % 2, n).then_inc(m_yv, 1)

            wait_full(dve, "so4")
            oh_step(0, 0)
            oh_step(1, 1)
            i_step(0, 0, None)
            i_step(1, 1, None)
            oh_step(2, 2)
            c_step(0, 0)
            i_step(2, 2, None)
            oh_step(3, 3)
            d_step(0, 0)

            def step(e, k, sc, si, more=True):
                c_step(e, k % 4)
                y_step(e - 1, (k - 1) % 4, sc)
                if more:
                    i_step(e + 2, (k + 2) % 4, si)
                    oh_step(e + 3, (k + 3) % 4)
                d_step(e, k % 4)

            for k in range(1, 5):
                step(k, k, None if k <= 2 else 16 * ((k - 1) // 2), None if k < 2 else 16 * ((k - 2) // 2 + 1))
            with dve.Fori(1, E // 4 - 1) as i:
                for k in range(1, 5):
                    step(4 * i + k, k, 32 * i + 16 * ((k - 1) // 2), 32 * i + 16 * ((k - 2) // 2 + 1))
            for k in range(1, 4):
                e = E - 4 + k
                c_step(e, k % 4)
                y_step(e - 1, (k - 1) % 4, 16 * ((e - 1) // 2))
                if e + 2 < EP:
                    i_step(e + 2, (k + 2) % 4, 16 * ((e - 2) // 2 + 1))
                if e + 3 < EP:
                    oh_step(e + 3, (k + 3) % 4)
                d_step(e, k % 4)
            y_step(E - 1, 3, 16 * ((E - 1) // 2))

            dve.wait_ge(s_over, 1)
            n_max = dve.value_load(over[0:1, 0:1], min_val=0, max_val=T)
            with dve.If(n_max > P):
                dve.wait_ge(m_s[0], 16 * (E // 2))
                dve.wait_ge(m_s[1], 16 * (E // 2))
                dve.wait_ge(m_g[0], 16 * (E // 2 + 1))
                dve.wait_ge(m_ip, EP)
                dve.wait_ge(s_late, 9)
                with dve.Fori(1, E * (ROUNDS - 1) + 1) as turn_i:
                    dve.wait_ge(f_sem["it"], turn_i)
                    i = turn_i - 1
                    link_r = dve.tensor_scalar(slots_r, slots, rounds_t[:, bass.ds(i // E, 1)], None, ALU.add)
                    link_r.then_inc(f_sem["iv"], 1)
                    dve.wait_ge(f_sem["iv"], 4 * i + 1)
                    oh(0, i % E, slots_r).then_inc(f_sem["oh"], 1)
                    dve.wait_ge(f_sem["ip"], i + 1)
                    indices(0, f_sem["iv"], 4 * i + 1).then_inc(f_sem["idx"], 1)
                    dve.wait_ge(f_sem["sl"], i + 1)
                    hd(0).then_inc(f_sem["hd"], 1)
                    dve.wait_ge(f_sem["ht"], i + 1)
                    hc(0).then_inc(f_sem["hc"], 1)
                    dve.wait_ge(f_sem["y"], i + 1)
                    yh(0, 0).then_inc(f_sem["yv"], 1)

            dve.wait_ge(s_lnw, 32)
            for t in range(TT):
                w = width(t)
                dve.wait_ge(s_yin[t % 3], 16 * (t // 3 + 1))
                x = base[0:w, t, :]
                for j in range(TOPK):
                    ins = dve.tensor_tensor(x, x, y_in[t % 3][0:w, j, :], ALU.add)
                    if j < TOPK - 1:
                        link(ins)
                ins.then_inc(s_rowv, 1)
                dve.wait_ge(s_rowv, t + 1)
                for n in range(2):
                    link(dve.bn_stats(st6[0:w, n, :], base[0:w, t, 512 * n:512 * n + 512]))
                dve.bn_aggr(small[0:w, 34:36], st6[0:w, :, :]).then_inc(s_var, 1)
                dve.wait_ge(s_var, t + 1)
                dve.wait_ge(s_sd, t + 1)
                link(dve.reciprocal(small[0:w, 37:38], small[0:w, 36:37]))
                link(dve.tensor_scalar(x, x, small[0:w, 34:35], small[0:w, 37:38], ALU.subtract, ALU.mult))
                link(dve.tensor_tensor(x, x, ln3g[0:w, :], ALU.mult))
                dve.tensor_tensor(x, x, ln3b[0:w, :], ALU.add).then_inc(s_res, 1)


_INS = ['x_prompt', 'x_sample', 'mem_prompt', 'state_rglru_h', 'state_rglru_conv', 'state_dwconv', 'cache_mem_k',
        'cache_mem_v', 'w_in', 'b_in', 'w_conv_a', 'b_conv_a', 'w_rg_a', 'b_rg_a', 'w_rg_x', 'b_rg_x', 'rg_lambda',
        'w_conv_b', 'b_conv_b', 'ln_c_g', 'ln_c_b', 'w_out', 'ln1_g', 'ln1_b', 'w_q', 'w_k', 'w_v', 'w_o', 'ln2_g',
        'ln2_b', 'w_router', 'router_bias', 'w1_e', 'w3_e', 'w2_e', 'w1_s', 'w3_s', 'w2_s', 'ln3_g', 'ln3_b']
_OUTS = [(1, 512, 1024), (8, 1, 1024), (1, 1, 512), (1, 1, 3, 512), (1, 1, 30, 512), (1, 1, 256, 4, 256),
         (1, 1, 256, 4, 256), (1, 8, 512), (1, 8, 3, 512), (1, 8, 30, 512)]


def kernel(**inputs):
    import numpy as _np
    import concourse.bacc as _bacc
    from concourse import mybir as _mybir
    from concourse.bass_utils import run_bass_kernel_spmd as _run

    nc = _bacc.Bacc("TRN2", target_bir_lowering=False, num_devices=1)
    arrays, ins = {}, {}
    for name in _INS:
        a = _np.ascontiguousarray(inputs[name])
        arrays[f"in_{name}_dram"] = a
        ins[name] = nc.dram_tensor(f"in_{name}_dram", a.shape, _mybir.dt.from_np(a.dtype), kind="ExternalInput").ap()
    outs = [nc.dram_tensor(f"out_{i}_dram", shape, _mybir.dt.float32, kind="ExternalOutput").ap()
            for i, shape in enumerate(_OUTS)]
    decoder_step(nc, ins, outs)
    r = _run(nc, [arrays], core_ids=[0])
    return tuple(r.results[0][f"out_{i}_dram"] for i in range(len(_OUTS)))
```

```python
from contextlib import ExitStack
import math

import concourse.bass as bass
from concourse import mybir

ALU = mybir.AluOpType
ACT = mybir.ActivationFunctionType
AX = mybir.AxisListType
F32 = mybir.dt.float32
I32 = mybir.dt.int32
U32 = mybir.dt.uint32
BF16 = mybir.dt.bfloat16

P = 128
D = 1024
KC = D // P
SEQ, NS = 512, 8
T = SEQ + NS
HALF = T // 2
RC = 4
TT = 5
N_MEM, XH, XD = 256, 4, 256
E, FE, TOPK = 64, 256, 8
WA, WB = 4, 31
ALPHA = 2.0 ** 0.25
EPS = 1e-5
RG_C = 8.0
ROUTED_SCALE = 2.5
CAP = 112
NROW = T * TOPK
FAR = 8192.0
ROUNDS = (T + CAP - 1) // CAP
NB = 8

PAR_SPEC = [("b_in", 16), ("w_conv_a", 16), ("b_conv_a", 4), ("b_rg_a", 4), ("b_rg_x", 4), ("rg_lambda", 4),
            ("b_conv_b", 4), ("ln_c_g", 4), ("ln_c_b", 4), ("ln1_g", 8), ("ln1_b", 8), ("ln2_g", 8), ("ln2_b", 8)]
PAR_AT = {}
_row = 0
for _n, _k in PAR_SPEC:
    PAR_AT[_n] = _row
    _row += _k
NPAR = _row

GROUPS = [(f"x{c}", "AV"[c % 2]) for c in range(KC)] + [("par", "V")]
GROUPS += [(f"zv{c}", "A") for c in range(RC)] + [("st", "V"), ("cb", "V")] + [(f"zs{c}", "A") for c in range(RC)]
GROUPS += [(f"zu{c}", "A") for c in range(RC)] + [(f"zg{c}", "A") for c in range(RC)]
GROUPS += [("mt0", "A"), ("mt1", "A"), ("v0", "A"), ("tails", "A")]
GROUPS += [(f"ra{c}", "A") for c in range(RC)] + [(f"ri{c}", "A") for c in range(RC)]
GROUPS += [("k0", "A"), ("cmean", "V"), ("k1", "A"), ("cvar", "A"), ("kt0", "A"), ("kt1", "A"), ("hlast", "V")]
GROUPS += [(f"wo{c}", "V") for c in range(KC)] + [("mean1", "V"), ("v1a", "A"), ("var1", "A"), ("v1b", "A")]
GROUPS += [(f"q{c}", "A") for c in range(KC)] + [("qs", "A")]
ATTENTION = ["sc0", "sc1", "sc2", "pt0", "sc3", "pt1", "pt2", "pt3", "o0", "o1", "o2", "o3", "o4", "o5", "o6", "o7",
             "ssT", "spT"]
GROUPS += [(name, "A") for name in ATTENTION]
GROUPS += [("osa", "A"), ("osb", "V"), ("osT", "A")]
GROUPS += [(f"xo{c}", "V") for c in range(KC)] + [("mean2", "V"), ("var2", "A")]
GROUPS += [("h1a", "A"), ("rt", "A")] + [(f"x2{t}", "A") for t in range(TT)]
GROUPS += [("h3a", "V"), ("h1b", "A"), ("h3b", "V"), ("rank", "V"), ("count", "V")]
GROUPS += [(f"so{t}", "V") for t in range(TT)]
GID = {name: g for g, (name, _) in enumerate(GROUPS)}
LAST_ORDER = [4, 0, 1, 2, 3]
PARTS = [(0, 5), (5, 8)]
POOL_ROWS = (0, 1)
PE_ROWS = [(2, 3, 4), (6, 7)]
DVE_ROWS = [(0,), (5,)]
SMALL_ROWS = [(0, 2, 3, 4), (5, 6, 7)]
PAIR = {f"so{t}": t % 3 for t in range(TT)}

POOL_CHUNKS = (3,)

A0, A1, A2, A3, A4 = 0, 4160, 8320, 12480, 16640
A_SIZE = A4 + 2080


def at_least(e, n):
    return not isinstance(e, int) or e >= n


def exists(e):
    return not isinstance(e, int) or e < E


def width(t):
    return P if t < TT - 1 else NS


def decoder_step(nc: bass.Bass, ins, outs):
    I = ins
    (o_yp, o_ys, o_hp, o_cap, o_cbp, o_mk, o_mv, o_hs, o_cas, o_cbs) = outs

    with ExitStack() as ctx:
        def sb(name, shape, dt=F32):
            return ctx.enter_context(nc.sbuf_tensor(name, shape, dt))

        def sem(name):
            return ctx.enter_context(nc.semaphore(name))

        x2_rows = nc.dram_tensor("x2_rows", [T, D], F32)
        q_rows = nc.dram_tensor("q_rows", [NS, D], F32)
        y_rows = nc.dram_tensor("y_rows", [NROW, D], F32)

        arena = sb("arena", [P, 3 * 8192])
        act_mem = sb("act_mem", [P, A_SIZE])
        kv_mem = sb("kv_mem", [P, 4096])
        mk_mem = sb("mk_mem", [P, 2048])
        ident = sb("ident", [P, P])
        mean_d = sb("mean_d", [P, P])
        mean_c = sb("mean_c", [P, P])
        ones = sb("ones", [P, P])
        par = sb("par", [P, NPAR])
        wcb = sb("wcb", [P, WB * RC])
        gate_w = sb("gate_w", [P, 2, RC, P])
        rstd = sb("rstd", [P, T])
        tail = sb("tail", [38, 2, 512])
        h0t = sb("h0t", [P, RC, NS])
        c8 = sb("c8", [P, 8, RC])
        eps_t = sb("eps_t", [P, 1])
        small = sb("small", [P, 44])
        psum = ctx.enter_context(nc.psum_tensor("psum", [P, 4, D], F32))

        def rows(at, k):
            return act_mem[:, at:at + k * T].rearrange("p (k t) -> p k t", k=k)

        def halves(ap):
            return ap.rearrange("p (h t) -> p h t", h=2)

        def col(name, c):
            return par[:, PAR_AT[name] + c:PAR_AT[name] + c + 1]

        xT = rows(A0, KC)
        gT, uT = rows(A1, RC), rows(A1 + RC * T, RC)
        gluT, rT = rows(A2, RC), rows(A2 + RC * T, RC)
        cT, ucT = rows(A3, RC), rows(A3 + RC * T, RC)
        thT = rows(A4, RC)
        x_tok = act_mem[:, A3:A3 + TT * D].rearrange("p (t n) -> p t n", t=TT)
        raw_par = act_mem[0:P, A1:A1 + P]
        raw_wcb = act_mem[0:P, A1 + P:A1 + 2 * P]
        cbT = act_mem[:, A4 + 960:A4 + 1920].rearrange("p (c n) -> p c n", c=RC)
        caT = act_mem[:, A4 + 1920:A4 + 1920 + 96].rearrange("p (c n) -> p c n", c=RC)
        cprod = act_mem[:, A4:A4 + 240].rearrange("p (b j) -> p b j", b=NS)
        tap_mem = kv_mem[:, 2048:4096].rearrange("p (b n) -> p b n", b=4)
        csum = act_mem[:, A4 + 240:A4 + 248]
        sq = rows(A1, KC)
        sq_c = rows(A2, RC)
        st_cb = mk_mem[0:120, 0:1024].rearrange("p (r n) -> p r n", r=2)
        st_ca = mk_mem[0:24, 1024:1536]
        st_h = mk_mem[0:NS, 1536:2048]
        mem_tok = mk_mem[:, :].rearrange("p (m n) -> p m n", m=2)
        memT = kv_mem[:, 0:2048].rearrange("p (k m) -> p k m", k=KC)
        keyT = memT
        memT_late = act_mem[:, A2 + RC * T:A2 + RC * T + KC * P].rearrange("p (k m) -> p k m", k=KC)
        v_tok = kv_mem[:, 2048:4096].rearrange("p (m n) -> p m n", m=2)
        k_tok = mem_tok
        qT = rows(A2, KC)
        prT = rows(A1, KC)
        oT = rows(A3, KC)
        probs = act_mem[:, A4:A4 + 2048].rearrange("p (b h m) -> p b h m", b=2, h=XH)
        q_s = mk_mem[0:NS, 0:1024]
        junk = mk_mem[:, 1024:1280]
        ss = mk_mem[:, 1280:1344].rearrange("p (m n) -> p m n", m=2)
        sp = mk_mem[0:32, 1344:1600]
        spread_p = act_mem[:, A4 + 1024:A4 + 1536].rearrange("p (m h q) -> p m h q", m=2, h=XH)
        o_s = q_s
        xsum = act_mem[:, A4:A4 + T].rearrange("p (k t) -> p k t", k=1)
        base = act_mem[:, A1:A1 + TT * D].rearrange("p (t n) -> p t n", t=TT)
        ys = act_mem[:, 9280:9280 + 2048].rearrange("p (b n) -> p b n", b=2)
        silu = act_mem[:, 11328:11328 + 4 * CAP].rearrange("p (b n) -> p b n", b=2)
        sh1 = rows(A3, 2)
        shT = rows(A3 + 2 * T, 2)
        onehot = act_mem[:, 14560:14560 + TT * CAP].bitcast(BF16).rearrange("p (b t s) -> p b t s", b=2, t=TT)
        hidT = act_mem[:, 15840:15840 + 4 * CAP].rearrange("p (b n) -> p b n", b=2)
        xg = [act_mem[:, 0:D], act_mem[:, D:2 * D], mk_mem[:, 0:D], mk_mem[:, D:2 * D]]
        xgT = act_mem[:, 2048:2048 + 2 * KC * CAP].rearrange("p (b k s) -> p b k s", b=2, k=KC)
        place = act_mem[:, A4:A4 + TT * E].rearrange("p (t e) -> p t e", t=TT)
        table = act_mem[:, A4 + 320:A4 + 320 + 3 * TT * E].bitcast(BF16).rearrange("p (t e c) -> p t e c", t=TT, e=E)
        picked = act_mem[:, A4 + 1280:A4 + 1280 + 2 * NB].rearrange("p (n c) -> p n c", c=2)
        idx_y = sb("idx_y", [P, NB], U32)
        idx_x = sb("idx_x", [P, NB], U32)
        over = sb("over", [P, 1], I32)
        ln3g, ln3b = kv_mem[:, 0:1024], kv_mem[:, 1024:2048]
        R = [kv_mem[:, 2048 + 320 * n:2368 + 320 * n].rearrange("p (t e) -> p t e", t=TT) for n in range(6)]
        rbias = mk_mem[:, 0:64]
        rmax = mk_mem[:, 64:64 + 320].rearrange("p (t g j) -> p t g j", t=TT, g=8)
        gscore = mk_mem[:, 384:424].rearrange("p (t g) -> p t g", t=TT)
        grank = mk_mem[:, 424:464].rearrange("p (t g) -> p t g", t=TT)
        top8 = mk_mem[:, 464:504].rearrange("p (t g) -> p t g", t=TT)
        gsum = mk_mem[:, 504:509]
        row8 = mk_mem[:, 509:514]
        rmask = mk_mem[:, 514:519]
        tile8 = mk_mem[:, 1290:1295]
        wsum = mk_mem[:, 520:584]
        tri8 = mk_mem[:, 584:648].rearrange("p (g j) -> p g j", g=8)
        pair = mk_mem[:, 648:968].rearrange("p (t g j) -> p t g j", t=TT, g=8)
        pair2 = mk_mem[:, 968:1288].rearrange("p (t g j) -> p t g j", t=TT, g=8)
        cmax = mk_mem[:, 1288:1289]
        tri = gate_w[:, 0, 0, :]
        slots = gate_w[:, 0, 1, 0:CAP]
        slots_r = gate_w[:, 0, 2, 0:CAP]
        wr = gate_w[:, 1, :, :].rearrange("p c n -> p (c n)").rearrange("p (k e) -> p k e", k=KC)
        rounds_t = small[:, 38:38 + ROUNDS - 1]
        st6 = sb("st6", [P, 2, 6])
        y_in = [arena[:, 8192 * n:8192 * n + 8192].rearrange("p (j n) -> p j n", j=TOPK) for n in range(3)]

        def wb_tap(c, j):
            return wcb[:, j * RC + c:j * RC + c + 1]

        def wslot(n):
            return arena[:, 8192 * n:8192 * n + 8192].rearrange("p (k n) -> p k n", k=KC)

        def cache(n, b):
            return arena[:, 8192 * n + 2048 * b:8192 * n + 2048 * b + 2048].rearrange("p (m n) -> p m n", m=2)

        def ew(n):
            at = 6144 * n
            return (arena[:, at:at + 4096].rearrange("p (w k n) -> p w k n", w=2, k=KC),
                    arena[:, at + 4096:at + 6144].rearrange("p (k n) -> p k n", k=2))

        q_all = arena[:, 0:NS * D].rearrange("p (b n) -> p b n", b=NS)
        w1s = arena[:, 16384:18432].rearrange("p (k n) -> p k n", k=KC)
        w3s = arena[:, 18432:20480].rearrange("p (k n) -> p k n", k=KC)
        w2s = arena[:, 20480:22528].rearrange("p (k n) -> p k n", k=2)

        s_full = sem("s_full")
        s_emA = sem("s_emA")
        s_emV = sem("s_emV")
        s_par = sem("s_par")
        s_par2 = sem("s_par2")
        s_wcbl = sem("s_wcbl")
        s_state = sem("s_state")
        s_x = sem("s_x")
        s_gw = sem("s_gw")
        s_mem = sem("s_mem")
        s_load = [sem(f"s_load{n}") for n in range(12)]
        s_win = [sem(f"s_win{n}") for n in range(4)]
        s_out = sem("s_out")
        s_tailout = sem("s_tailout")
        s_stateout = sem("s_stateout")
        s_kout = sem("s_kout")
        s_const = sem("s_const")
        s_gwz = sem("s_gwz")
        s_late = sem("s_late")
        s_v = sem("s_v")
        s_glu = sem("s_glu")
        s_uc = sem("s_uc")
        s_convb = sem("s_convb")
        s_convp = sem("s_convp")
        s_memc = sem("s_memc")
        s_tap = sem("s_tap")
        s_c8 = sem("s_c8")
        s_tanh = sem("s_tanh")
        s_srt = sem("s_srt")
        s_root = sem("s_root")
        s_h = sem("s_h")
        s_ya = sem("s_ya")
        s_sub = sem("s_sub")
        s_sq = sem("s_sq")
        s_nrm = sem("s_nrm")
        s_ln = sem("s_ln")
        s_smax = sem("s_smax")
        s_prob = sem("s_prob")
        s_ssum = sem("s_ssum")
        s_x2out = sem("s_x2out")
        s_rt = sem("s_rt")
        s_wr = sem("s_wr")
        s_c8e = sem("s_c8e")
        s_late2 = sem("s_late2")
        s_rz = sem("s_rz")
        s_qrow = sem("s_qrow")
        s_qall = [sem(f"s_qall{n}") for n in range(4)]
        s_ss = sem("s_ss")
        s_spr = sem("s_spr")
        s_zero = sem("s_zero")
        s_xsum = sem("s_xsum")
        s_done = sem("s_done")
        s_lnw = sem("s_lnw")
        s_sel = sem("s_sel")
        s_table = sem("s_table")
        s_over = sem("s_over")
        s_rowv = sem("s_rowv")
        s_abs = sem("s_abs")

        s_w = [sem(f"s_w{n}") for n in range(4)]
        m_oh = sem("m_oh")
        m_ip = sem("m_ip")
        m_idx = sem("m_idx")
        m_iv = sem("m_iv")
        m_g = [sem(f"m_g{n}") for n in range(4)]
        m_xt = sem("m_xt")
        m_xc = sem("m_xc")
        m_h = sem("m_h")
        m_sl = sem("m_sl")
        m_hd = sem("m_hd")
        m_y = sem("m_y")
        m_ya = sem("m_ya")
        m_yv = sem("m_yv")
        m_s = [sem(f"m_s{n}") for n in range(2)]
        m_z = sem("m_z")
        m_go = sem("m_go")
        f_sem = {n: sem("f_" + n) for n in ("w", "oh", "ip", "iv", "idx", "g", "xt", "xc", "h", "sl", "hd", "y", "ya",
                                            "yv", "s", "it")}
        s_yin = [[sem(f"s_yin{q}{n}") for n in range(3)] for q in range(2)]
        s_ypool = sem("s_ypool")
        s_ysum = sem("s_ysum")
        s_final = sem("s_final")
        s_fin = sem("s_fin")
        s_sd = sem("s_sd")
        s_var = sem("s_var")
        s_res = sem("s_res")

        def emptied(eng, g):
            who = GROUPS[g][1]
            n = sum(1 for _, w in GROUPS[:g + 1] if w == who)
            eng.wait_ge(s_emA if who == "A" else s_emV, n)

        def wait_out(eng, name):
            emptied(eng, GID[name])

        def wait_full(eng, name):
            eng.wait_ge(s_full, GID[name] + 1)

        def bank(name):
            return psum[:, PAIR.get(name, GID[name] % 4), :]

        def two(ap):
            return ap.rearrange("p (h n) -> p h n", h=2)[:, :, 0:HALF]

        def load_parameters(eng, spec, s):
            for name, k in spec:
                a = I[name][0]
                src = a.rearrange("j (c p) -> (j c) p", p=P) if name == "w_conv_a" else a.rearrange("(c p) -> c p", p=P)
                eng.dma_start(raw_par[PAR_AT[name]:PAR_AT[name] + k, :], src).then_inc(s, 16)

        block = ctx.enter_context(nc.Block())

        @block.sync
        def _(sp):
            for t in range(4):
                sp.dma_start(x_tok[:, t, :], I["x_prompt"][0, t * P:(t + 1) * P, :]).then_inc(s_x, 16)
            sp.dma_start(x_tok[0:NS, 4, :], I["x_sample"][:, 0, :]).then_inc(s_x, 16)
            w_in = I["w_in"][0].rearrange("(k p) n -> p k n", p=P)
            for k in range(KC):
                sp.dma_start(wslot(0)[:, k, :], w_in[:, k, 1024:2048]).then_inc(s_win[k // 2], 16)
            for k in range(KC):
                sp.dma_start(wslot(1)[:, k, :], w_in[:, k, 0:1024]).then_inc(s_load[1], 16)

            def big(n, slot, src):
                sp.dma_start(wslot(slot), src.rearrange("(k p) n -> p k n", p=P)).then_inc(s_load[n], 16)

            def big_cache(n, slot, src, b0):
                for b in range(4):
                    sp.dma_start(cache(slot, b), src[0, b0 + b].rearrange("(p m) h d -> p m (h d)", m=2)).then_inc(
                        s_load[n], 16)

            big(2, 2, I["w_v"][0])
            wait_out(sp, "cb")
            sp.dma_start(mem_tok, I["mem_prompt"][0].rearrange("(m p) n -> p m n", p=P)).then_inc(s_mem, 16)
            wait_full(sp, "zs3")
            big(3, 0, I["w_k"][0])
            wait_full(sp, "zg3")
            big(4, 1, I["w_out"][0])
            wait_out(sp, "v0")
            sp.dma_start(o_mv[0, 0, 0:P].rearrange("m h d -> m (h d)"), v_tok[:, 0, :]).then_inc(s_out, 16)
            wait_full(sp, "ri3")
            sp.dma_start(wr, I["w_router"][0].rearrange("(k p) e -> p k e", p=P)).then_inc(s_wr, 16)
            wait_out(sp, "tails")
            sp.dma_start(o_cap[0, 0], tail[27:30, 0, :]).then_inc(s_tailout, 16)
            sp.dma_start(o_cas[0, :, 2, :], tail[30:38, 0, :]).then_inc(s_tailout, 16)
            sp.dma_start(o_cbp[0, 0], tail[0:30, 1, :]).then_inc(s_tailout, 16)
            sp.dma_start(o_cbs[0, :, 29, :], tail[30:38, 1, :]).then_inc(s_tailout, 16)
            wait_full(sp, "k1")
            big(5, 0, I["w_q"][0])
            for m in range(2):
                wait_out(sp, f"k{m}")
                sp.dma_start(o_mk[0, 0, m * P:(m + 1) * P].rearrange("m h d -> m (h d)"), k_tok[:, m, :]).then_inc(s_kout, 16)
            wait_out(sp, "hlast")
            sp.dma_start(o_hp[0], tail[0:1, 0, :]).then_inc(s_out, 16)
            sp.dma_start(o_hs[0], tail[1:9, 0, :]).then_inc(s_out, 16)
            wait_full(sp, "wo7")
            big_cache(6, 1, I["cache_mem_k"], 0)
            wait_full(sp, "v1b")
            big_cache(7, 2, I["cache_mem_k"], 4)
            wait_out(sp, "v1b")
            sp.dma_start(o_mv[0, 0, P:2 * P].rearrange("m h d -> m (h d)"), v_tok[:, 1, :]).then_inc(s_out, 16)
            wait_full(sp, "q7")
            wait_out(sp, "qs")
            sp.dma_start(q_rows[:, :], q_s).then_inc(s_qrow, 16)
            sp.wait_ge(s_qrow, 16)
            for b in range(NS):
                sp.dma_start(q_all[:, b, :], q_rows[b:b + 1, :].broadcast_to([P, D])).then_inc(s_qall[b // 2], 16)
            sp.wait_ge(s_ss, 4)
            big_cache(9, 1, I["cache_mem_v"], 0)
            sp.wait_ge(s_ss, NS)
            big_cache(10, 2, I["cache_mem_v"], 4)
            big(8, 0, I["w_o"][0])
            wait_full(sp, "osb")
            sp.dma_start(w1s, I["w1_s"][0].rearrange("(k p) n -> p k n", p=P)).then_inc(s_load[11], 16)
            sp.dma_start(w3s, I["w3_s"][0].rearrange("(k p) n -> p k n", p=P)).then_inc(s_load[11], 16)
            sp.dma_start(w2s, I["w2_s"][0].rearrange("(k p) n -> p k n", p=P)).then_inc(s_load[11], 16)
            wait_full(sp, "xo7")

            def expert(n, e, s):
                wu, wd = ew(n)
                sp.dma_start(wu[:, 0], I["w1_e"][0, e].rearrange("(p k) n -> p k n", k=KC)).then_inc(s, 16)
                sp.dma_start(wu[:, 1], I["w3_e"][0, e].rearrange("(p k) n -> p k n", k=KC)).then_inc(s, 16)
                sp.dma_start(wd, I["w2_e"][0, e].rearrange("(k p) n -> p k n", p=P)).then_inc(s, 16)

            expert(0, 0, s_w[0])
            expert(1, 1, s_w[1])
            wait_out(sp, "rank")
            sp.dma_start(ln3g, I["ln3_g"][0].rearrange("(a n) -> a n", a=1).broadcast_to([P, D])).then_inc(s_lnw, 16)
            sp.dma_start(ln3b, I["ln3_b"][0].rearrange("(a n) -> a n", a=1).broadcast_to([P, D])).then_inc(s_lnw, 16)
            wait_full(sp, "so4")
            expert(2, 2, s_w[2])
            expert(3, 3, s_w[3])
            with sp.Fori(0, E // 4 - 1) as i:
                for n in range(4):
                    sp.wait_ge(m_y, 4 * i + (n + 1))
                    expert(n, 4 * i + (n + 4), s_w[n])

            sp.wait_ge(s_over, 1)
            sp.wait_ge(m_y, E)
            n_max = sp.value_load(over[0:1, 0:1], min_val=0, max_val=T)
            with sp.If(n_max > CAP):
                with sp.Fori(1, E * (ROUNDS - 1) + 1) as i:
                    sp.wait_ge(f_sem["it"], i)
                    expert(0, (i - 1) % E, f_sem["w"])

            for p in range(2):
                sp.wait_ge(m_s[p], 16 * (E // 2))
            sp.wait_ge(s_done, 1)
            for n, t in enumerate(LAST_ORDER):
                w = width(t)
                if n >= 3:
                    sp.wait_ge(s_rowv, n - 2)
                for q, (j0, j1) in enumerate(PARTS):
                    sp.dma_start(y_in[n % 3][0:w, j0:j1, :],
                                 y_rows[t * D:t * D + w * TOPK, :].rearrange("(p j) n -> p j n", j=TOPK)[:, j0:j1, :]).then_inc(
                        s_yin[q][n % 3], 16)
            sp.wait_ge(s_out, 16 * (2 + 2))
            sp.wait_ge(s_final, 16 * TT)
            sp.wait_ge(s_tailout, 16 * 4)
            sp.wait_ge(s_stateout, 16 * 2)
            sp.wait_ge(s_kout, 16 * 2)

        @block.gpsimd
        def _(gp):
            load_parameters(gp, PAR_SPEC[8:], s_par2)
            gp.memset(ident[:, :], 0.0).then_inc(s_const, 1)
            gp.dma_start(st_h, I["state_rglru_h"][0]).then_inc(s_state, 16)
            gp.dma_start(st_ca, I["state_rglru_conv"][0].rearrange("b j n -> (b j) n")).then_inc(s_state, 16)
            for r in range(2):
                gp.dma_start(st_cb[:, r, :], I["state_dwconv"][0, 4 * r:4 * r + 4].rearrange("b j n -> (b j) n")).then_inc(s_state, 16)
            gp.wait_ge(s_const, 1)
            gp.affine_select(out=ident[:, :], in_=ident[:, :], compare_op=ALU.not_equal, fill=1.0, base=0,
                             pattern=[[-1, P]], channel_multiplier=1).then_inc(s_const, 1)
            gp.memset(mean_d[:, :], 1.0 / D).then_inc(s_const, 1)
            gp.memset(mean_c[:, :], 1.0 / 512).then_inc(s_const, 1)
            gp.memset(ones[:, :], 1.0).then_inc(s_const, 1)
            gp.memset(eps_t[:, :], EPS).then_inc(s_const, 1)
            gp.memset(gate_w[:, :, :, :], 0.0).then_inc(s_gwz, 1)
            gp.wait_ge(s_gwz, 1)
            for m, name in enumerate(("w_rg_a", "w_rg_x")):
                for q in range(2):
                    gp.dma_start(gate_w[64 * q:64 * q + 64, m, :, 64 * q:64 * q + 64],
                                 I[name][0].rearrange("(c q) i j -> q i c j", q=2)[q]).then_inc(s_gw, 16)
            gp.dma_start(o_cas[0, :, 0:WA - 2, :], I["state_rglru_conv"][0, :, 1:WA - 1, :]).then_inc(s_stateout, 16)
            gp.dma_start(o_cbs[0, :, 0:WB - 2, :], I["state_dwconv"][0, :, 1:WB - 1, :]).then_inc(s_stateout, 16)
            gp.wait_ge(s_glu, RC)
            for turn, c in enumerate(POOL_CHUNKS):
                x, out = gluT[:, c, :], cT[:, c, :]
                gp.tensor_scalar(out[:, 0:SEQ], x[:, 0:SEQ], wb_tap(c, WB - 1), col("b_conv_b", c),
                                 ALU.mult, ALU.add).then_inc(s_convp, 1)
                for n in range(1, WB):
                    product = turn * (WB - 1) + n - 1
                    gp.wait_ge(s_convp, turn * WB + n)
                    gp.wait_ge(s_tap, product + 1)
                    gp.tensor_tensor(out[:, n:SEQ], out[:, n:SEQ], tap_mem[:, product % 4, 0:SEQ - n], ALU.add).then_inc(s_convp, 1)
            wait_full(gp, "ri3")
            gp.memset(tri, 1.0).then_inc(s_late, 1)
            gp.iota(slots, pattern=[[1, CAP]], base=0, channel_multiplier=0, allow_small_or_imprecise_dtypes=True).then_inc(s_late, 1)
            gp.wait_ge(s_late, 2)
            gp.affine_select(out=tri, in_=tri, compare_op=ALU.is_gt, fill=0.0, base=0, pattern=[[1, P]],
                             channel_multiplier=-1).then_inc(s_late, 1)
            wait_full(gp, "pt3")
            gp.memset(spread_p, 0.0).then_inc(s_zero, 1)
            wait_full(gp, "osT")
            gp.memset(rmask, 1.0).then_inc(s_late, 1)
            gp.memset(tri8, 1.0).then_inc(s_late, 1)
            gp.iota(row8, pattern=[[0, TT]], base=0, channel_multiplier=TOPK,
                    allow_small_or_imprecise_dtypes=True).then_inc(s_late, 1)
            gp.iota(tile8, pattern=[[TOPK * P, TT]], base=-int(FAR), channel_multiplier=0,
                    allow_small_or_imprecise_dtypes=True).then_inc(s_late, 1)
            gp.wait_ge(s_late, 7)
            gp.affine_select(out=rmask[:, 4:5], in_=rmask[:, 4:5], compare_op=ALU.is_gt, fill=0.0, base=NS,
                             pattern=[[0, 1]], channel_multiplier=-1).then_inc(s_late, 1)
            gp.affine_select(out=tri8, in_=tri8, compare_op=ALU.is_gt, fill=0.0, base=0, pattern=[[1, 8], [-1, 8]],
                             channel_multiplier=0).then_inc(s_late, 1)
            gp.dma_start(rbias, I["router_bias"][0].rearrange("(a n) -> a n", a=1).broadcast_to([P, E])).then_inc(s_rt, 16)
            wait_full(gp, "h3b")
            gp.iota(rounds_t, pattern=[[CAP, ROUNDS - 1]], base=CAP, channel_multiplier=0,
                    allow_small_or_imprecise_dtypes=True).then_inc(s_late, 1)
            for n in range(2):
                gp.memset(xg[n], 0.0).then_inc(m_z, 1)
            gp.wait_ge(m_z, 2)
            gp.wait_ge(s_x2out, 16 * TT)

            last_x = gp.to_reg(T - 1)
            last_y = gp.to_reg(NROW - 1)

            def gather(n, b, s):
                gp.indirect_dma_start(
                    out=xg[b][0:CAP, :], out_offset=None, in_=x2_rows[:, :],
                    in_offset=bass.IndirectOffsetOnAxis(ap=idx_x[0:CAP, n:n + 1], axis=0),
                    bounds_check=last_x, oob_is_err=False).then_inc(s, 16)

            def scatter(n, b, s):
                gp.indirect_dma_start(
                    out=y_rows[:, :], out_offset=bass.IndirectOffsetOnAxis(ap=idx_y[0:CAP, n:n + 1], axis=0),
                    in_=ys[0:CAP, b, :], in_offset=None,
                    bounds_check=last_y, oob_is_err=False).then_inc(s, 16)

            def g_step(e, n):
                gp.wait_ge(s_x2out, 16 * TT)
                gp.wait_ge(m_idx, e + 1)
                if at_least(e, 4):
                    gp.wait_ge(m_xt, e - 3)
                gp.sem_inc(m_go, 1)
                gather(n, n % 4, m_g[n % 4])

            def s_step(e, n):
                gp.wait_ge(m_ya, e + 1)
                gp.wait_ge(m_yv, e + 1)
                gp.sem_inc(m_go, 1)
                scatter(n, n % 2, m_s[n % 2])

            g_step(0, 0)
            g_step(1, 1)
            gp.wait_ge(s_table, 1)
            gp.wait_ge(s_over, 1)
            for n in range(2, 4):
                gp.memset(xg[n], 0.0).then_inc(m_z, 1)
            gp.wait_ge(m_z, 4)
            g_step(2, 2)
            g_step(3, 3)
            for e in range(1, NB + 1):
                s_step(e - 1, (e - 1) % NB)
                g_step(e + 3, (e + 3) % NB)
            with gp.Fori(1, E // NB - 1) as i:
                for k in range(1, NB + 1):
                    s_step(NB * i + (k - 1), (k - 1) % NB)
                    g_step(NB * i + (k + 3), (k + 3) % NB)
            for e in range(E - NB + 1, E + 1):
                s_step(e - 1, (e - 1) % NB)
                if e + 3 < E:
                    g_step(e + 3, (e + 3) % NB)

            gp.wait_ge(s_over, 1)
            n_max = gp.value_load(over[0:1, 0:1], min_val=0, max_val=T)
            with gp.If(n_max > CAP):
                gp.wait_ge(m_g[0], 16 * (E // 4))
                gp.wait_ge(m_s[0], 16 * (E // 2))
                gp.wait_ge(m_s[1], 16 * (E // 2))
                gp.sem_inc(f_sem["it"], 1)
                with gp.Fori(1, E * (ROUNDS - 1) + 1) as i:
                    gp.wait_ge(s_x2out, 16 * TT)
                    gp.wait_ge(f_sem["idx"], i)
                    gp.sem_inc(m_go, 1)
                    gather(0, 0, f_sem["g"])
                    gp.wait_ge(f_sem["ya"], i)
                    gp.wait_ge(f_sem["yv"], i)
                    gp.sem_inc(m_go, 1)
                    scatter(0, 0, f_sem["s"])
                    gp.wait_ge(f_sem["s"], 16 * i)
                    gp.sem_inc(f_sem["it"], 1)
            gp.sem_inc(s_done, 1)
            for n, t in enumerate(LAST_ORDER):
                w = width(t)
                a, b = (y_in[n % 3][0:w, j, :] for j in POOL_ROWS)
                gp.wait_ge(s_yin[0][n % 3], 16 * (n // 3 + 1))
                gp.tensor_tensor(a, a, b, ALU.add).then_inc(s_ypool, 1)

        @block.tensor
        def _(pe):
            def open_group(name):
                g = GID[name]
                if g >= 4:
                    emptied(pe, g - 4)
                return bank(name)

            def mm(out, lhsT, rhs, first, last):
                return pe.matmul(out, lhsT, rhs, start=first, stop=last)

            def wide(name, w, act, ks, before=None):
                ps = open_group(name)
                for n, k in enumerate(ks):
                    if before is not None:
                        before(k)
                    for h in range(2):
                        last = mm(ps[:, 512 * h:512 * h + HALF], w(k), act(k)[:, HALF * h:HALF * h + HALF],
                                  n == 0, n == len(ks) - 1)
                last.then_inc(s_full, 1)

            def turn(out, in_, n=P):
                return pe.transpose(out, in_, ident[0:n, 0:n])

            pe.wait_ge(s_const, 2)
            pe.wait_ge(s_x, 16 * TT)
            for c in range(KC):
                ps = open_group(f"x{c}")
                for t in range(TT):
                    w = width(t)
                    last = turn(ps[:, t * P:t * P + w], x_tok[0:w, t, c * P:(c + 1) * P], w)
                last.then_inc(s_full, 1)
            pe.wait_ge(s_const, 6)
            pe.wait_ge(s_par, 16 * 8)
            pe.wait_ge(s_par2, 16 * (len(PAR_SPEC) - 8))
            pe.wait_ge(s_wcbl, 16)
            ps = open_group("par")
            turn(ps[:, 0:NPAR], raw_par[0:NPAR, :], NPAR)
            turn(ps[:, 512:512 + WB * RC], raw_wcb[0:WB * RC, :], WB * RC).then_inc(s_full, 1)

            def first_weights(k):
                wait_out(pe, f"x{k}")
                if k % 2 == 0:
                    pe.wait_ge(s_win[k // 2], 16 * 2)

            def turn_states():
                pe.wait_ge(s_state, 16 * 4)
                ps = open_group("st")
                for c in range(RC):
                    turn(ps[:, NS * c:NS * c + NS], st_h[:, c * P:(c + 1) * P], NS)
                for c in range(RC):
                    last = turn(ps[:, 32 + 24 * c:32 + 24 * c + 24], st_ca[:, c * P:(c + 1) * P], 24)
                last.then_inc(s_full, 1)
                ps = open_group("cb")
                for c in range(RC):
                    for r in range(2):
                        at = 512 * (c // 2) + 240 * (c % 2) + 120 * r
                        last = turn(ps[:, at:at + 120], st_cb[:, r, c * P:(c + 1) * P], 120)
                last.then_inc(s_full, 1)

            for j in range(2 * RC):
                if j == RC:
                    turn_states()
                name = ("zv", "zs")[j // RC] + str(j % RC)
                wide(name, lambda k: wslot(0)[:, k, j * P:(j + 1) * P], lambda k: xT[:, k, :], range(KC),
                     before=first_weights if j == 0 else None)
            pe.wait_ge(s_load[1], 16 * KC)
            for j in range(2 * RC):
                name = ("zu", "zg")[j // RC] + str(j % RC)
                at = (j + RC) % (2 * RC)
                wide(name, lambda k: wslot(1)[:, k, at * P:(at + 1) * P], lambda k: xT[:, k, :], range(KC))
            pe.wait_ge(s_mem, 16)
            for g in range(2):
                ps = open_group(f"mt{g}")
                for c in range(4):
                    for m in range(2):
                        last = turn(ps[:, 256 * c + P * m:256 * c + P * m + P], mem_tok[:, m, (4 * g + c) * P:(4 * g + c + 1) * P])
                last.then_inc(s_full, 1)

            def memory(names, w, s, first=0):
                pe.wait_ge(s, 16)
                for m, name in enumerate(names, first):
                    ps = open_group(name)
                    for k in range(KC):
                        for n in range(2):
                            last = mm(ps[:, 512 * n:512 * n + 512], memT[:, k, m * P:(m + 1) * P],
                                      w[:, k, 512 * n:512 * n + 512], k == 0, k == KC - 1)
                    last.then_inc(s_full, 1)

            wait_out(pe, "mt1")
            memory(("v0",), wslot(2), s_load[2])
            wait_out(pe, "zu3")
            pe.wait_ge(s_glu, RC)
            ps = open_group("tails")
            for c in range(RC):
                turn(ps[0:38, c * P:(c + 1) * P], uT[:, c, T - 38:T])
            for c in range(RC):
                last = turn(ps[0:38, 512 + c * P:512 + (c + 1) * P], gluT[:, c, T - 38:T])
            last.then_inc(s_full, 1)
            pe.wait_ge(s_gw, 16 * 4)
            pe.wait_ge(s_uc, 1)
            for m, name in enumerate(("ra", "ri")):
                for c in range(RC):
                    wide(f"{name}{c}", lambda k: gate_w[:, m, c, :], lambda k: ucT[:, c, :], range(1))

            norm_at = [0]

            def norm_mean(name, w, x, n):
                wide(name, lambda k: w[:, :], lambda k: x[:, k, :], range(n))

            def norm_var(name, w, sqs, n):
                wide(name, lambda k: w[:, :], lambda k: sqs[:, k, :], range(n),
                     before=lambda k: pe.wait_ge(s_sq, norm_at[0] + k + 1))
                norm_at[0] += n

            memory(("k0",), wslot(0), s_load[3])
            pe.wait_ge(s_convb, 1)
            pe.wait_ge(s_convp, len(POOL_CHUNKS) * WB)
            norm_mean("cmean", mean_c, cT, RC)
            memory(("k1",), wslot(0), s_load[3], 1)
            norm_var("cvar", mean_c, sq_c, RC)
            wait_out(pe, "k1")
            for g in range(2):
                ps = open_group(f"kt{g}")
                for c in range(4):
                    for m in range(2):
                        last = turn(ps[:, 256 * c + P * m:256 * c + P * m + P], k_tok[:, m, (4 * g + c) * P:(4 * g + c + 1) * P])
                last.then_inc(s_full, 1)
            pe.wait_ge(s_h, RC)
            ps = open_group("hlast")
            for c in range(RC):
                last = turn(ps[0:9, c * P:(c + 1) * P], ucT[:, c, SEQ - 1:T])
            last.then_inc(s_full, 1)
            pe.wait_ge(s_load[4], 16)

            def mixed(k):
                if k < RC:
                    pe.wait_ge(s_ya, k + 1)
                else:
                    pe.wait_ge(s_ln, k - RC + 1)

            for j in range(KC):
                wide(f"wo{j}", lambda k: wslot(1)[:, k, j * P:(j + 1) * P],
                     lambda k: gT[:, k, :] if k < RC else cT[:, k - RC, :], range(KC), before=mixed if j == 0 else None)
            wait_out(pe, "wo7")

            def value_half(name, n):
                ps = open_group(name)
                pe.wait_ge(s_memc, 1)
                for k in range(KC):
                    last = mm(ps[:, 0:512], memT_late[:, k, :], wslot(2)[:, k, 512 * n:512 * n + 512], k == 0, k == KC - 1)
                last.then_inc(s_full, 1)

            pe.wait_ge(s_xsum, 1)
            norm_mean("mean1", mean_d, xsum, 1)
            value_half("v1a", 0)
            norm_var("var1", mean_d, sq, KC)
            value_half("v1b", 1)
            pe.wait_ge(s_load[5], 16)
            for j in range(KC):
                wide(f"q{j}", lambda k: wslot(0)[:, k, j * P:(j + 1) * P], lambda k: xT[:, k, :], range(KC),
                     before=(lambda k: pe.wait_ge(s_ln, RC + k + 1)) if j == 0 else None)
            wait_out(pe, "q7")
            ps = open_group("qs")
            for c in range(KC):
                last = turn(ps[0:NS, c * P:(c + 1) * P], qT[:, c, SEQ:T])
            last.then_inc(s_full, 1)

            def scores(t):
                ps = open_group(f"sc{t}")
                for h in range(XH):
                    for d in range(2):
                        last = mm(ps[:, XD * h:XD * h + XD], qT[:, 2 * h + d, t * P:(t + 1) * P], keyT[:, 2 * h + d, :],
                                  d == 0, d == 1)
                last.then_inc(s_full, 1)

            def turn_probs(t):
                pe.wait_ge(s_prob, t + 1)
                ps = open_group(f"pt{t}")
                for h in range(XH):
                    for m in range(2):
                        at = (2 * h + m) * P
                        last = turn(ps[:, at:at + P], probs[:, t % 2, h, m * P:(m + 1) * P])
                last.then_inc(s_full, 1)

            def prompt_out(j):
                ps = open_group(f"o{j}")
                if j == 0:
                    wait_out(pe, "pt3")
                for m in range(2):
                    last = mm(ps[:, 0:SEQ], v_tok[:, m, j * P:(j + 1) * P], prT[:, 2 * (j // 2) + m, 0:SEQ], m == 0, m == 1)
                last.then_inc(s_full, 1)

            def turn_sample_scores():
                ps = open_group("ssT")
                pe.wait_ge(s_ss, NS)
                for m in range(2):
                    last = turn(ps[0:32, m * P:(m + 1) * P], ss[:, m, :])
                last.then_inc(s_full, 1)

            def turn_sample_probs():
                ps = open_group("spT")
                pe.wait_ge(s_prob, 5)
                for m in range(2):
                    last = turn(ps[:, 32 * m:32 * m + 32], sp[:, m * P:(m + 1) * P], 32)
                last.then_inc(s_full, 1)

            for name in ATTENTION:
                if name == "ssT":
                    turn_sample_scores()
                elif name == "spT":
                    turn_sample_probs()
                elif name[0] == "o":
                    prompt_out(int(name[1]))
                else:
                    {"sc": scores, "pt": turn_probs}[name[0:2]](int(name[2]))
            wait_out(pe, "spT")
            pe.wait_ge(s_spr, 1)
            for half, name in enumerate(("osa", "osb")):
                pe.wait_ge(s_load[9 + half], 16 * 4)
                ps = open_group(name)
                for h in range(XH):
                    for b in range(4 * half, 4 * half + 4):
                        for m in range(2):
                            last = mm(ps[0:NS, XD * h:XD * h + XD], spread_p[:, m, h, NS * b:NS * b + NS],
                                      cache(1 + half, b % 4)[:, m, XD * h:XD * h + XD], (b % 4, m) == (0, 0), (b % 4, m) == (3, 1))
                last.then_inc(s_full, 1)
            wait_out(pe, "osb")
            ps = open_group("osT")
            for j in range(KC):
                last = turn(ps[:, NS * j:NS * j + NS], o_s[:, j * P:(j + 1) * P], NS)
            last.then_inc(s_full, 1)
            pe.wait_ge(s_load[8], 16)
            ps = open_group("xo0")
            for h in range(2):
                if h == 1:
                    wait_out(pe, "osT")
                for k in range(KC):
                    last = mm(ps[:, 512 * h:512 * h + HALF], wslot(0)[:, k, 0:P], oT[:, k, HALF * h:HALF * h + HALF], k == 0, k == KC - 1)
            last.then_inc(s_full, 1)
            for j in range(1, KC):
                wide(f"xo{j}", lambda k: wslot(0)[:, k, j * P:(j + 1) * P], lambda k: oT[:, k, :], range(KC))
            pe.wait_ge(s_xsum, 2)
            norm_mean("mean2", mean_d, xsum, 1)
            norm_var("var2", mean_d, sq, KC)
            pe.wait_ge(s_load[11], 16 * 3)
            wide("h1a", lambda k: w1s[:, k, 0:P], lambda k: xT[:, k, :], range(KC),
                 before=lambda k: pe.wait_ge(s_ln, RC + KC + k + 1))
            pe.wait_ge(s_wr, 16)
            ps = open_group("rt")
            for t in range(TT):
                w = width(t)
                for k in range(KC):
                    last = mm(ps[0:w, E * t:E * t + E], xT[:, k, t * P:t * P + w], wr[:, k, :], k == 0, k == KC - 1)
            last.then_inc(s_full, 1)
            for t in range(TT):
                w = width(t)
                ps = open_group(f"x2{t}")
                for k in range(KC):
                    last = turn(ps[0:w, k * P:(k + 1) * P], xT[:, k, t * P:t * P + w])
                last.then_inc(s_full, 1)
            for j in range(2):
                for name, w in (("h1", w1s), ("h3", w3s)):
                    if (name, j) == ("h1", 0):
                        continue
                    wide(name + "ab"[j], lambda k: w[:, k, j * P:(j + 1) * P], lambda k: xT[:, k, :], range(KC))
            pe.wait_ge(s_late, 9)
            pe.wait_ge(s_sel, 1)
            ps = open_group("rank")
            sel = R[2]
            for t in range(TT):
                for u in range(t + 1):
                    last = mm(ps[:, E * t:E * t + E], tri if u == t else ones[:, :], sel[:, u, :], u == 0, u == t)
            last.then_inc(s_full, 1)
            ps = open_group("count")
            for t in range(TT):
                last = mm(ps[:, 0:E], ones[:, :], sel[:, t, :], t == 0, t == TT - 1)
            last.then_inc(s_full, 1)
            wait_out(pe, "h1b")
            wait_out(pe, "count")

            def shared_out(t):
                w = width(t)
                if t >= 3:
                    wait_out(pe, f"so{t - 3}")
                ps = bank(f"so{t}")
                for k in range(2):
                    for n in range(2):
                        last = mm(ps[0:w, 512 * n:512 * n + 512], shT[:, k, t * P:t * P + w], w2s[:, k, 512 * n:512 * n + 512],
                                  k == 0, k == 1)
                last.then_inc(s_full, 1)

            pe.wait_ge(s_table, 1)

            def find(n, e):
                for t in range(TT):
                    last = mm(psum[0:CAP, 3, 512 * (n % 2):512 * (n % 2) + 6], onehot[:, n % 2, t, :], table[:, t, e, :],
                              t == 0, t == TT - 1)
                return last

            def turn_rows(n):
                for k in range(KC):
                    at = 512 * (k // 4) + CAP * (k % 4)
                    last = turn(psum[:, 1, at:at + CAP], xg[n % 4][0:CAP, k:D:KC], CAP)
                return last

            def up(b, part):
                wu, _ = ew(part)
                for j in range(4):
                    at = 512 * b + CAP * j
                    for k in range(KC):
                        last = mm(psum[:, 2, at:at + CAP], wu[:, j // 2, k, P * (j % 2):P * (j % 2) + P], xgT[:, b, k, :],
                                  k == 0, k == KC - 1)
                return last

            def down(b, part):
                _, wd = ew(part)
                for n in range(2):
                    for k in range(2):
                        last = mm(psum[0:CAP, 0, 512 * n:512 * n + 512], hidT[:, b, CAP * k:CAP * k + CAP],
                                  wd[:, k, 512 * n:512 * n + 512], k == 0, k == 1)
                return last

            def a_step(e, n):
                pe.wait_ge(m_oh, e + 1)
                if at_least(e, 2):
                    pe.wait_ge(m_idx, e - 1)
                find(n, e).then_inc(m_ip, 1)

            def b_step(e, n, gath):
                pe.wait_ge(m_g[n % 4], gath)
                if at_least(e, 1):
                    pe.wait_ge(m_xc, e)
                turn_rows(n).then_inc(m_xt, 1)

            def c_step(e, n, wait_w):
                pe.wait_ge(m_xc, e + 1)
                pe.wait_ge(s_w[n % 4], wait_w)
                if at_least(e, 2):
                    pe.wait_ge(m_hd, e - 1)
                up(n % 2, n % 4).then_inc(m_h, 1)

            def y_step(e, n):
                pe.wait_ge(m_hd, e + 1)
                if at_least(e, 1):
                    pe.wait_ge(m_ya, e)
                    pe.wait_ge(m_yv, e)
                down(n % 2, n % 4).then_inc(m_y, 1)

            a_step(0, 0)
            a_step(1, 1)
            shared_out(0)
            shared_out(1)
            a_step(2, 2)
            shared_out(2)
            a_step(3, 3)
            shared_out(3)
            shared_out(4)
            wait_out(pe, "so4")
            b_step(0, 0, 16)
            c_step(0, 0, 48)
            b_step(1, 1, 16)

            def step(e, k, i):
                c_step(e, k % NB, 48 * (2 * i + (k // 4 + 1)))
                if exists(e + 1):
                    b_step(e + 1, (k + 1) % NB, 16 * (2 * i + ((k + 1) // 4 + 1)))
                y_step(e - 1, (k - 1) % NB)
                if exists(e + 3):
                    a_step(e + 3, (k + 3) % NB)

            LAST = E // NB - 1
            for k in range(1, NB + 1):
                step(k, k, 0)
            with pe.Fori(1, LAST) as i:
                for k in range(1, NB + 1):
                    step(NB * i + k, k, i)
            for k in range(1, NB):
                step(NB * LAST + k, k, LAST)
            y_step(E - 1, NB - 1)

            pe.wait_ge(s_over, 1)
            n_max = pe.value_load(over[0:1, 0:1], min_val=0, max_val=T)
            with pe.If(n_max > CAP):
                pe.wait_ge(m_ya, E)
                pe.wait_ge(m_yv, E)
                with pe.Fori(0, E * (ROUNDS - 1)) as i:
                    pe.wait_ge(f_sem["oh"], i + 1)
                    find(0, i % E).then_inc(f_sem["ip"], 1)
                    pe.wait_ge(f_sem["g"], 16 * i + 16)
                    turn_rows(0).then_inc(f_sem["xt"], 1)
                    pe.wait_ge(f_sem["xc"], i + 1)
                    pe.wait_ge(f_sem["w"], 48 * i + 48)
                    up(0, 0).then_inc(f_sem["h"], 1)
                    pe.wait_ge(f_sem["hd"], i + 1)
                    down(0, 0).then_inc(f_sem["y"], 1)

            pe.wait_ge(m_ya, E)
            pe.wait_ge(m_yv, E)
            for n, t in enumerate(LAST_ORDER):
                w = width(t)
                if w < P:
                    continue
                if n >= 4:
                    pe.wait_ge(s_rowv, n - 3)
                for q in range(2):
                    pe.wait_ge(s_yin[q][n % 3], 16 * (n // 3 + 1))
                    for j in PE_ROWS[q]:
                        for h in range(2):
                            last = mm(psum[0:w, n % 4, 512 * h:512 * h + 512], ident[0:w, 0:w],
                                      y_in[n % 3][0:w, j, 512 * h:512 * h + 512], j == 2, j == 7)
                last.then_inc(s_ysum, 1)

        @block.scalar
        def _(act):
            load_parameters(act, PAR_SPEC[:8], s_par)
            act.dma_start(raw_wcb[0:WB * RC, :], I["w_conv_b"][0].rearrange("j (c p) -> (j c) p", p=P)).then_inc(s_wcbl, 16)

            def empty(name, out, func=ACT.Copy, **kw):
                wait_full(act, name)
                act.activation(out, two(bank(name)), func, **kw).then_inc(s_emA, 1)

            for c in range(0, KC, 2):
                wait_full(act, f"x{c}")
                act.activation(xT[:, c, :], bank(f"x{c}")[:, 0:T], ACT.Copy).then_inc(s_emA, 1)
            wait_out(act, "par")
            act.activation(c8[:, 0, :], par[:, PAR_AT["rg_lambda"]:PAR_AT["rg_lambda"] + RC], ACT.Abs).then_inc(s_abs, 1)
            act.wait_ge(s_abs, 1)
            act.activation(c8[:, 1, :], c8[:, 0, :], ACT.Exp, scale=-1.0).then_inc(s_c8e, 1)
            for c in range(RC):
                empty(f"zv{c}", halves(gluT[:, c, :]), ACT.Identity, bias=col("b_in", 8 + c))
            for c in range(RC):
                empty(f"zs{c}", halves(rT[:, c, :]), ACT.Sigmoid, bias=col("b_in", 12 + c))

            def tap_products(products):
                for product in products:
                    turn, n = product // (WB - 1), product % (WB - 1) + 1
                    c = POOL_CHUNKS[turn]
                    if product >= 4:
                        before = product - 4
                        act.wait_ge(s_convp, before // (WB - 1) * WB + before % (WB - 1) + 2)
                    act.activation(tap_mem[:, product % 4, 0:SEQ - n], gluT[:, c, 0:SEQ - n], ACT.Copy,
                                   scale=wb_tap(c, WB - 1 - n)).then_inc(s_tap, 1)

            for j in range(2 * RC):
                c = j % RC
                if j < RC:
                    empty(f"zu{c}", halves(uT[:, c, :]), ACT.Identity, bias=col("b_in", 4 + c))
                else:
                    empty(f"zg{c}", halves(gT[:, c, :]), ACT.Gelu_apprx_tanh, bias=col("b_in", c))
                if j == 0:
                    act.wait_ge(s_glu, RC)
                n_products = len(POOL_CHUNKS) * (WB - 1)
                tap_products(range(n_products * j // (2 * RC), n_products * (j + 1) // (2 * RC)))
            for g in range(2):
                wait_full(act, f"mt{g}")
                act.activation(memT[:, 4 * g:4 * g + 4, :], bank(f"mt{g}").rearrange("p (c m) -> p c m", c=4), ACT.Copy).then_inc(s_emA, 1)
            act.wait_ge(s_convp, len(POOL_CHUNKS) * WB)
            wait_full(act, "v0")
            act.activation(v_tok[:, 0, :], bank("v0"), ACT.Copy).then_inc(s_emA, 1)
            wait_full(act, "tails")
            act.activation(tail[:, :, :], bank("tails")[0:38, :].rearrange("p (m n) -> p m n", m=2), ACT.Copy).then_inc(s_emA, 1)
            act.wait_ge(s_glu, RC)
            for c in range(RC):
                empty(f"ra{c}", halves(rT[:, c, :]), ACT.Sigmoid, bias=col("b_rg_a", c))
            wait_full(act, "tails")
            act.wait_ge(s_uc, 1)
            for c in range(RC):
                empty(f"ri{c}", halves(uT[:, c, :]), ACT.Sigmoid, bias=col("b_rg_x", c))
            act.wait_ge(s_c8, 1)
            act.wait_ge(s_convb, 1)
            wait_out(act, "ra3")
            for c in range(RC):
                act.activation(thT[:, c, :], rT[:, c, :], ACT.Tanh, scale=c8[:, 7, c:c + 1]).then_inc(s_tanh, 1)

            wait_full(act, "k0")
            act.activation(k_tok[:, 0, :], bank("k0"), ACT.Copy).then_inc(s_emA, 1)
            norm_at = [0]

            def norm_squares(x, sqs, n):
                for k in range(n):
                    act.wait_ge(s_sub, norm_at[0] + k + 1)
                    act.activation(sqs[:, k, :], x[:, k, :], ACT.Square).then_inc(s_sq, 1)

            def norm_root(var):
                empty(var, halves(rstd[:, :]), ACT.Sqrt, bias=eps_t[:, 0:1])

            def norm_gain(x, n, g, b, func):
                for k in range(n):
                    act.wait_ge(s_nrm, norm_at[0] + k + 1)
                    act.activation(x[:, k, :], x[:, k, :], func, bias=col(b, k), scale=col(g, k)).then_inc(s_ln, 1)
                norm_at[0] += n

            norm_squares(cT, sq_c, RC)
            wait_full(act, "k1")
            act.activation(k_tok[:, 1, :], bank("k1"), ACT.Copy).then_inc(s_emA, 1)
            for c in range(RC):
                act.wait_ge(s_srt, c + 1)
                act.activation(thT[:, c, :], thT[:, c, :], ACT.Sqrt, scale=-2.0).then_inc(s_root, 1)
            norm_root("cvar")
            act.wait_ge(s_h, RC)
            act.activation(memT_late, memT[:, :, P:2 * P], ACT.Copy).then_inc(s_memc, 1)
            act.wait_ge(s_memc, 1)
            for g in range(2):
                wait_full(act, f"kt{g}")
                act.activation(keyT[:, 4 * g:4 * g + 4, :], bank(f"kt{g}").rearrange("p (c m) -> p c m", c=4), ACT.Copy).then_inc(s_emA, 1)
            norm_gain(cT, RC, "ln_c_g", "ln_c_b", ACT.Silu)
            wait_full(act, "wo7")
            norm_squares(xT, sq, KC)
            wait_full(act, "v1a")
            act.activation(v_tok[:, 1, 0:512], bank("v1a")[:, 0:512], ACT.Copy).then_inc(s_emA, 1)
            norm_root("var1")
            norm_gain(xT, KC, "ln1_g", "ln1_b", ACT.Identity)
            wait_full(act, "v1b")
            act.activation(v_tok[:, 1, 512:1024], bank("v1b")[:, 0:512], ACT.Copy).then_inc(s_emA, 1)
            for c in range(KC):
                empty(f"q{c}", halves(qT[:, c, :]))
            act.wait_ge(s_kout, 16 * 2)
            wait_full(act, "qs")
            act.activation(q_s, bank("qs")[0:NS, :], ACT.Copy).then_inc(s_emA, 1)

            def softmax_exp(t):
                act.wait_ge(s_smax, t + 1)
                if t >= 2:
                    wait_full(act, f"pt{t - 2}")
                for h in range(XH):
                    last = act.activation(probs[:, t % 2, h, :], bank(f"sc{t}")[:, XD * h:XD * h + XD], ACT.Exp,
                                          bias=small[:, 4 + h:5 + h] if t % 2 == 0 else small[:, 12 + h:13 + h],
                                          scale=XD ** -0.5,
                                          accum_out=small[:, 16 + 4 * (t % 2) + h:17 + 4 * (t % 2) + h])
                    if h < XH - 1:
                        last.then_inc(s_ssum, 1)
                last.then_inc(s_emA, 1)

            def take_probs(t):
                wait_full(act, f"pt{t}")
                act.activation(prT[:, :, t * P:(t + 1) * P], bank(f"pt{t}").rearrange("p (k n) -> p k n", k=KC), ACT.Copy).then_inc(s_emA, 1)

            def take_out(j):
                wait_full(act, f"o{j}")
                act.activation(oT[:, j, 0:SEQ], bank(f"o{j}")[:, 0:SEQ], ACT.Copy).then_inc(s_emA, 1)

            for name in ATTENTION:
                if name == "ssT":
                    act.wait_ge(s_smax, 5)
                    act.activation(sp, bank("ssT")[0:32, 0:N_MEM], ACT.Exp, bias=small[0:32, 25:26], scale=XD ** -0.5,
                                   accum_out=small[0:32, 26:27]).then_inc(s_emA, 1)
                elif name == "spT":
                    wait_full(act, "spT")
                    act.wait_ge(s_zero, 1)
                    for m in range(2):
                        last = act.activation(spread_p[:, m, :, 0:64:NS + 1],
                                              bank("spT")[:, 32 * m:32 * m + 32].rearrange("p (b h) -> p h b", h=XH), ACT.Copy)
                        if m == 0:
                            last.then_inc(s_spr, 1)
                    last.then_inc(s_emA, 1)
                elif name[0] == "o":
                    take_out(int(name[1]))
                elif name[0:2] == "sc":
                    softmax_exp(int(name[2]))
                elif name[0:2] == "pt":
                    take_probs(int(name[2]))
            wait_full(act, "osa")
            act.activation(o_s, bank("osa")[0:NS, :], ACT.Copy).then_inc(s_emA, 1)
            wait_full(act, "osT")
            act.activation(oT[:, :, SEQ:T], bank("osT")[:, 0:64].rearrange("p (j b) -> p j b", j=KC), ACT.Copy).then_inc(s_emA, 1)
            norm_squares(xT, sq, KC)
            norm_root("var2")
            norm_gain(xT, KC, "ln2_g", "ln2_b", ACT.Identity)
            empty("h1a", halves(sh1[:, 0, :]), ACT.Silu)
            act.wait_ge(s_rz, 1)
            wait_full(act, "rt")
            act.activation(R[0][:, 0:4, :], bank("rt")[:, 0:4 * E].rearrange("p (t e) -> p t e", t=4), ACT.Sigmoid).then_inc(s_ssum, 1)
            act.activation(R[0][0:NS, 4, :], bank("rt")[0:NS, 4 * E:5 * E], ACT.Sigmoid).then_inc(s_emA, 1)
            for t in range(TT):
                w = width(t)
                wait_full(act, f"x2{t}")
                act.activation(base[0:w, t, :], bank(f"x2{t}")[0:w, :], ACT.Copy).then_inc(s_emA, 1)
                emptied(act, GID[f"x2{t}"])
                act.dma_start(x2_rows[t * P:t * P + w, :], base[0:w, t, :]).then_inc(s_x2out, 16)
            empty("h1b", halves(sh1[:, 1, :]), ACT.Silu)

            def xc(b):
                return act.activation(xgT[:, b, :, :].rearrange("p (h k) s -> p h (k s)", h=2),
                                      psum[:, 1, :].rearrange("p (h n) -> p h n", h=2)[:, :, 0:4 * CAP], ACT.Copy)

            def sl(b):
                return act.activation(silu[:, b, :], psum[:, 2, 512 * b:512 * b + 2 * CAP], ACT.Silu)

            def yh(b, n):
                return act.activation(ys[0:CAP, b, 0:512], psum[0:CAP, 0, 0:512], ACT.Copy, scale=picked[0:CAP, n, 1:2])

            def b_step(e, n):
                act.wait_ge(m_xt, e + 1)
                if at_least(e, 2):
                    act.wait_ge(m_h, e - 1)
                xc(n % 2).then_inc(m_xc, 1)

            def c_step(e, n):
                act.wait_ge(m_h, e + 1)
                if at_least(e, 2):
                    act.wait_ge(m_hd, e - 1)
                sl(n % 2).then_inc(m_sl, 1)

            def y_step(e, n, sc):
                act.wait_ge(m_y, e + 1)
                if sc is not None:
                    act.wait_ge(m_s[n % 2], sc)
                yh(n % 2, n).then_inc(m_ya, 1)

            def step(e, k, i, sc):
                c_step(e, k % NB)
                if exists(e + 1):
                    b_step(e + 1, (k + 1) % NB)
                y_step(e - 1, (k - 1) % NB, sc)

            LAST = E // NB - 1
            b_step(0, 0)
            c_step(0, 0)
            b_step(1, 1)
            for k in range(1, NB + 1):
                step(k, k, 0, None if k <= 2 else 16 * ((k - 1) // 2))
            with act.Fori(1, LAST) as i:
                for k in range(1, NB + 1):
                    step(NB * i + k, k, i, 16 * (NB // 2) * i + 16 * ((k - 1) // 2))
            for k in range(1, NB):
                step(NB * LAST + k, k, LAST, 16 * ((NB * LAST + k - 1) // 2))
            y_step(E - 1, NB - 1, 16 * ((E - 1) // 2))

            act.wait_ge(s_over, 1)
            n_max = act.value_load(over[0:1, 0:1], min_val=0, max_val=T)
            with act.If(n_max > CAP):
                act.wait_ge(m_s[0], 16 * (E // 2))
                with act.Fori(0, E * (ROUNDS - 1)) as i:
                    act.wait_ge(f_sem["xt"], i + 1)
                    xc(0).then_inc(f_sem["xc"], 1)
                    act.wait_ge(f_sem["h"], i + 1)
                    sl(0).then_inc(f_sem["sl"], 1)
                    act.wait_ge(f_sem["y"], i + 1)
                    yh(0, 0).then_inc(f_sem["ya"], 1)

            for n, t in enumerate(LAST_ORDER):
                w = width(t)
                act.wait_ge(s_var, n + 1)
                act.activation(small[0:w, 36:37], small[0:w, 35:36], ACT.Sqrt, bias=eps_t[0:w, 0:1]).then_inc(s_sd, 1)
                dst = o_yp[0, t * P:(t + 1) * P, :] if t < 4 else o_ys[:, 0, :]
                act.wait_ge(s_res, n + 1)
                act.dma_start(dst, base[0:w, t, :]).then_inc(s_final, 16)

        @block.vector
        def _(dve):
            count = [0]

            def chain(ins):
                count[0] += 1
                ins.then_inc(s_v, 1)
                return count[0]

            def link(ins):
                dve.wait_ge(s_v, chain(ins))

            for c in range(1, KC, 2):
                wait_full(dve, f"x{c}")
                dve.tensor_copy(xT[:, c, :], bank(f"x{c}")[:, 0:T]).then_inc(s_emV, 1)
            wait_full(dve, "par")
            link(dve.tensor_copy(par[:, :], bank("par")[:, 0:NPAR]))
            dve.tensor_copy(wcb[:, :], bank("par")[:, 512:512 + WB * RC]).then_inc(s_emV, 1)
            wait_full(dve, "st")
            link(dve.tensor_copy(h0t[:, :, :], bank("st")[:, 0:32].rearrange("p (c b) -> p c b", c=RC)))
            dve.tensor_copy(caT, bank("st")[:, 32:128].rearrange("p (c b) -> p c b", c=RC)).then_inc(s_emV, 1)
            wait_full(dve, "cb")
            chain(dve.tensor_copy(cbT[:, 0:2, :], bank("cb")[:, 0:480].rearrange("p (c b) -> p c b", c=2)))
            dve.tensor_copy(cbT[:, 2:4, :], bank("cb")[:, 512:992].rearrange("p (c b) -> p c b", c=2)).then_inc(s_emV, 1)
            lam = par[:, PAR_AT["rg_lambda"]:PAR_AT["rg_lambda"] + RC]
            dve.wait_ge(s_c8e, 1)
            y, s, s2, acc = c8[:, 1, :], c8[:, 2, :], c8[:, 3, :], c8[:, 4, :]
            link(dve.tensor_scalar(s, y, 2.0, None, ALU.add))
            link(dve.reciprocal(s2, s))
            link(dve.tensor_tensor(s, y, s2, ALU.mult))
            link(dve.tensor_tensor(s2, s, s, ALU.mult))
            terms = 9
            link(dve.tensor_scalar(acc, s2, 1.0 / (2 * terms + 1), 1.0 / (2 * terms - 1), ALU.mult, ALU.add))
            for n in range(terms - 2, -1, -1):
                link(dve.tensor_tensor(acc, acc, s2, ALU.mult))
                link(dve.tensor_scalar(acc, acc, 1.0 / (2 * n + 1), None, ALU.add))
            link(dve.tensor_tensor(acc, acc, s, ALU.mult))
            link(dve.tensor_scalar(c8[:, 5, :], lam, -1.0, 0.0, ALU.mult, ALU.max))
            link(dve.scalar_tensor_tensor(c8[:, 6, :], acc, 2.0, c8[:, 5, :], ALU.mult, ALU.add))
            dve.tensor_scalar(c8[:, 7, :], c8[:, 6, :], -RG_C / 2, None, ALU.mult).then_inc(s_c8, 1)

            def mult_add(out, in0, w, in1):
                return dve.scalar_tensor_tensor(out, in0, w, in1, ALU.mult, ALU.add)

            def conv_sample(x, state, out, taps, wtap, wrow, bias, c):
                link(dve.tensor_scalar(out[:, c, SEQ:T], x[:, c, SEQ:T], wtap(taps - 1), bias, ALU.mult, ALU.add))
                pr = cprod[:, :, 0:taps - 1]
                link(dve.tensor_tensor(pr, state[:, c, :].rearrange("p (b j) -> p b j", b=NS), wrow, ALU.mult))
                link(dve.tensor_reduce(csum, pr, AX.X, ALU.add))
                return dve.tensor_tensor(out[:, c, SEQ:T], out[:, c, SEQ:T], csum, ALU.add)

            def conv_prompt(x, out, taps, wtap, bias, chunks):
                done = {}
                for c in chunks:
                    done[c] = chain(dve.tensor_scalar(out[:, c, 0:SEQ], x[:, c, 0:SEQ], wtap(c, taps - 1), bias(c),
                                                      ALU.mult, ALU.add))
                for s in range(1, taps):
                    for c in chunks:
                        dve.wait_ge(s_v, done[c])
                        done[c] = chain(mult_add(out[:, c, s:SEQ], x[:, c, 0:SEQ - s], wtap(c, taps - 1 - s),
                                                 out[:, c, s:SEQ]))
                dve.wait_ge(s_v, count[0])

            def wa_tap(c, j):
                return col("w_conv_a", j * RC + c)

            def wb_row(c):
                return wcb[:, c:(WB - 1) * RC:RC].unsqueeze(1).broadcast_to([P, NS, WB - 1])

            def wa_row(c):
                a = PAR_AT["w_conv_a"]
                return par[:, a + c:a + (WA - 1) * RC:RC].unsqueeze(1).broadcast_to([P, NS, WA - 1])

            wait_out(dve, "cb")
            for c in range(RC):
                wait_out(dve, f"zs{c}")
                dve.tensor_tensor(gluT[:, c, :], gluT[:, c, :], rT[:, c, :], ALU.mult).then_inc(s_glu, 1)
            dve.wait_ge(s_glu, RC)
            for c in range(RC):
                link(conv_sample(gluT, cbT, cT, WB, lambda j: wb_tap(c, j), wb_row(c), col("b_conv_b", c), c))
            conv_prompt(gluT, cT, WB, wb_tap, lambda c: col("b_conv_b", c), range(0, 2))
            for c in range(RC):
                wait_out(dve, f"zu{c}")
            for c in range(RC):
                link(conv_sample(uT, caT, ucT, WA, lambda j: wa_tap(c, j), wa_row(c), col("b_conv_a", c), c))
            conv_prompt(uT, ucT, WA, wa_tap, lambda c: col("b_conv_a", c), range(RC))
            dve.tensor_copy(csum[:, 0:1], csum[:, 0:1]).then_inc(s_uc, 1)
            conv_prompt(gluT, cT, WB, wb_tap, lambda c: col("b_conv_b", c), range(2, 3))
            dve.tensor_copy(csum[:, 0:1], csum[:, 0:1]).then_inc(s_convb, 1)

            done = {}
            th, a, b, d = ([m[:, c, :] for c in range(RC)] for m in (thT, rT, uT, ucT))
            for c in range(RC):
                wait_out(dve, f"ri{c}")
                done[c] = chain(dve.tensor_tensor(b[c], b[c], d[c], ALU.mult))

            def per_chunk(op):
                for c in range(RC):
                    dve.wait_ge(s_v, done[c])
                    done[c] = chain(op(c))

            for c in range(RC):
                dve.wait_ge(s_v, done[c])
                dve.wait_ge(s_tanh, c + 1)
                done[c] = chain(dve.tensor_scalar(d[c], th[c], -1.0, 1.0, ALU.mult, ALU.add))
            per_chunk(lambda c: dve.reciprocal(d[c], d[c]))
            per_chunk(lambda c: dve.scalar_tensor_tensor(a[c], th[c], 1.0, d[c], ALU.add, ALU.mult))
            per_chunk(lambda c: dve.tensor_tensor(th[c], th[c], d[c], ALU.mult))
            for c in range(RC):
                dve.wait_ge(s_v, done[c])
                dve.scalar_tensor_tensor(th[c], a[c], 1.0, th[c], ALU.add, ALU.mult).then_inc(s_srt, 1)

            def norm_mean(mean, x, n):
                wait_full(dve, mean)
                for k in range(n):
                    ins = dve.tensor_tensor(halves(x[:, k, :]), halves(x[:, k, :]), two(bank(mean)), ALU.subtract)
                    if k < n - 1:
                        ins.then_inc(s_sub, 1)
                    else:
                        ins.then_inc(s_emV, 1)
                        emptied(dve, GID[mean])
                        dve.sem_inc(s_sub, 1)

            def norm_scale(var, x, n):
                wait_out(dve, var)
                link(dve.reciprocal(rstd[:, :], rstd[:, :]))
                for k in range(n):
                    dve.tensor_tensor(x[:, k, :], x[:, k, :], rstd[:, :], ALU.mult).then_inc(s_nrm, 1)

            norm_mean("cmean", cT, RC)
            for c in range(RC):
                dve.wait_ge(s_root, c + 1)
                done[c] = chain(dve.tensor_tensor(b[c], b[c], th[c], ALU.mult))
            h = d
            per_chunk(lambda c: dve.tensor_tensor_scan(h[c][:, 0:SEQ], a[c][:, 0:SEQ], b[c][:, 0:SEQ], 0.0, ALU.mult, ALU.add))
            per_chunk(lambda c: dve.tensor_tensor(h[c][:, SEQ:T], a[c][:, SEQ:T], h0t[:, c, :], ALU.mult))
            for c in range(RC):
                dve.wait_ge(s_v, done[c])
                dve.tensor_tensor(h[c][:, SEQ:T], h[c][:, SEQ:T], b[c][:, SEQ:T], ALU.add).then_inc(s_h, 1)
            for c in range(RC):
                dve.wait_ge(s_h, c + 1)
                wait_out(dve, f"zg{c}")
                dve.tensor_tensor(gT[:, c, :], gT[:, c, :], h[c], ALU.mult).then_inc(s_ya, 1)
            norm_scale("cvar", cT, RC)
            wait_full(dve, "hlast")
            dve.wait_ge(s_tailout, 16 * 4)
            dve.tensor_copy(tail[0:9, 0, :], bank("hlast")[0:9, 0:512]).then_inc(s_emV, 1)

            def residual(name, k):
                wait_full(dve, name)
                dve.scalar_tensor_tensor(halves(xT[:, k, :]), halves(xT[:, k, :]), ALPHA, two(bank(name)),
                                         ALU.mult, ALU.add).then_inc(s_emV, 1)
                wait_out(dve, name)
                if k > 0:
                    first = xT[:, 0, :] if k == 1 else xsum[:, 0, :]
                    ins = dve.tensor_tensor(xsum[:, 0, :], first, xT[:, k, :], ALU.add)
                    if k < KC - 1:
                        link(ins)
                    else:
                        ins.then_inc(s_xsum, 1)

            for k in range(KC):
                residual(f"wo{k}", k)
            norm_mean("mean1", xT, KC)
            norm_scale("var1", xT, KC)

            def softmax_max(t):
                o = 8 * (t % 2)
                wait_full(dve, f"sc{t}")
                link(dve.tensor_reduce(small[:, o:o + 4], bank(f"sc{t}").rearrange("p (h m) -> p h m", h=XH), AX.X, ALU.max))
                dve.tensor_scalar(small[:, o + 4:o + 8], small[:, o:o + 4], -XD ** -0.5, None, ALU.mult).then_inc(s_smax, 1)

            def softmax_scale(t):
                so = 16 + 4 * (t % 2)
                wait_out(dve, f"sc{t}")
                dve.wait_ge(s_ssum, (XH - 1) * (t + 1))
                if t > 0:
                    dve.wait_ge(s_v, count[0])
                    dve.wait_ge(s_prob, t)
                link(dve.reciprocal(small[:, 27:31], small[:, so:so + 4]))
                for h in range(XH):
                    pr = probs[:, t % 2, h, :]
                    ins = dve.tensor_scalar(pr, pr, small[:, 27 + h:28 + h], None, ALU.mult)
                    if h < XH - 1:
                        chain(ins)
                ins.then_inc(s_prob, 1)

            def sample_scores(b):
                if b % 4 == 0:
                    dve.wait_ge(s_load[6 + b // 4], 16 * 4)
                if b % 2 == 0:
                    dve.wait_ge(s_qall[b // 2], 16 * 2)
                kc = cache(1 + b // 4, b % 4)
                for m in range(2):
                    for h in range(XH):
                        ins = dve.tensor_tensor_reduce(junk, kc[:, m, XD * h:XD * h + XD], q_all[:, b, XD * h:XD * h + XD],
                                                       1.0, 0.0, ALU.mult, ALU.add, ss[:, m, 4 * b + h:4 * b + h + 1])
                        if (m, h) != (1, XH - 1):
                            link(ins)
                ins.then_inc(s_ss, 1)
                dve.wait_ge(s_ss, b + 1)

            softmax_max(0)
            softmax_max(1)
            softmax_scale(0)
            softmax_max(2)
            softmax_scale(1)
            sample_scores(0)
            softmax_max(3)
            softmax_scale(2)
            sample_scores(1)
            softmax_scale(3)
            for b in range(2, NS):
                sample_scores(b)
            wait_full(dve, "ssT")
            link(dve.tensor_reduce(small[0:32, 24:25], bank("ssT")[0:32, 0:N_MEM], AX.X, ALU.max))
            dve.tensor_scalar(small[0:32, 25:26], small[0:32, 24:25], -XD ** -0.5, None, ALU.mult).then_inc(s_smax, 1)
            wait_out(dve, "ssT")
            link(dve.reciprocal(small[0:32, 31:32], small[0:32, 26:27]))
            dve.tensor_scalar(sp, sp, small[0:32, 31:32], None, ALU.mult).then_inc(s_prob, 1)
            wait_full(dve, "osb")
            wait_out(dve, "osa")
            dve.tensor_tensor(o_s, o_s, bank("osb")[0:NS, :], ALU.add).then_inc(s_emV, 1)
            for k in range(KC):
                residual(f"xo{k}", k)
            norm_mean("mean2", xT, KC)
            norm_scale("var2", xT, KC)

            dve.memset(R[0], 0.0).then_inc(s_rz, 1)
            dve.memset(place, -1.0).then_inc(s_late2, 1)
            dve.wait_ge(s_late2, 1)
            dve.wait_ge(s_rt, 16)
            dve.wait_ge(s_late, 9)
            wait_out(dve, "rt")
            dve.wait_ge(s_ssum, (XH - 1) * 4 + 1)
            score, biased, sel, tmp, left = R[0], R[1], R[2], R[3], R[4]
            link(dve.tensor_tensor(biased, score, rbias.unsqueeze(1).broadcast_to([P, TT, E]), ALU.add))
            for t in range(TT):
                for g in range(8):
                    n = chain(dve.max(rmax[:, t, g, :], biased[:, t, 8 * g:8 * g + 8]))
            dve.wait_ge(s_v, n)
            link(dve.tensor_tensor(gscore, rmax[:, :, :, 0], rmax[:, :, :, 1], ALU.add))
            mine = gscore.unsqueeze(3).broadcast_to([P, TT, 8, 8])
            other = gscore.unsqueeze(2).broadcast_to([P, TT, 8, 8])
            link(dve.tensor_tensor(pair, other, mine, ALU.is_equal))
            link(dve.tensor_tensor(pair, pair, tri8.unsqueeze(1).broadcast_to([P, TT, 8, 8]), ALU.mult))
            link(dve.tensor_tensor(pair2, other, mine, ALU.is_gt))
            link(dve.tensor_tensor(pair, pair, pair2, ALU.add))
            link(dve.tensor_reduce(grank, pair, AX.X, ALU.add))
            link(dve.tensor_scalar(grank, grank, 4.0, None, ALU.is_lt))
            gm = grank.unsqueeze(3).broadcast_to([P, TT, 8, 8])
            b4 = biased.rearrange("p t (g j) -> p t g j", g=8)
            t4 = tmp.rearrange("p t (g j) -> p t g j", g=8)
            link(dve.tensor_tensor(t4, b4, gm, ALU.mult))
            link(dve.tensor_scalar(grank, grank, 1.0, 1e30, ALU.subtract, ALU.mult))
            link(dve.tensor_tensor(t4, t4, gm, ALU.add))
            for t in range(TT):
                n = chain(dve.max(top8[:, t, :], tmp[:, t, :]))
            dve.wait_ge(s_v, n)
            for t in range(TT):
                n = chain(dve.match_replace(left[:, t, :], top8[:, t, :], tmp[:, t, :], -2e30))
            dve.wait_ge(s_v, n)
            link(dve.tensor_scalar(sel, left, -2e30, None, ALU.is_equal))
            dve.tensor_tensor(sel, sel, rmask.unsqueeze(2).broadcast_to([P, TT, E]), ALU.mult).then_inc(s_sel, 1)
            dve.wait_ge(s_sel, 1)
            link(dve.tensor_tensor(tmp, score, sel, ALU.mult))
            link(dve.tensor_reduce(gsum, tmp, AX.X, ALU.add))
            link(dve.tensor_scalar(gsum, gsum, 1e-30, None, ALU.max))
            link(dve.reciprocal(gsum, gsum))
            link(dve.tensor_scalar(gsum, gsum, ROUTED_SCALE, None, ALU.mult))
            link(dve.tensor_tensor(tmp, tmp, gsum.unsqueeze(2).broadcast_to([P, TT, E]), ALU.mult))
            link(dve.tensor_copy(table[:, :, :, 3], tmp))
            link(dve.tensor_tensor(tmp, tmp, table[:, :, :, 3], ALU.subtract))
            link(dve.tensor_copy(table[:, :, :, 4], tmp))
            link(dve.tensor_tensor(table[:, :, :, 5], tmp, table[:, :, :, 4], ALU.subtract))
            link(dve.tensor_copy(table[:, :, :, 0], row8.unsqueeze(2).broadcast_to([P, TT, E])))
            link(dve.tensor_copy(table[:, :, :, 1], tile8.unsqueeze(2).broadcast_to([P, TT, E])))
            link(dve.memset(wsum, 1.0))
            for t in range(TT):
                n = chain(dve.tensor_tensor_scan(left[:, t, :], wsum, sel[:, t, :], 0.0, ALU.mult, ALU.add))
            dve.wait_ge(s_v, n)
            link(dve.tensor_scalar(table[:, :, :, 2], left, 1.0, None, ALU.subtract))

            def gated(name, j):
                wait_full(dve, name)
                wait_out(dve, "h1" + name[2])
                dve.tensor_tensor(halves(shT[:, j, :]), halves(sh1[:, j, :]), two(bank(name)), ALU.mult).then_inc(s_emV, 1)

            gated("h3a", 0)
            gated("h3b", 1)
            wait_full(dve, "rank")
            link(dve.scalar_tensor_tensor(place[:, :, 0:E], bank("rank")[:, 0:TT * E].rearrange("p (t e) -> p t e", t=TT),
                                          1.0, sel, ALU.add, ALU.mult))
            dve.tensor_scalar(place[:, :, 0:E], place[:, :, 0:E], 1.0, None, ALU.subtract).then_inc(s_emV, 1)
            wait_full(dve, "count")
            dve.tensor_reduce(cmax, bank("count")[:, 0:E], AX.X, ALU.max).then_inc(s_emV, 1)
            wait_out(dve, "count")
            dve.tensor_copy(over[:, :], cmax).then_inc(s_over, 1)
            wait_out(dve, "rank")
            dve.sem_inc(s_table, 1)

            def shared_sum(t):
                w = width(t)
                wait_full(dve, f"so{t}")
                wait_out(dve, f"x2{t}")
                dve.wait_ge(s_x2out, 16 * TT)
                dve.scalar_tensor_tensor(base[0:w, t, :], base[0:w, t, :], ALPHA, bank(f"so{t}")[0:w, :],
                                         ALU.mult, ALU.add).then_inc(s_emV, 1)

            def oh(n, e, numbers):
                return dve.tensor_tensor(onehot[:, n % 2, :, :], place[:, :, bass.ds(e, 1)].broadcast_to([P, TT, CAP]),
                                         numbers.unsqueeze(1).broadcast_to([P, TT, CAP]), ALU.is_equal)

            def indices(n, s, base_count):
                at = 512 * (n % 2)
                dve.tensor_reduce(picked[0:CAP, n, :], psum[0:CAP, 3, at:at + 6].rearrange("p (v c) -> p v c", v=2), AX.X,
                                  ALU.add).then_inc(s, 1)
                dve.wait_ge(s, base_count + 1)
                dve.tensor_scalar(idx_y[0:CAP, n:n + 1], picked[0:CAP, n, 0:1], FAR, None, ALU.add).then_inc(s, 1)
                dve.wait_ge(s, base_count + 2)
                return dve.tensor_scalar(idx_x[0:CAP, n:n + 1], idx_y[0:CAP, n:n + 1], 3, None, ALU.logical_shift_right)

            def hd(b):
                return dve.tensor_tensor(hidT[:, b, :], silu[:, b, :], psum[:, 2, 512 * b + 2 * CAP:512 * b + 4 * CAP], ALU.mult)

            def yh(b, n):
                return dve.tensor_scalar(ys[0:CAP, b, 512:1024], psum[0:CAP, 0, 512:1024], picked[0:CAP, n, 1:2], None, ALU.mult)

            def oh_step(e, n):
                if at_least(e, 2):
                    dve.wait_ge(m_ip, e - 1)
                oh(n, e, slots).then_inc(m_oh, 1)

            def i_step(e, n, sc):
                dve.wait_ge(m_ip, e + 1)
                if sc is not None:
                    dve.wait_ge(m_s[n % 2], sc)
                indices(n, m_iv, 2 * e).then_inc(m_idx, 1)

            def c_step(e, n):
                dve.wait_ge(m_sl, e + 1)
                if at_least(e, 2):
                    dve.wait_ge(m_y, e - 1)
                hd(n % 2).then_inc(m_hd, 1)

            def y_step(e, n, sc):
                dve.wait_ge(m_y, e + 1)
                if sc is not None:
                    dve.wait_ge(m_s[n % 2], sc)
                yh(n % 2, n).then_inc(m_yv, 1)

            oh_step(0, 0)
            oh_step(1, 1)
            i_step(0, 0, None)
            oh_step(2, 2)
            i_step(1, 1, None)
            oh_step(3, 3)
            shared_sum(0)
            shared_sum(1)
            i_step(2, 2, None)
            oh_step(4, 4)
            shared_sum(2)
            i_step(3, 3, None)
            oh_step(5, 5)
            shared_sum(3)
            shared_sum(4)
            c_step(0, 0)

            def step(e, k, i, sc, si):
                c_step(e, k % NB)
                y_step(e - 1, (k - 1) % NB, sc)
                if exists(e + 3):
                    i_step(e + 3, (k + 3) % NB, si)
                if exists(e + 5):
                    oh_step(e + 5, (k + 5) % NB)

            LAST = E // NB - 1
            for k in range(1, NB + 1):
                step(k, k, 0, None if k <= 2 else 16 * ((k - 1) // 2), None if k < 5 else 16 * ((k - 5) // 2 + 1))
            with dve.Fori(1, LAST) as i:
                for k in range(1, NB + 1):
                    step(NB * i + k, k, i, 16 * (NB // 2) * i + 16 * ((k - 1) // 2),
                         16 * (NB // 2) * i + 16 * ((k - 5) // 2 + 1))
            for k in range(1, NB):
                e = NB * LAST + k
                step(e, k, LAST, 16 * ((e - 1) // 2), 16 * ((e - 5) // 2 + 1))
            y_step(E - 1, NB - 1, 16 * ((E - 1) // 2))

            dve.wait_ge(s_over, 1)
            n_max = dve.value_load(over[0:1, 0:1], min_val=0, max_val=T)
            with dve.If(n_max > CAP):
                dve.wait_ge(m_s[0], 16 * (E // 2))
                dve.wait_ge(m_s[1], 16 * (E // 2))
                dve.wait_ge(m_g[0], 16 * (E // 4))
                dve.wait_ge(m_ip, E)
                dve.wait_ge(s_late, 10)
                with dve.Fori(1, E * (ROUNDS - 1) + 1) as turn_i:
                    dve.wait_ge(f_sem["it"], turn_i)
                    i = turn_i - 1
                    link_r = dve.tensor_scalar(slots_r, slots, rounds_t[:, bass.ds(i // E, 1)], None, ALU.add)
                    link_r.then_inc(f_sem["iv"], 1)
                    dve.wait_ge(f_sem["iv"], 3 * i + 1)
                    oh(0, i % E, slots_r).then_inc(f_sem["oh"], 1)
                    dve.wait_ge(f_sem["ip"], i + 1)
                    indices(0, f_sem["iv"], 3 * i + 1).then_inc(f_sem["idx"], 1)
                    dve.wait_ge(f_sem["sl"], i + 1)
                    hd(0).then_inc(f_sem["hd"], 1)
                    dve.wait_ge(f_sem["y"], i + 1)
                    yh(0, 0).then_inc(f_sem["yv"], 1)

            dve.wait_ge(s_lnw, 32)
            for m, t in enumerate(LAST_ORDER):
                w = width(t)
                x = base[0:w, t, :]
                for q in range(2):
                    if q == 0:
                        dve.wait_ge(s_ypool, m + 1)
                    else:
                        dve.wait_ge(s_yin[q][m % 3], 16 * (m // 3 + 1))
                    rows_here = (DVE_ROWS if w == P else SMALL_ROWS)[q]
                    for j in rows_here:
                        ins = dve.tensor_tensor(x, x, y_in[m % 3][0:w, j, :], ALU.add)
                        if w == P or j != SMALL_ROWS[1][-1]:
                            link(ins)
                if w == P:
                    dve.wait_ge(s_ysum, m)
                    ins = dve.tensor_tensor(x, x, psum[0:w, m % 4, :], ALU.add)
                ins.then_inc(s_rowv, 1)
                dve.wait_ge(s_rowv, m + 1)
                for n in range(2):
                    link(dve.bn_stats(st6[0:w, n, :], base[0:w, t, 512 * n:512 * n + 512]))
                dve.bn_aggr(small[0:w, 34:36], st6[0:w, :, :]).then_inc(s_var, 1)
                dve.wait_ge(s_var, m + 1)
                dve.wait_ge(s_sd, m + 1)
                link(dve.reciprocal(small[0:w, 37:38], small[0:w, 36:37]))
                link(dve.scalar_tensor_tensor(x, x, small[0:w, 34:35], ln3g[0:w, :], ALU.subtract, ALU.mult))
                dve.scalar_tensor_tensor(x, x, small[0:w, 37:38], ln3b[0:w, :], ALU.mult, ALU.add).then_inc(s_res, 1)


_INS = ['x_prompt', 'x_sample', 'mem_prompt', 'state_rglru_h', 'state_rglru_conv', 'state_dwconv', 'cache_mem_k',
        'cache_mem_v', 'w_in', 'b_in', 'w_conv_a', 'b_conv_a', 'w_rg_a', 'b_rg_a', 'w_rg_x', 'b_rg_x', 'rg_lambda',
        'w_conv_b', 'b_conv_b', 'ln_c_g', 'ln_c_b', 'w_out', 'ln1_g', 'ln1_b', 'w_q', 'w_k', 'w_v', 'w_o', 'ln2_g',
        'ln2_b', 'w_router', 'router_bias', 'w1_e', 'w3_e', 'w2_e', 'w1_s', 'w3_s', 'w2_s', 'ln3_g', 'ln3_b']
_OUTS = [(1, 512, 1024), (8, 1, 1024), (1, 1, 512), (1, 1, 3, 512), (1, 1, 30, 512), (1, 1, 256, 4, 256),
         (1, 1, 256, 4, 256), (1, 8, 512), (1, 8, 3, 512), (1, 8, 30, 512)]


def kernel(**inputs):
    import numpy as _np
    import concourse.bacc as _bacc
    from concourse import mybir as _mybir
    from concourse.bass_utils import run_bass_kernel_spmd as _run

    nc = _bacc.Bacc("TRN2", target_bir_lowering=False, num_devices=1)
    arrays, ins = {}, {}
    for name in _INS:
        a = _np.ascontiguousarray(inputs[name])
        arrays[f"in_{name}_dram"] = a
        ins[name] = nc.dram_tensor(f"in_{name}_dram", a.shape, _mybir.dt.from_np(a.dtype), kind="ExternalInput").ap()
    outs = [nc.dram_tensor(f"out_{i}_dram", shape, _mybir.dt.float32, kind="ExternalOutput").ap()
            for i, shape in enumerate(_OUTS)]
    decoder_step(nc, ins, outs)
    r = _run(nc, [arrays], core_ids=[0])
    return tuple(r.results[0][f"out_{i}_dram"] for i in range(len(_OUTS)))
```

```python
from contextlib import ExitStack
import math

import concourse.bass as bass
from concourse import mybir

ALU = mybir.AluOpType
ACT = mybir.ActivationFunctionType
AX = mybir.AxisListType
F32 = mybir.dt.float32
I32 = mybir.dt.int32
U32 = mybir.dt.uint32
BF16 = mybir.dt.bfloat16

P = 128
D = 1024
KC = D // P
SEQ, NS = 512, 8
T = SEQ + NS
HALF = T // 2
RC = 4
TT = 5
N_MEM, XH, XD = 256, 4, 256
E, FE, TOPK = 64, 256, 8
WA, WB = 4, 31
ALPHA = 2.0 ** 0.25
EPS = 1e-5
RG_C = 8.0
ROUTED_SCALE = 2.5
CAP = 112
NROW = T * TOPK
FAR = 8192.0
ROUNDS = (T + CAP - 1) // CAP
NB = 8

PAR_SPEC = [("b_in", 16), ("w_conv_a", 16), ("b_conv_a", 4), ("b_rg_a", 4), ("b_rg_x", 4), ("rg_lambda", 4),
            ("b_conv_b", 4), ("ln_c_g", 4), ("ln_c_b", 4), ("ln1_g", 8), ("ln1_b", 8), ("ln2_g", 8), ("ln2_b", 8)]
PAR_AT = {}
_row = 0
for _n, _k in PAR_SPEC:
    PAR_AT[_n] = _row
    _row += _k
NPAR = _row

GROUPS = [(f"x{c}", "AV"[c % 2]) for c in range(KC)] + [("par", "V")]
GROUPS += [(f"zv{c}", "A") for c in range(RC)] + [("st", "V"), ("cb", "V")] + [(f"zs{c}", "A") for c in range(RC)]
GROUPS += [(f"zu{c}", "A") for c in range(RC)] + [(f"zg{c}", "A") for c in range(RC)]
GROUPS += [("mt0", "A"), ("mt1", "A"), ("v0", "A"), ("tails", "A")]
GROUPS += [(f"ra{c}", "A") for c in range(RC)] + [(f"ri{c}", "A") for c in range(RC)]
GROUPS += [("k0", "A"), ("cmean", "V"), ("k1", "A"), ("cvar", "A"), ("kt0", "A"), ("kt1", "A"), ("hlast", "V")]
GROUPS += [(f"wo{c}", "V") for c in range(KC)] + [("mean1", "V"), ("v1a", "A"), ("var1", "A"), ("v1b", "A")]
GROUPS += [(f"q{c}", "A") for c in range(KC)] + [("qs", "A")]
ATTENTION = ["sc0", "sc1", "sc2", "pt0", "sc3", "pt1", "pt2", "pt3", "o0", "o1", "o2", "o3", "o4", "o5", "o6", "o7",
             "xa0", "xa1", "ssT", "xa2", "spT", "xa3"]
GROUPS += [(name, "V" if name[0] == "x" else "A") for name in ATTENTION]
GROUPS += [(f"xa{c}", "V") for c in range(4, KC)]
GROUPS += [("mean2a", "V"), ("var2a", "A"), ("os", "A"), ("osT", "A")]
GROUPS += [(f"xb{c}", "V") for c in range(KC)]
GROUPS += [("h1a0", "A"), ("mean2b", "V"), ("h3a0", "V"), ("var2b", "A"), ("h1b0", "A"), ("rt0", "A"),
           ("rt1", "A"), ("x20", "A"), ("rtT", "A")]
GROUPS += [(f"x2{t}", "A") for t in range(1, TT)]
GROUPS += [("h3b0", "V"), ("h1a1", "A"), ("h3a1", "V"), ("h1b1", "A"), ("h3b1", "V"), ("rank", "V"), ("count", "V")]
GROUPS += [(f"so{t}", "V") for t in range(TT)]
GID = {name: g for g, (name, _) in enumerate(GROUPS)}
LAST_ORDER = [4, 0, 1, 2, 3]
PARTS = [(0, 3), (3, 5), (5, 7), (7, 8)]
POOL_ROWS = (1, 4)
PE_ROWS = [(2,), (3,), (5,), ()]
DVE_ROWS = [(0,), (), (6,), (7,)]
SMALL_ROWS = [(0, 2), (3,), (5, 6), (7,)]
PAIR = {f"so{t}": (t + 2) % 3 for t in range(TT)}

POOL_CHUNKS = (3,)

A0, A1, A2, A3, A4 = 0, 4160, 8320, 12480, 16640
A_SIZE = A4 + 2080


def at_least(e, n):
    return not isinstance(e, int) or e >= n


def exists(e):
    return not isinstance(e, int) or e < E


def width(t):
    return P if t < TT - 1 else NS


def decoder_step(nc: bass.Bass, ins, outs):
    I = ins
    (o_yp, o_ys, o_hp, o_cap, o_cbp, o_mk, o_mv, o_hs, o_cas, o_cbs) = outs

    with ExitStack() as ctx:
        def sb(name, shape, dt=F32):
            return ctx.enter_context(nc.sbuf_tensor(name, shape, dt))

        def sem(name):
            return ctx.enter_context(nc.semaphore(name))

        x2_rows = nc.dram_tensor("x2_rows", [T, D], F32)
        q_rows = nc.dram_tensor("q_rows", [NS, D], F32)
        y_rows = nc.dram_tensor("y_rows", [NROW, D], F32)

        arena = sb("arena", [P, 3 * 8192])
        act_mem = sb("act_mem", [P, A_SIZE])
        kv_mem = sb("kv_mem", [P, 4096])
        mk_mem = sb("mk_mem", [P, 2048])
        ident = sb("ident", [P, P])
        mean_d = sb("mean_d", [P, P])
        mean_c = sb("mean_c", [P, P])
        ones = sb("ones", [P, P], BF16)
        par = sb("par", [P, NPAR])
        wcb = sb("wcb", [P, WB * RC])
        gate_w = sb("gate_w", [P, 2, RC, P])
        rstd = sb("rstd", [P, T])
        tail = sb("tail", [38, 2, 512])
        h0t = sb("h0t", [P, RC, NS])
        c8 = sb("c8", [P, 8, RC])
        eps_t = sb("eps_t", [P, 1])
        small = sb("small", [P, 44])
        psum = ctx.enter_context(nc.psum_tensor("psum", [P, 4, D], F32))

        def rows(at, k):
            return act_mem[:, at:at + k * T].rearrange("p (k t) -> p k t", k=k)

        def halves(ap):
            return ap.rearrange("p (h t) -> p h t", h=2)

        def col(name, c):
            return par[:, PAR_AT[name] + c:PAR_AT[name] + c + 1]

        xT = rows(A0, KC)
        gT, uT = rows(A1, RC), rows(A1 + RC * T, RC)
        gluT, rT = rows(A2, RC), rows(A2 + RC * T, RC)
        cT, ucT = rows(A3, RC), rows(A3 + RC * T, RC)
        thT = rows(A4, RC)
        x_tok = act_mem[:, A3:A3 + TT * D].rearrange("p (t n) -> p t n", t=TT)
        raw_par = act_mem[0:P, A1:A1 + P]
        raw_wcb = act_mem[0:P, A1 + P:A1 + 2 * P]
        cbT = act_mem[:, A4 + 960:A4 + 1920].rearrange("p (c n) -> p c n", c=RC)
        caT = act_mem[:, A4 + 1920:A4 + 1920 + 96].rearrange("p (c n) -> p c n", c=RC)
        cprod = act_mem[:, A4:A4 + 240].rearrange("p (b j) -> p b j", b=NS)
        tap_mem = kv_mem[:, 2048:4096].rearrange("p (b n) -> p b n", b=4)
        csum = act_mem[:, A4 + 240:A4 + 248]
        sq = rows(A1, KC)
        sq_c = rows(A2, RC)
        st_cb = mk_mem[0:120, 0:1024].rearrange("p (r n) -> p r n", r=2)
        st_ca = mk_mem[0:24, 1024:1536]
        st_h = mk_mem[0:NS, 1536:2048]
        mem_tok = mk_mem[:, :].rearrange("p (m n) -> p m n", m=2)
        memT = kv_mem[:, 0:2048].rearrange("p (k m) -> p k m", k=KC)
        keyT = memT
        memT_late = act_mem[:, A2 + RC * T:A2 + RC * T + KC * P].rearrange("p (k m) -> p k m", k=KC)
        v_tok = kv_mem[:, 2048:4096].rearrange("p (m n) -> p m n", m=2)
        k_tok = mem_tok
        qT = rows(A2, KC)
        prT = rows(A1, KC)
        oT = rows(A3, KC)
        probs = act_mem[:, A4:A4 + 2048].rearrange("p (b h m) -> p b h m", b=2, h=XH)
        q_s = mk_mem[0:NS, 0:1024]
        junk = mk_mem[:, 1024:1280]
        ss = mk_mem[:, 1280:1344].rearrange("p (m n) -> p m n", m=2)
        sp = mk_mem[0:32, 1344:1600]
        sample_p = mk_mem[:, 1600:1664].rearrange("p (m n) -> p m n", m=2)
        unit = act_mem[:, A4 + 1024:A4 + 1024 + NS * NS]
        o_s = q_s
        xsum = act_mem[:, A4:A4 + T].rearrange("p (k t) -> p k t", k=1)
        base = act_mem[:, A1:A1 + TT * D].rearrange("p (t n) -> p t n", t=TT)
        ys = act_mem[:, 9280:9280 + 2048].rearrange("p (b n) -> p b n", b=2)
        silu = act_mem[:, 11328:11328 + 4 * CAP].rearrange("p (b n) -> p b n", b=2)
        sh1 = rows(A3, 2)
        shT = rows(A3 + 2 * T, 2)
        onehot = act_mem[:, 14560:14560 + TT * CAP].bitcast(BF16).rearrange("p (b t s) -> p b t s", b=2, t=TT)
        hidT = act_mem[:, 15840:15840 + 4 * CAP].rearrange("p (b n) -> p b n", b=2)
        xg = [act_mem[:, 0:D], act_mem[:, D:2 * D], mk_mem[:, 0:D], mk_mem[:, D:2 * D]]
        xgT = act_mem[:, 2048:2048 + 2 * KC * CAP].rearrange("p (b k s) -> p b k s", b=2, k=KC)
        place = act_mem[:, A4:A4 + TT * E].rearrange("p (t e) -> p t e", t=TT)
        table = act_mem[:, A4 + 320:A4 + 320 + 3 * TT * E].bitcast(BF16).rearrange("p (t e c) -> p t e c", t=TT, e=E)
        picked = act_mem[:, A4 + 1280:A4 + 1280 + 2 * NB].rearrange("p (n c) -> p n c", c=2)
        idx_y = sb("idx_y", [P, NB], U32)
        idx_x = sb("idx_x", [P, NB], U32)
        over = sb("over", [P, 1], I32)
        ln3g, ln3b = kv_mem[:, 0:1024], kv_mem[:, 1024:2048]
        R = [kv_mem[:, 2048 + 320 * n:2368 + 320 * n].rearrange("p (t e) -> p t e", t=TT) for n in range(6)]
        score_t = kv_mem[0:E, 0:T]
        rbias = mk_mem[:, 0:64]
        rmax = mk_mem[:, 64:64 + 320].rearrange("p (t g j) -> p t g j", t=TT, g=8)
        gscore = mk_mem[:, 384:424].rearrange("p (t g) -> p t g", t=TT)
        grank = mk_mem[:, 424:464].rearrange("p (t g) -> p t g", t=TT)
        top8 = mk_mem[:, 464:504].rearrange("p (t g) -> p t g", t=TT)
        gsum = mk_mem[:, 504:509]
        row8 = mk_mem[:, 509:514]
        rmask = mk_mem[:, 514:519]
        tile8 = mk_mem[:, 1290:1295]
        wsum = mk_mem[:, 520:584]
        tri8 = mk_mem[:, 584:648].rearrange("p (g j) -> p g j", g=8)
        pair = mk_mem[:, 648:968].rearrange("p (t g j) -> p t g j", t=TT, g=8)
        pair2 = mk_mem[:, 968:1288].rearrange("p (t g j) -> p t g j", t=TT, g=8)
        cmax = mk_mem[:, 1288:1289]
        tri = gate_w[:, 0, 0, 0:64].bitcast(BF16)
        sel_b = kv_mem[:, 520:680].bitcast(BF16).rearrange("p (t e) -> p t e", t=TT)
        slots = gate_w[:, 0, 1, 0:CAP]
        slots_r = gate_w[:, 0, 2, 0:CAP]
        wr = gate_w[:, 1, :, :].rearrange("p c n -> p (c n)").rearrange("p (k e) -> p k e", k=KC)
        rounds_t = small[:, 38:38 + ROUNDS - 1]
        st6 = sb("st6", [P, 2, 6])
        y_in = [arena[:, 8192 * n:8192 * n + 8192].rearrange("p (j n) -> p j n", j=TOPK) for n in range(3)]

        def wb_tap(c, j):
            return wcb[:, j * RC + c:j * RC + c + 1]

        def value_cache(b):
            return cache(0, b) if b < 4 else cache(2, b - 4)

        def wslot(n):
            return arena[:, 8192 * n:8192 * n + 8192].rearrange("p (k n) -> p k n", k=KC)

        def cache(n, b):
            return arena[:, 8192 * n + 2048 * b:8192 * n + 2048 * b + 2048].rearrange("p (m n) -> p m n", m=2)

        def ew(n):
            at = 6144 * n
            return (arena[:, at:at + 4096].rearrange("p (w k n) -> p w k n", w=2, k=KC),
                    arena[:, at + 4096:at + 6144].rearrange("p (k n) -> p k n", k=2))

        q_all = arena[:, 0:NS * D].rearrange("p (b n) -> p b n", b=NS)
        w1s = arena[:, 16384:18432].rearrange("p (k n) -> p k n", k=KC)
        w3s = arena[:, 18432:20480].rearrange("p (k n) -> p k n", k=KC)
        w2s = arena[:, 20480:22528].rearrange("p (k n) -> p k n", k=2)

        s_full = sem("s_full")
        s_emA = sem("s_emA")
        s_emV = sem("s_emV")
        s_par = sem("s_par")
        s_par2 = sem("s_par2")
        s_wcbl = sem("s_wcbl")
        s_state = sem("s_state")
        s_x = sem("s_x")
        s_gw = sem("s_gw")
        s_mem = sem("s_mem")
        s_load = [sem(f"s_load{n}") for n in range(9)]
        s_win = [sem(f"s_win{n}") for n in range(4)]
        s_wo = [sem(f"s_wo{n}") for n in range(4)]
        s_out = sem("s_out")
        s_tailout = sem("s_tailout")
        s_stateout = sem("s_stateout")
        s_kout = sem("s_kout")
        s_const = sem("s_const")
        s_gwz = sem("s_gwz")
        s_late = sem("s_late")
        s_v = sem("s_v")
        s_glu = sem("s_glu")
        s_uc = sem("s_uc")
        s_convb = sem("s_convb")
        s_convp = sem("s_convp")
        s_memc = sem("s_memc")
        s_tap = sem("s_tap")
        s_c8 = sem("s_c8")
        s_tanh = sem("s_tanh")
        s_srt = sem("s_srt")
        s_root = sem("s_root")
        s_h = sem("s_h")
        s_ya = sem("s_ya")
        s_sub = sem("s_sub")
        s_sq = sem("s_sq")
        s_nrm = sem("s_nrm")
        s_ln = sem("s_ln")
        s_smax = sem("s_smax")
        s_prob = sem("s_prob")
        s_ssum = sem("s_ssum")
        s_x2out = sem("s_x2out")
        s_rt = sem("s_rt")
        s_wr = sem("s_wr")
        s_c8e = sem("s_c8e")
        s_late2 = sem("s_late2")
        s_rz = sem("s_rz")
        s_qrow = sem("s_qrow")
        s_qall = [sem(f"s_qall{n}") for n in range(4)]
        s_ss = sem("s_ss")
        s_val = [sem(f"s_val{n}") for n in range(NS // 2)]
        s_pv0 = sem("s_pv0")
        s_pv = sem("s_pv")
        s_unit = sem("s_unit")
        s_xsum = sem("s_xsum")
        s_done = sem("s_done")
        s_lnw = sem("s_lnw")
        s_sel = sem("s_sel")
        s_table = sem("s_table")
        s_over = sem("s_over")
        s_rowv = sem("s_rowv")
        s_abs = sem("s_abs")

        s_w = [sem(f"s_w{n}") for n in range(4)]
        m_oh = sem("m_oh")
        m_ip = sem("m_ip")
        m_idx = sem("m_idx")
        m_iv = sem("m_iv")
        m_g = [sem(f"m_g{n}") for n in range(4)]
        m_xt = sem("m_xt")
        m_xc = sem("m_xc")
        m_h = sem("m_h")
        m_sl = sem("m_sl")
        m_hd = sem("m_hd")
        m_y = sem("m_y")
        m_ya = sem("m_ya")
        m_yv = sem("m_yv")
        m_s = [sem(f"m_s{n}") for n in range(2)]
        m_z = sem("m_z")
        m_go = sem("m_go")
        f_sem = {n: sem("f_" + n) for n in ("w", "oh", "ip", "iv", "idx", "g", "xt", "xc", "h", "sl", "hd", "y", "ya",
                                            "yv", "s", "it")}
        s_yin = [[sem(f"s_yin{q}{n}") for n in range(3)] for q in range(len(PARTS))]
        s_ypool = sem("s_ypool")
        s_ysum = sem("s_ysum")
        s_final = sem("s_final")
        s_fin = sem("s_fin")
        s_sd = sem("s_sd")
        s_var = sem("s_var")
        s_res = sem("s_res")

        def emptied(eng, g):
            who = GROUPS[g][1]
            n = sum(1 for _, w in GROUPS[:g + 1] if w == who)
            eng.wait_ge(s_emA if who == "A" else s_emV, n)

        def wait_out(eng, name):
            emptied(eng, GID[name])

        def wait_full(eng, name):
            eng.wait_ge(s_full, GID[name] + 1)

        def bank(name):
            return psum[:, PAIR.get(name, GID[name] % 4), :]

        def two(ap):
            return ap.rearrange("p (h n) -> p h n", h=2)[:, :, 0:HALF]

        def load_parameters(eng, spec, s):
            for name, k in spec:
                a = I[name][0]
                src = a.rearrange("j (c p) -> (j c) p", p=P) if name == "w_conv_a" else a.rearrange("(c p) -> c p", p=P)
                eng.dma_start(raw_par[PAR_AT[name]:PAR_AT[name] + k, :], src).then_inc(s, 16)

        block = ctx.enter_context(nc.Block())

        @block.sync
        def _(sp):
            for t in range(4):
                sp.dma_start(x_tok[:, t, :], I["x_prompt"][0, t * P:(t + 1) * P, :]).then_inc(s_x, 16)
            sp.dma_start(x_tok[0:NS, 4, :], I["x_sample"][:, 0, :]).then_inc(s_x, 16)
            w_in = I["w_in"][0].rearrange("(k p) n -> p k n", p=P)
            for k in range(KC):
                sp.dma_start(wslot(0)[:, k, :], w_in[:, k, 1024:2048]).then_inc(s_win[k // 2], 16)
            for k in range(KC):
                sp.dma_start(wslot(1)[:, k, :], w_in[:, k, 0:1024]).then_inc(s_load[1], 16)

            def big(n, slot, src):
                sp.dma_start(wslot(slot), src.rearrange("(k p) n -> p k n", p=P)).then_inc(s_load[n], 16)

            def big_cache(n, slot, src, b0):
                for b in range(4):
                    sp.dma_start(cache(slot, b), src[0, b0 + b].rearrange("(p m) h d -> p m (h d)", m=2)).then_inc(
                        s_load[n], 16)

            big(2, 2, I["w_v"][0])
            wait_out(sp, "cb")
            sp.dma_start(mem_tok, I["mem_prompt"][0].rearrange("(m p) n -> p m n", p=P)).then_inc(s_mem, 16)
            wait_full(sp, "zs3")
            big(3, 0, I["w_k"][0])
            wait_full(sp, "zg3")
            big(4, 1, I["w_out"][0])
            wait_out(sp, "v0")
            sp.dma_start(o_mv[0, 0, 0:P].rearrange("m h d -> m (h d)"), v_tok[:, 0, :]).then_inc(s_out, 16)
            wait_full(sp, "ri3")
            sp.dma_start(wr, I["w_router"][0].rearrange("(k p) e -> p k e", p=P)).then_inc(s_wr, 16)
            wait_out(sp, "tails")
            sp.dma_start(o_cap[0, 0], tail[27:30, 0, :]).then_inc(s_tailout, 16)
            sp.dma_start(o_cas[0, :, 2, :], tail[30:38, 0, :]).then_inc(s_tailout, 16)
            sp.dma_start(o_cbp[0, 0], tail[0:30, 1, :]).then_inc(s_tailout, 16)
            sp.dma_start(o_cbs[0, :, 29, :], tail[30:38, 1, :]).then_inc(s_tailout, 16)
            wait_full(sp, "k1")
            big(5, 0, I["w_q"][0])
            for m in range(2):
                wait_out(sp, f"k{m}")
                sp.dma_start(o_mk[0, 0, m * P:(m + 1) * P].rearrange("m h d -> m (h d)"), k_tok[:, m, :]).then_inc(s_kout, 16)
            wait_out(sp, "hlast")
            sp.dma_start(o_hp[0], tail[0:1, 0, :]).then_inc(s_out, 16)
            sp.dma_start(o_hs[0], tail[1:9, 0, :]).then_inc(s_out, 16)
            wait_full(sp, "wo7")
            big_cache(6, 1, I["cache_mem_k"], 0)
            wait_full(sp, "v1b")
            big_cache(7, 2, I["cache_mem_k"], 4)
            wait_out(sp, "v1b")
            sp.dma_start(o_mv[0, 0, P:2 * P].rearrange("m h d -> m (h d)"), v_tok[:, 1, :]).then_inc(s_out, 16)
            wait_full(sp, "q7")
            wait_out(sp, "qs")
            sp.dma_start(q_rows[:, :], q_s).then_inc(s_qrow, 16)
            sp.wait_ge(s_qrow, 16)
            for b in range(NS):
                sp.dma_start(q_all[:, b, :], q_rows[b:b + 1, :].broadcast_to([P, D])).then_inc(s_qall[b // 2], 16)
            def values(b):
                sp.dma_start(value_cache(b), I["cache_mem_v"][0, b].rearrange("(p m) h d -> p m (h d)", m=2)).then_inc(
                    s_val[b // 2], 16)

            sp.wait_ge(s_ss, 2)
            values(0)
            sp.wait_ge(s_ss, 4)
            w_o = I["w_o"][0].rearrange("(k p) n -> p k n", p=P)
            for n in range(4):
                sp.dma_start(wslot(1)[:, :, 256 * n:256 * n + 256], w_o[:, :, 256 * n:256 * n + 256]).then_inc(s_wo[n], 16)
            values(1)
            sp.wait_ge(s_ss, 6)
            values(2)
            sp.wait_ge(s_ss, NS)
            for b in range(3, NS):
                values(b)
            wait_full(sp, "os")
            sp.dma_start(w1s, I["w1_s"][0].rearrange("(k p) n -> p k n", p=P)).then_inc(s_load[8], 16)
            sp.dma_start(w3s, I["w3_s"][0].rearrange("(k p) n -> p k n", p=P)).then_inc(s_load[8], 16)
            sp.dma_start(w2s, I["w2_s"][0].rearrange("(k p) n -> p k n", p=P)).then_inc(s_load[8], 16)
            def expert(n, e, s):
                wu, wd = ew(n)
                sp.dma_start(wu[:, 0], I["w1_e"][0, e].rearrange("(p k) n -> p k n", k=KC)).then_inc(s, 16)
                sp.dma_start(wu[:, 1], I["w3_e"][0, e].rearrange("(p k) n -> p k n", k=KC)).then_inc(s, 16)
                sp.dma_start(wd, I["w2_e"][0, e].rearrange("(k p) n -> p k n", p=P)).then_inc(s, 16)

            expert(0, 0, s_w[0])
            wait_full(sp, "xb7")
            expert(1, 1, s_w[1])
            wait_out(sp, "count")
            sp.dma_start(ln3g, I["ln3_g"][0].rearrange("(a n) -> a n", a=1).broadcast_to([P, D])).then_inc(s_lnw, 16)
            sp.dma_start(ln3b, I["ln3_b"][0].rearrange("(a n) -> a n", a=1).broadcast_to([P, D])).then_inc(s_lnw, 16)
            wait_full(sp, "so4")
            expert(2, 2, s_w[2])
            expert(3, 3, s_w[3])
            with sp.Fori(0, E // 4 - 1) as i:
                for n in range(4):
                    sp.wait_ge(m_y, 4 * i + (n + 1))
                    expert(n, 4 * i + (n + 4), s_w[n])

            sp.wait_ge(s_over, 1)
            sp.wait_ge(m_y, E)
            n_max = sp.value_load(over[0:1, 0:1], min_val=0, max_val=T)
            with sp.If(n_max > CAP):
                with sp.Fori(1, E * (ROUNDS - 1) + 1) as i:
                    sp.wait_ge(f_sem["it"], i)
                    expert(0, (i - 1) % E, f_sem["w"])

            for p in range(2):
                sp.wait_ge(m_s[p], 16 * (E // 2))
            sp.wait_ge(s_done, 1)
            for n, t in enumerate(LAST_ORDER):
                w = width(t)
                if n >= 3:
                    sp.wait_ge(s_rowv, n - 2)
                for q, (j0, j1) in enumerate(PARTS):
                    sp.dma_start(y_in[n % 3][0:w, j0:j1, :],
                                 y_rows[t * D:t * D + w * TOPK, :].rearrange("(p j) n -> p j n", j=TOPK)[:, j0:j1, :]).then_inc(
                        s_yin[q][n % 3], 16)
            sp.wait_ge(s_out, 16 * (2 + 2))
            sp.wait_ge(s_final, 16 * TT)
            sp.wait_ge(s_tailout, 16 * 4)
            sp.wait_ge(s_stateout, 16 * 2)
            sp.wait_ge(s_kout, 16 * 2)

        @block.gpsimd
        def _(gp):
            load_parameters(gp, PAR_SPEC[8:], s_par2)
            gp.memset(ident[:, :], 0.0).then_inc(s_const, 1)
            gp.dma_start(st_h, I["state_rglru_h"][0]).then_inc(s_state, 16)
            gp.dma_start(st_ca, I["state_rglru_conv"][0].rearrange("b j n -> (b j) n")).then_inc(s_state, 16)
            for r in range(2):
                gp.dma_start(st_cb[:, r, :], I["state_dwconv"][0, 4 * r:4 * r + 4].rearrange("b j n -> (b j) n")).then_inc(s_state, 16)
            gp.wait_ge(s_const, 1)
            gp.affine_select(out=ident[:, :], in_=ident[:, :], compare_op=ALU.not_equal, fill=1.0, base=0,
                             pattern=[[-1, P]], channel_multiplier=1).then_inc(s_const, 1)
            gp.memset(mean_d[:, :], 1.0 / D).then_inc(s_const, 1)
            gp.memset(mean_c[:, :], 1.0 / 512).then_inc(s_const, 1)
            gp.memset(ones[:, :], 1.0).then_inc(s_const, 1)
            gp.memset(eps_t[:, :], EPS).then_inc(s_const, 1)
            gp.memset(gate_w[:, :, :, :], 0.0).then_inc(s_gwz, 1)
            gp.wait_ge(s_gwz, 1)
            for m, name in enumerate(("w_rg_a", "w_rg_x")):
                for q in range(2):
                    gp.dma_start(gate_w[64 * q:64 * q + 64, m, :, 64 * q:64 * q + 64],
                                 I[name][0].rearrange("(c q) i j -> q i c j", q=2)[q]).then_inc(s_gw, 16)
            gp.dma_start(o_cas[0, :, 0:WA - 2, :], I["state_rglru_conv"][0, :, 1:WA - 1, :]).then_inc(s_stateout, 16)
            gp.dma_start(o_cbs[0, :, 0:WB - 2, :], I["state_dwconv"][0, :, 1:WB - 1, :]).then_inc(s_stateout, 16)
            gp.wait_ge(s_glu, RC)
            for turn, c in enumerate(POOL_CHUNKS):
                x, out = gluT[:, c, :], cT[:, c, :]
                gp.tensor_scalar(out[:, 0:SEQ], x[:, 0:SEQ], wb_tap(c, WB - 1), col("b_conv_b", c),
                                 ALU.mult, ALU.add).then_inc(s_convp, 1)
                for n in range(1, WB):
                    product = turn * (WB - 1) + n - 1
                    gp.wait_ge(s_convp, turn * WB + n)
                    gp.wait_ge(s_tap, product + 1)
                    gp.tensor_tensor(out[:, n:SEQ], out[:, n:SEQ], tap_mem[:, product % 4, 0:SEQ - n], ALU.add).then_inc(s_convp, 1)
            wait_full(gp, "ri3")
            gp.memset(tri, 1.0).then_inc(s_late, 1)
            gp.iota(slots, pattern=[[1, CAP]], base=0, channel_multiplier=0, allow_small_or_imprecise_dtypes=True).then_inc(s_late, 1)
            gp.wait_ge(s_late, 2)
            gp.affine_select(out=tri, in_=tri, compare_op=ALU.is_gt, fill=0.0, base=0, pattern=[[1, P]],
                             channel_multiplier=-1).then_inc(s_late, 1)
            wait_full(gp, "pt3")
            gp.memset(unit, 0.0).then_inc(s_unit, 1)
            gp.wait_ge(s_unit, 1)
            gp.memset(unit[:, 0:NS * NS:NS + 1], 1.0).then_inc(s_unit, 1)
            wait_full(gp, "osT")
            gp.memset(rmask, 1.0).then_inc(s_late, 1)
            gp.memset(tri8, 1.0).then_inc(s_late, 1)
            gp.iota(row8, pattern=[[0, TT]], base=0, channel_multiplier=TOPK,
                    allow_small_or_imprecise_dtypes=True).then_inc(s_late, 1)
            gp.iota(tile8, pattern=[[TOPK * P, TT]], base=-int(FAR), channel_multiplier=0,
                    allow_small_or_imprecise_dtypes=True).then_inc(s_late, 1)
            gp.wait_ge(s_late, 7)
            gp.affine_select(out=rmask[:, 4:5], in_=rmask[:, 4:5], compare_op=ALU.is_gt, fill=0.0, base=NS,
                             pattern=[[0, 1]], channel_multiplier=-1).then_inc(s_late, 1)
            gp.affine_select(out=tri8, in_=tri8, compare_op=ALU.is_gt, fill=0.0, base=0, pattern=[[1, 8], [-1, 8]],
                             channel_multiplier=0).then_inc(s_late, 1)
            gp.dma_start(rbias, I["router_bias"][0].rearrange("(a n) -> a n", a=1).broadcast_to([P, E])).then_inc(s_rt, 16)
            wait_full(gp, "h3b1")
            gp.iota(rounds_t, pattern=[[CAP, ROUNDS - 1]], base=CAP, channel_multiplier=0,
                    allow_small_or_imprecise_dtypes=True).then_inc(s_late, 1)
            for n in range(2):
                gp.memset(xg[n], 0.0).then_inc(m_z, 1)
            gp.wait_ge(m_z, 2)
            gp.wait_ge(s_x2out, 16 * TT)

            last_x = gp.to_reg(T - 1)
            last_y = gp.to_reg(NROW - 1)

            def gather(n, b, s):
                gp.indirect_dma_start(
                    out=xg[b][0:CAP, :], out_offset=None, in_=x2_rows[:, :],
                    in_offset=bass.IndirectOffsetOnAxis(ap=idx_x[0:CAP, n:n + 1], axis=0),
                    bounds_check=last_x, oob_is_err=False).then_inc(s, 16)

            def scatter(n, b, s):
                gp.indirect_dma_start(
                    out=y_rows[:, :], out_offset=bass.IndirectOffsetOnAxis(ap=idx_y[0:CAP, n:n + 1], axis=0),
                    in_=ys[0:CAP, b, :], in_offset=None,
                    bounds_check=last_y, oob_is_err=False).then_inc(s, 16)

            def g_step(e, n):
                gp.wait_ge(s_x2out, 16 * TT)
                gp.wait_ge(m_idx, e + 1)
                if at_least(e, 4):
                    gp.wait_ge(m_xt, e - 3)
                gp.sem_inc(m_go, 1)
                gather(n, n % 4, m_g[n % 4])

            def s_step(e, n):
                gp.wait_ge(m_ya, e + 1)
                gp.wait_ge(m_yv, e + 1)
                gp.sem_inc(m_go, 1)
                scatter(n, n % 2, m_s[n % 2])

            g_step(0, 0)
            g_step(1, 1)
            gp.wait_ge(s_table, 1)
            gp.wait_ge(s_over, 1)
            for n in range(2, 4):
                gp.memset(xg[n], 0.0).then_inc(m_z, 1)
            gp.wait_ge(m_z, 4)
            g_step(2, 2)
            g_step(3, 3)
            for e in range(1, NB + 1):
                s_step(e - 1, (e - 1) % NB)
                g_step(e + 3, (e + 3) % NB)
            with gp.Fori(1, E // NB - 1) as i:
                for k in range(1, NB + 1):
                    s_step(NB * i + (k - 1), (k - 1) % NB)
                    g_step(NB * i + (k + 3), (k + 3) % NB)
            for e in range(E - NB + 1, E + 1):
                s_step(e - 1, (e - 1) % NB)
                if e + 3 < E:
                    g_step(e + 3, (e + 3) % NB)

            gp.wait_ge(s_over, 1)
            n_max = gp.value_load(over[0:1, 0:1], min_val=0, max_val=T)
            with gp.If(n_max > CAP):
                gp.wait_ge(m_g[0], 16 * (E // 4))
                gp.wait_ge(m_s[0], 16 * (E // 2))
                gp.wait_ge(m_s[1], 16 * (E // 2))
                gp.sem_inc(f_sem["it"], 1)
                with gp.Fori(1, E * (ROUNDS - 1) + 1) as i:
                    gp.wait_ge(s_x2out, 16 * TT)
                    gp.wait_ge(f_sem["idx"], i)
                    gp.sem_inc(m_go, 1)
                    gather(0, 0, f_sem["g"])
                    gp.wait_ge(f_sem["ya"], i)
                    gp.wait_ge(f_sem["yv"], i)
                    gp.sem_inc(m_go, 1)
                    scatter(0, 0, f_sem["s"])
                    gp.wait_ge(f_sem["s"], 16 * i)
                    gp.sem_inc(f_sem["it"], 1)
            gp.sem_inc(s_done, 1)
            for n, t in enumerate(LAST_ORDER):
                w = width(t)
                rows_in = y_in[n % 3][0:w]
                gp.wait_ge(s_yin[0][n % 3], 16 * (n // 3 + 1))
                gp.tensor_tensor(rows_in[:, 0, :], rows_in[:, 0, :], rows_in[:, POOL_ROWS[0], :], ALU.add).then_inc(s_ypool, 1)
                gp.wait_ge(s_ypool, 2 * n + 1)
                gp.wait_ge(s_yin[1][n % 3], 16 * (n // 3 + 1))
                gp.tensor_tensor(rows_in[:, 0, :], rows_in[:, 0, :], rows_in[:, POOL_ROWS[1], :], ALU.add).then_inc(s_ypool, 1)

        @block.tensor
        def _(pe):
            def open_group(name):
                g = GID[name]
                if g >= 4:
                    emptied(pe, g - 4)
                return bank(name)

            def mm(out, lhsT, rhs, first, last):
                return pe.matmul(out, lhsT, rhs, start=first, stop=last)

            def wide(name, w, act, ks, before=None):
                ps = open_group(name)
                for n, k in enumerate(ks):
                    if before is not None:
                        before(k)
                    for h in range(2):
                        last = mm(ps[:, 512 * h:512 * h + HALF], w(k), act(k)[:, HALF * h:HALF * h + HALF],
                                  n == 0, n == len(ks) - 1)
                last.then_inc(s_full, 1)

            def turn(out, in_, n=P):
                return pe.transpose(out, in_, ident[0:n, 0:n])

            pe.wait_ge(s_const, 2)
            pe.wait_ge(s_x, 16 * TT)
            for c in range(KC):
                ps = open_group(f"x{c}")
                for t in range(TT):
                    w = width(t)
                    last = turn(ps[:, t * P:t * P + w], x_tok[0:w, t, c * P:(c + 1) * P], w)
                last.then_inc(s_full, 1)
            pe.wait_ge(s_const, 6)
            pe.wait_ge(s_par, 16 * 8)
            pe.wait_ge(s_par2, 16 * (len(PAR_SPEC) - 8))
            pe.wait_ge(s_wcbl, 16)
            ps = open_group("par")
            turn(ps[:, 0:NPAR], raw_par[0:NPAR, :], NPAR)
            turn(ps[:, 512:512 + WB * RC], raw_wcb[0:WB * RC, :], WB * RC).then_inc(s_full, 1)

            def first_weights(k):
                wait_out(pe, f"x{k}")
                if k % 2 == 0:
                    pe.wait_ge(s_win[k // 2], 16 * 2)

            def turn_states():
                pe.wait_ge(s_state, 16 * 4)
                ps = open_group("st")
                for c in range(RC):
                    turn(ps[:, NS * c:NS * c + NS], st_h[:, c * P:(c + 1) * P], NS)
                for c in range(RC):
                    last = turn(ps[:, 32 + 24 * c:32 + 24 * c + 24], st_ca[:, c * P:(c + 1) * P], 24)
                last.then_inc(s_full, 1)
                ps = open_group("cb")
                for c in range(RC):
                    for r in range(2):
                        at = 512 * (c // 2) + 240 * (c % 2) + 120 * r
                        last = turn(ps[:, at:at + 120], st_cb[:, r, c * P:(c + 1) * P], 120)
                last.then_inc(s_full, 1)

            for j in range(2 * RC):
                if j == RC:
                    turn_states()
                name = ("zv", "zs")[j // RC] + str(j % RC)
                wide(name, lambda k: wslot(0)[:, k, j * P:(j + 1) * P], lambda k: xT[:, k, :], range(KC),
                     before=first_weights if j == 0 else None)
            pe.wait_ge(s_load[1], 16 * KC)
            for j in range(2 * RC):
                name = ("zu", "zg")[j // RC] + str(j % RC)
                at = (j + RC) % (2 * RC)
                wide(name, lambda k: wslot(1)[:, k, at * P:(at + 1) * P], lambda k: xT[:, k, :], range(KC))
            pe.wait_ge(s_mem, 16)
            for g in range(2):
                ps = open_group(f"mt{g}")
                for c in range(4):
                    for m in range(2):
                        last = turn(ps[:, 256 * c + P * m:256 * c + P * m + P], mem_tok[:, m, (4 * g + c) * P:(4 * g + c + 1) * P])
                last.then_inc(s_full, 1)

            def memory(names, w, s, first=0):
                pe.wait_ge(s, 16)
                for m, name in enumerate(names, first):
                    ps = open_group(name)
                    for k in range(KC):
                        for n in range(2):
                            last = mm(ps[:, 512 * n:512 * n + 512], memT[:, k, m * P:(m + 1) * P],
                                      w[:, k, 512 * n:512 * n + 512], k == 0, k == KC - 1)
                    last.then_inc(s_full, 1)

            wait_out(pe, "mt1")
            memory(("v0",), wslot(2), s_load[2])
            wait_out(pe, "zu3")
            pe.wait_ge(s_glu, RC)
            ps = open_group("tails")
            for c in range(RC):
                turn(ps[0:38, c * P:(c + 1) * P], uT[:, c, T - 38:T])
            for c in range(RC):
                last = turn(ps[0:38, 512 + c * P:512 + (c + 1) * P], gluT[:, c, T - 38:T])
            last.then_inc(s_full, 1)
            pe.wait_ge(s_gw, 16 * 4)
            pe.wait_ge(s_uc, 1)
            for m, name in enumerate(("ra", "ri")):
                for c in range(RC):
                    wide(f"{name}{c}", lambda k: gate_w[:, m, c, :], lambda k: ucT[:, c, :], range(1))

            norm_at = [0]

            def norm_mean(name, w, x, n):
                wide(name, lambda k: w[:, :], lambda k: x[:, k, :], range(n))

            def norm_var(name, w, sqs, n):
                wide(name, lambda k: w[:, :], lambda k: sqs[:, k, :], range(n),
                     before=lambda k: pe.wait_ge(s_sq, norm_at[0] + k + 1))
                norm_at[0] += n

            memory(("k0",), wslot(0), s_load[3])
            pe.wait_ge(s_convb, 1)
            pe.wait_ge(s_convp, len(POOL_CHUNKS) * WB)
            norm_mean("cmean", mean_c, cT, RC)
            memory(("k1",), wslot(0), s_load[3], 1)
            norm_var("cvar", mean_c, sq_c, RC)
            wait_out(pe, "k1")
            for g in range(2):
                ps = open_group(f"kt{g}")
                for c in range(4):
                    for m in range(2):
                        last = turn(ps[:, 256 * c + P * m:256 * c + P * m + P], k_tok[:, m, (4 * g + c) * P:(4 * g + c + 1) * P])
                last.then_inc(s_full, 1)
            pe.wait_ge(s_h, RC)
            ps = open_group("hlast")
            for c in range(RC):
                last = turn(ps[0:9, c * P:(c + 1) * P], ucT[:, c, SEQ - 1:T])
            last.then_inc(s_full, 1)
            pe.wait_ge(s_load[4], 16)

            def mixed(k):
                if k < RC:
                    pe.wait_ge(s_ya, k + 1)
                else:
                    pe.wait_ge(s_ln, k - RC + 1)

            for j in range(KC):
                wide(f"wo{j}", lambda k: wslot(1)[:, k, j * P:(j + 1) * P],
                     lambda k: gT[:, k, :] if k < RC else cT[:, k - RC, :], range(KC), before=mixed if j == 0 else None)
            wait_out(pe, "wo7")

            def value_half(name, n):
                ps = open_group(name)
                pe.wait_ge(s_memc, 1)
                for k in range(KC):
                    last = mm(ps[:, 0:512], memT_late[:, k, :], wslot(2)[:, k, 512 * n:512 * n + 512], k == 0, k == KC - 1)
                last.then_inc(s_full, 1)

            pe.wait_ge(s_xsum, 1)
            norm_mean("mean1", mean_d, xsum, 1)
            value_half("v1a", 0)
            norm_var("var1", mean_d, sq, KC)
            value_half("v1b", 1)
            pe.wait_ge(s_load[5], 16)
            for j in range(KC):
                wide(f"q{j}", lambda k: wslot(0)[:, k, j * P:(j + 1) * P], lambda k: xT[:, k, :], range(KC),
                     before=(lambda k: pe.wait_ge(s_ln, RC + k + 1)) if j == 0 else None)
            wait_out(pe, "q7")
            ps = open_group("qs")
            for c in range(KC):
                last = turn(ps[0:NS, c * P:(c + 1) * P], qT[:, c, SEQ:T])
            last.then_inc(s_full, 1)

            def scores(t):
                ps = open_group(f"sc{t}")
                for h in range(XH):
                    for d in range(2):
                        last = mm(ps[:, XD * h:XD * h + XD], qT[:, 2 * h + d, t * P:(t + 1) * P], keyT[:, 2 * h + d, :],
                                  d == 0, d == 1)
                last.then_inc(s_full, 1)

            def turn_probs(t):
                pe.wait_ge(s_prob, t + 1)
                ps = open_group(f"pt{t}")
                for h in range(XH):
                    for m in range(2):
                        at = (2 * h + m) * P
                        last = turn(ps[:, at:at + P], probs[:, t % 2, h, m * P:(m + 1) * P])
                last.then_inc(s_full, 1)

            def prompt_out(j):
                ps = open_group(f"o{j}")
                if j == 0:
                    wait_out(pe, "pt3")
                for m in range(2):
                    last = mm(ps[:, 0:SEQ], v_tok[:, m, j * P:(j + 1) * P], prT[:, 2 * (j // 2) + m, 0:SEQ], m == 0, m == 1)
                last.then_inc(s_full, 1)

            def turn_sample_scores():
                ps = open_group("ssT")
                pe.wait_ge(s_ss, NS)
                for m in range(2):
                    last = turn(ps[0:32, m * P:(m + 1) * P], ss[:, m, :])
                last.then_inc(s_full, 1)

            def turn_sample_probs():
                ps = open_group("spT")
                pe.wait_ge(s_prob, 5)
                for m in range(2):
                    last = turn(ps[:, 32 * m:32 * m + 32], sp[:, m * P:(m + 1) * P], 32)
                last.then_inc(s_full, 1)

            def half_wide(name, w, act, ks, h, before=None):
                ps = open_group(name)
                for n, k in enumerate(ks):
                    if before is not None:
                        before(k)
                    last = mm(ps[:, 0:HALF], w(k), act(k)[:, HALF * h:HALF * h + HALF], n == 0, n == len(ks) - 1)
                last.then_inc(s_full, 1)

            def project(name, h):
                j = int(name[2])
                if h == 0 and j % 2 == 0:
                    pe.wait_ge(s_wo[j // 2], 16)
                if (h, j) == (0, 0):
                    wait_out(pe, "o7")
                half_wide(name, lambda k: wslot(1)[:, k, j * P:(j + 1) * P], lambda k: oT[:, k, :], range(KC), h)

            for name in ATTENTION:
                if name == "ssT":
                    turn_sample_scores()
                elif name == "spT":
                    turn_sample_probs()
                elif name[0] == "o":
                    prompt_out(int(name[1]))
                elif name[0] == "x":
                    project(name, 0)
                else:
                    {"sc": scores, "pt": turn_probs}[name[0:2]](int(name[2]))
            for c in range(4, KC):
                project(f"xa{c}", 0)

            def half_mean(name, h, turn_no):
                pe.wait_ge(s_xsum, turn_no)
                half_wide(name, lambda k: mean_d[:, :], lambda k: xsum[:, 0, :], range(1), h)

            def half_var(name, h):
                half_wide(name, lambda k: mean_d[:, :], lambda k: sq[:, k, :], range(KC), h,
                          before=lambda k: pe.wait_ge(s_sq, norm_at[0] + k + 1))
                norm_at[0] += KC

            half_mean("mean2a", 0, 2)
            pe.wait_ge(s_unit, 2)
            ps = open_group("os")
            for b in range(NS):
                if b == 5:
                    half_var("var2a", 0)
                pe.wait_ge(s_pv, b + 1)
                for n in range(2):
                    last = mm(ps[0:NS, 512 * n:512 * n + 512], unit[:, NS * b:NS * b + NS],
                              value_cache(b)[:, 0, 512 * n:512 * n + 512], b == 0, b == NS - 1)
            last.then_inc(s_full, 1)
            wait_out(pe, "os")
            ps = open_group("osT")
            for j in range(KC):
                last = turn(ps[:, NS * j:NS * j + NS], o_s[:, j * P:(j + 1) * P], NS)
            last.then_inc(s_full, 1)
            wait_out(pe, "osT")
            for c in range(KC):
                project(f"xb{c}", 1)

            def shared_up(name, h):
                w, j = (w1s, w3s)["13".index(name[1])], "ab".index(name[2])
                half_wide(name, lambda k: w[:, k, j * P:(j + 1) * P], lambda k: xT[:, k, :], range(KC), h)

            pe.wait_ge(s_load[8], 16 * 3)
            pe.wait_ge(s_ln, RC + 2 * KC)
            shared_up("h1a0", 0)
            half_mean("mean2b", 1, 3)
            shared_up("h3a0", 0)
            half_var("var2b", 1)
            shared_up("h1b0", 0)
            pe.wait_ge(s_wr, 16)

            def router(name, h, before=None):
                ps = open_group(name)
                for k in range(KC):
                    if before is not None:
                        before(k)
                    last = mm(ps[0:E, 0:HALF], wr[:, k, :], xT[:, k, HALF * h:HALF * h + HALF], k == 0, k == KC - 1)
                last.then_inc(s_full, 1)

            def turn_x(t):
                w = width(t)
                ps = open_group(f"x2{t}")
                for k in range(KC):
                    last = turn(ps[0:w, k * P:(k + 1) * P], xT[:, k, t * P:t * P + w])
                last.then_inc(s_full, 1)

            router("rt0", 0)
            router("rt1", 1, before=lambda k: pe.wait_ge(s_ln, RC + 2 * KC + k + 1))
            turn_x(0)
            wait_out(pe, "rt1")
            ps = open_group("rtT")
            for t in range(TT):
                w = width(t)
                last = turn(ps[0:w, E * t:E * t + E], score_t[:, t * P:t * P + w], E)
            last.then_inc(s_full, 1)
            for t in range(1, TT):
                turn_x(t)
            shared_up("h3b0", 0)
            for name in ("h1a1", "h3a1", "h1b1", "h3b1"):
                shared_up(name, 1)
            pe.wait_ge(s_late, 9)
            pe.wait_ge(s_sel, 1)
            ps = open_group("rank")
            for t in range(TT):
                for u in range(t + 1):
                    last = mm(ps[:, E * t:E * t + E], tri if u == t else ones[:, :], sel_b[:, u, :], u == 0, u == t)
            last.then_inc(s_full, 1)
            ps = open_group("count")
            for t in range(TT):
                last = mm(ps[:, 0:E], ones[:, :], sel_b[:, t, :], t == 0, t == TT - 1)
            last.then_inc(s_full, 1)
            wait_out(pe, "h1b1")
            wait_out(pe, "h3b1")

            def shared_out(t):
                w = width(t)
                if t >= 3:
                    wait_out(pe, f"so{t - 3}")
                elif t > 0:
                    wait_out(pe, "count")
                ps = bank(f"so{t}")
                for k in range(2):
                    for n in range(2):
                        last = mm(ps[0:w, 512 * n:512 * n + 512], shT[:, k, t * P:t * P + w], w2s[:, k, 512 * n:512 * n + 512],
                                  k == 0, k == 1)
                last.then_inc(s_full, 1)

            shared_out(0)
            pe.wait_ge(s_table, 1)
            wait_out(pe, "count")

            def find(n, e):
                for t in range(TT):
                    last = mm(psum[0:CAP, 3, 512 * (n % 2):512 * (n % 2) + 6], onehot[:, n % 2, t, :], table[:, t, e, :],
                              t == 0, t == TT - 1)
                return last

            def turn_rows(n):
                for k in range(KC):
                    at = 512 * (k // 4) + CAP * (k % 4)
                    last = turn(psum[:, 1, at:at + CAP], xg[n % 4][0:CAP, k:D:KC], CAP)
                return last

            def up(b, part):
                wu, _ = ew(part)
                for j in range(4):
                    at = 512 * b + CAP * j
                    for k in range(KC):
                        last = mm(psum[:, 2, at:at + CAP], wu[:, j // 2, k, P * (j % 2):P * (j % 2) + P], xgT[:, b, k, :],
                                  k == 0, k == KC - 1)
                return last

            def down(b, part):
                _, wd = ew(part)
                for n in range(2):
                    for k in range(2):
                        last = mm(psum[0:CAP, 0, 512 * n:512 * n + 512], hidT[:, b, CAP * k:CAP * k + CAP],
                                  wd[:, k, 512 * n:512 * n + 512], k == 0, k == 1)
                return last

            def a_step(e, n):
                pe.wait_ge(m_oh, e + 1)
                if at_least(e, 2):
                    pe.wait_ge(m_idx, e - 1)
                find(n, e).then_inc(m_ip, 1)

            def b_step(e, n, gath):
                pe.wait_ge(m_g[n % 4], gath)
                if at_least(e, 1):
                    pe.wait_ge(m_xc, e)
                turn_rows(n).then_inc(m_xt, 1)

            def c_step(e, n, wait_w):
                pe.wait_ge(m_xc, e + 1)
                pe.wait_ge(s_w[n % 4], wait_w)
                if at_least(e, 2):
                    pe.wait_ge(m_hd, e - 1)
                up(n % 2, n % 4).then_inc(m_h, 1)

            def y_step(e, n):
                pe.wait_ge(m_hd, e + 1)
                if at_least(e, 1):
                    pe.wait_ge(m_ya, e)
                    pe.wait_ge(m_yv, e)
                down(n % 2, n % 4).then_inc(m_y, 1)

            a_step(0, 0)
            a_step(1, 1)
            shared_out(1)
            a_step(2, 2)
            shared_out(2)
            a_step(3, 3)
            shared_out(3)
            shared_out(4)
            wait_out(pe, "so4")
            b_step(0, 0, 16)
            c_step(0, 0, 48)
            b_step(1, 1, 16)

            def step(e, k, i):
                c_step(e, k % NB, 48 * (2 * i + (k // 4 + 1)))
                if exists(e + 1):
                    b_step(e + 1, (k + 1) % NB, 16 * (2 * i + ((k + 1) // 4 + 1)))
                y_step(e - 1, (k - 1) % NB)
                if exists(e + 3):
                    a_step(e + 3, (k + 3) % NB)

            LAST = E // NB - 1
            for k in range(1, NB + 1):
                step(k, k, 0)
            with pe.Fori(1, LAST) as i:
                for k in range(1, NB + 1):
                    step(NB * i + k, k, i)
            for k in range(1, NB):
                step(NB * LAST + k, k, LAST)
            y_step(E - 1, NB - 1)

            pe.wait_ge(s_over, 1)
            n_max = pe.value_load(over[0:1, 0:1], min_val=0, max_val=T)
            with pe.If(n_max > CAP):
                pe.wait_ge(m_ya, E)
                pe.wait_ge(m_yv, E)
                with pe.Fori(0, E * (ROUNDS - 1)) as i:
                    pe.wait_ge(f_sem["oh"], i + 1)
                    find(0, i % E).then_inc(f_sem["ip"], 1)
                    pe.wait_ge(f_sem["g"], 16 * i + 16)
                    turn_rows(0).then_inc(f_sem["xt"], 1)
                    pe.wait_ge(f_sem["xc"], i + 1)
                    pe.wait_ge(f_sem["w"], 48 * i + 48)
                    up(0, 0).then_inc(f_sem["h"], 1)
                    pe.wait_ge(f_sem["hd"], i + 1)
                    down(0, 0).then_inc(f_sem["y"], 1)

            pe.wait_ge(m_ya, E)
            pe.wait_ge(m_yv, E)
            for n, t in enumerate(LAST_ORDER):
                w = width(t)
                if w < P:
                    continue
                if n >= 4:
                    pe.wait_ge(s_rowv, n - 3)
                for q in range(3):
                    pe.wait_ge(s_yin[q][n % 3], 16 * (n // 3 + 1))
                    for j in PE_ROWS[q]:
                        for h in range(2):
                            last = mm(psum[0:w, n % 4, 512 * h:512 * h + 512], ident[0:w, 0:w],
                                      y_in[n % 3][0:w, j, 512 * h:512 * h + 512], j == 2, j == 5)
                last.then_inc(s_ysum, 1)

        @block.scalar
        def _(act):
            load_parameters(act, PAR_SPEC[:8], s_par)
            act.dma_start(raw_wcb[0:WB * RC, :], I["w_conv_b"][0].rearrange("j (c p) -> (j c) p", p=P)).then_inc(s_wcbl, 16)

            def empty(name, out, func=ACT.Copy, **kw):
                wait_full(act, name)
                act.activation(out, two(bank(name)), func, **kw).then_inc(s_emA, 1)

            for c in range(0, KC, 2):
                wait_full(act, f"x{c}")
                act.activation(xT[:, c, :], bank(f"x{c}")[:, 0:T], ACT.Copy).then_inc(s_emA, 1)
            wait_out(act, "par")
            act.activation(c8[:, 0, :], par[:, PAR_AT["rg_lambda"]:PAR_AT["rg_lambda"] + RC], ACT.Abs).then_inc(s_abs, 1)
            act.wait_ge(s_abs, 1)
            act.activation(c8[:, 1, :], c8[:, 0, :], ACT.Exp, scale=-1.0).then_inc(s_c8e, 1)
            for c in range(RC):
                empty(f"zv{c}", halves(gluT[:, c, :]), ACT.Identity, bias=col("b_in", 8 + c))
            for c in range(RC):
                empty(f"zs{c}", halves(rT[:, c, :]), ACT.Sigmoid, bias=col("b_in", 12 + c))

            def tap_products(products):
                for product in products:
                    turn, n = product // (WB - 1), product % (WB - 1) + 1
                    c = POOL_CHUNKS[turn]
                    if product >= 4:
                        before = product - 4
                        act.wait_ge(s_convp, before // (WB - 1) * WB + before % (WB - 1) + 2)
                    act.activation(tap_mem[:, product % 4, 0:SEQ - n], gluT[:, c, 0:SEQ - n], ACT.Copy,
                                   scale=wb_tap(c, WB - 1 - n)).then_inc(s_tap, 1)

            for j in range(2 * RC):
                c = j % RC
                if j < RC:
                    empty(f"zu{c}", halves(uT[:, c, :]), ACT.Identity, bias=col("b_in", 4 + c))
                else:
                    empty(f"zg{c}", halves(gT[:, c, :]), ACT.Gelu_apprx_tanh, bias=col("b_in", c))
                if j == 0:
                    act.wait_ge(s_glu, RC)
                n_products = len(POOL_CHUNKS) * (WB - 1)
                if j < 2 * RC - 1:
                    tap_products(range(n_products * j // (2 * RC - 1), n_products * (j + 1) // (2 * RC - 1)))
            for g in range(2):
                wait_full(act, f"mt{g}")
                act.activation(memT[:, 4 * g:4 * g + 4, :], bank(f"mt{g}").rearrange("p (c m) -> p c m", c=4), ACT.Copy).then_inc(s_emA, 1)
            act.wait_ge(s_convp, len(POOL_CHUNKS) * WB)
            wait_full(act, "v0")
            act.activation(v_tok[:, 0, :], bank("v0"), ACT.Copy).then_inc(s_emA, 1)
            wait_full(act, "tails")
            act.activation(tail[:, :, :], bank("tails")[0:38, :].rearrange("p (m n) -> p m n", m=2), ACT.Copy).then_inc(s_emA, 1)
            act.wait_ge(s_glu, RC)
            for c in range(RC):
                empty(f"ra{c}", halves(rT[:, c, :]), ACT.Sigmoid, bias=col("b_rg_a", c))
            wait_full(act, "tails")
            act.wait_ge(s_uc, 1)
            for c in range(RC):
                empty(f"ri{c}", halves(uT[:, c, :]), ACT.Sigmoid, bias=col("b_rg_x", c))
            act.wait_ge(s_c8, 1)
            act.wait_ge(s_convb, 1)
            wait_out(act, "ra3")
            for c in range(RC):
                act.activation(thT[:, c, :], rT[:, c, :], ACT.Tanh, scale=c8[:, 7, c:c + 1]).then_inc(s_tanh, 1)

            wait_full(act, "k0")
            act.activation(k_tok[:, 0, :], bank("k0"), ACT.Copy).then_inc(s_emA, 1)
            norm_at = [0]

            def norm_squares(x, sqs, n):
                for k in range(n):
                    act.wait_ge(s_sub, norm_at[0] + k + 1)
                    act.activation(sqs[:, k, :], x[:, k, :], ACT.Square).then_inc(s_sq, 1)

            def norm_root(var):
                empty(var, halves(rstd[:, :]), ACT.Sqrt, bias=eps_t[:, 0:1])

            def norm_gain(x, n, g, b, func):
                for k in range(n):
                    act.wait_ge(s_nrm, norm_at[0] + k + 1)
                    act.activation(x[:, k, :], x[:, k, :], func, bias=col(b, k), scale=col(g, k)).then_inc(s_ln, 1)
                norm_at[0] += n

            norm_squares(cT, sq_c, RC)
            wait_full(act, "k1")
            act.activation(k_tok[:, 1, :], bank("k1"), ACT.Copy).then_inc(s_emA, 1)
            for c in range(RC):
                act.wait_ge(s_srt, c + 1)
                act.activation(thT[:, c, :], thT[:, c, :], ACT.Sqrt, scale=-2.0).then_inc(s_root, 1)
            norm_root("cvar")
            act.wait_ge(s_h, RC)
            act.activation(memT_late, memT[:, :, P:2 * P], ACT.Copy).then_inc(s_memc, 1)
            act.wait_ge(s_memc, 1)
            for g in range(2):
                wait_full(act, f"kt{g}")
                act.activation(keyT[:, 4 * g:4 * g + 4, :], bank(f"kt{g}").rearrange("p (c m) -> p c m", c=4), ACT.Copy).then_inc(s_emA, 1)
            norm_gain(cT, RC, "ln_c_g", "ln_c_b", ACT.Silu)
            wait_full(act, "wo7")
            norm_squares(xT, sq, KC)
            wait_full(act, "v1a")
            act.activation(v_tok[:, 1, 0:512], bank("v1a")[:, 0:512], ACT.Copy).then_inc(s_emA, 1)
            norm_root("var1")
            norm_gain(xT, KC, "ln1_g", "ln1_b", ACT.Identity)
            wait_full(act, "v1b")
            act.activation(v_tok[:, 1, 512:1024], bank("v1b")[:, 0:512], ACT.Copy).then_inc(s_emA, 1)
            for c in range(KC):
                empty(f"q{c}", halves(qT[:, c, :]))
            act.wait_ge(s_kout, 16 * 2)
            wait_full(act, "qs")
            act.activation(q_s, bank("qs")[0:NS, :], ACT.Copy).then_inc(s_emA, 1)

            def softmax_exp(t):
                act.wait_ge(s_smax, t + 1)
                if t >= 2:
                    wait_full(act, f"pt{t - 2}")
                for h in range(XH):
                    last = act.activation(probs[:, t % 2, h, :], bank(f"sc{t}")[:, XD * h:XD * h + XD], ACT.Exp,
                                          bias=small[:, 4 + h:5 + h] if t % 2 == 0 else small[:, 12 + h:13 + h],
                                          scale=XD ** -0.5,
                                          accum_out=small[:, 16 + 4 * (t % 2) + h:17 + 4 * (t % 2) + h])
                    if h < XH - 1:
                        last.then_inc(s_ssum, 1)
                last.then_inc(s_emA, 1)

            def take_probs(t):
                wait_full(act, f"pt{t}")
                act.activation(prT[:, :, t * P:(t + 1) * P], bank(f"pt{t}").rearrange("p (k n) -> p k n", k=KC), ACT.Copy).then_inc(s_emA, 1)

            def take_out(j):
                wait_full(act, f"o{j}")
                act.activation(oT[:, j, 0:SEQ], bank(f"o{j}")[:, 0:SEQ], ACT.Copy).then_inc(s_emA, 1)

            for name in ATTENTION:
                if name == "ssT":
                    act.wait_ge(s_smax, 5)
                    act.activation(sp, bank("ssT")[0:32, 0:N_MEM], ACT.Exp, bias=small[0:32, 25:26], scale=XD ** -0.5,
                                   accum_out=small[0:32, 26:27]).then_inc(s_emA, 1)
                elif name == "spT":
                    wait_full(act, "spT")
                    act.activation(sample_p, bank("spT")[:, 0:64].rearrange("p (m n) -> p m n", m=2), ACT.Copy).then_inc(s_emA, 1)
                    wait_out(act, "spT")
                    for b in range(NS):
                        if b % 2 == 0:
                            act.wait_ge(s_val[b // 2], 16 * 2)
                        for h in range(XH):
                            v = value_cache(b)[:, 0, XD * h:XD * h + XD]
                            last = act.activation(v, v, ACT.Copy, scale=sample_p[:, 0, 4 * b + h:4 * b + h + 1])
                        last.then_inc(s_pv0, 1)
                elif name[0] == "o":
                    take_out(int(name[1]))
                elif name[0:2] == "sc":
                    softmax_exp(int(name[2]))
                elif name[0:2] == "pt":
                    take_probs(int(name[2]))

            def half(ap, h):
                return ap[:, HALF * h:HALF * h + HALF]

            def half_squares(h):
                for k in range(KC):
                    act.wait_ge(s_sub, norm_at[0] + k + 1)
                    act.activation(half(sq[:, k, :], h), half(xT[:, k, :], h), ACT.Square).then_inc(s_sq, 1)

            def half_root(name, h):
                wait_full(act, name)
                act.activation(half(rstd[:, :], h), bank(name)[:, 0:HALF], ACT.Sqrt, bias=eps_t[:, 0:1]).then_inc(s_emA, 1)

            def half_gain(h):
                for k in range(KC):
                    act.wait_ge(s_nrm, norm_at[0] + k + 1)
                    act.activation(half(xT[:, k, :], h), half(xT[:, k, :], h), ACT.Identity, bias=col("ln2_b", k),
                                   scale=col("ln2_g", k)).then_inc(s_ln, 1)
                norm_at[0] += KC

            def shared_silu(name, h):
                wait_full(act, name)
                act.activation(half(sh1[:, "ab".index(name[2]), :], h), bank(name)[:, 0:HALF], ACT.Silu).then_inc(s_emA, 1)

            half_squares(0)
            half_root("var2a", 0)
            wait_full(act, "os")
            act.activation(o_s, bank("os")[0:NS, :], ACT.Copy).then_inc(s_emA, 1)
            wait_full(act, "osT")
            act.activation(oT[:, :, SEQ:T], bank("osT")[:, 0:64].rearrange("p (j b) -> p j b", j=KC), ACT.Copy).then_inc(s_emA, 1)
            half_gain(0)
            shared_silu("h1a0", 0)
            half_squares(1)
            half_root("var2b", 1)
            half_gain(1)
            shared_silu("h1b0", 0)
            for h in range(2):
                wait_full(act, f"rt{h}")
                act.activation(score_t[:, HALF * h:HALF * h + HALF], bank(f"rt{h}")[0:E, 0:HALF], ACT.Sigmoid).then_inc(s_emA, 1)

            def take_x(t):
                w = width(t)
                wait_full(act, f"x2{t}")
                act.activation(base[0:w, t, :], bank(f"x2{t}")[0:w, :], ACT.Copy).then_inc(s_emA, 1)
                emptied(act, GID[f"x2{t}"])
                act.dma_start(x2_rows[t * P:t * P + w, :], base[0:w, t, :]).then_inc(s_x2out, 16)

            take_x(0)
            act.wait_ge(s_rz, 1)
            wait_full(act, "rtT")
            act.activation(R[0][:, 0:4, :], bank("rtT")[:, 0:4 * E].rearrange("p (t e) -> p t e", t=4), ACT.Copy).then_inc(s_ssum, 1)
            act.activation(R[0][0:NS, 4, :], bank("rtT")[0:NS, 4 * E:5 * E], ACT.Copy).then_inc(s_emA, 1)
            for t in range(1, TT):
                take_x(t)
            shared_silu("h1a1", 1)
            shared_silu("h1b1", 1)

            def xc(b):
                return act.activation(xgT[:, b, :, :].rearrange("p (h k) s -> p h (k s)", h=2),
                                      psum[:, 1, :].rearrange("p (h n) -> p h n", h=2)[:, :, 0:4 * CAP], ACT.Copy)

            def sl(b):
                return act.activation(silu[:, b, :], psum[:, 2, 512 * b:512 * b + 2 * CAP], ACT.Silu)

            def yh(b, n):
                return act.activation(ys[0:CAP, b, 0:512], psum[0:CAP, 0, 0:512], ACT.Copy, scale=picked[0:CAP, n, 1:2])

            def b_step(e, n):
                act.wait_ge(m_xt, e + 1)
                if at_least(e, 2):
                    act.wait_ge(m_h, e - 1)
                xc(n % 2).then_inc(m_xc, 1)

            def c_step(e, n):
                act.wait_ge(m_h, e + 1)
                if at_least(e, 2):
                    act.wait_ge(m_hd, e - 1)
                sl(n % 2).then_inc(m_sl, 1)

            def y_step(e, n, sc):
                act.wait_ge(m_y, e + 1)
                if sc is not None:
                    act.wait_ge(m_s[n % 2], sc)
                yh(n % 2, n).then_inc(m_ya, 1)

            def step(e, k, i, sc):
                c_step(e, k % NB)
                if exists(e + 1):
                    b_step(e + 1, (k + 1) % NB)
                y_step(e - 1, (k - 1) % NB, sc)

            LAST = E // NB - 1
            b_step(0, 0)
            c_step(0, 0)
            b_step(1, 1)
            for k in range(1, NB + 1):
                step(k, k, 0, None if k <= 2 else 16 * ((k - 1) // 2))
            with act.Fori(1, LAST) as i:
                for k in range(1, NB + 1):
                    step(NB * i + k, k, i, 16 * (NB // 2) * i + 16 * ((k - 1) // 2))
            for k in range(1, NB):
                step(NB * LAST + k, k, LAST, 16 * ((NB * LAST + k - 1) // 2))
            y_step(E - 1, NB - 1, 16 * ((E - 1) // 2))

            act.wait_ge(s_over, 1)
            n_max = act.value_load(over[0:1, 0:1], min_val=0, max_val=T)
            with act.If(n_max > CAP):
                act.wait_ge(m_s[0], 16 * (E // 2))
                with act.Fori(0, E * (ROUNDS - 1)) as i:
                    act.wait_ge(f_sem["xt"], i + 1)
                    xc(0).then_inc(f_sem["xc"], 1)
                    act.wait_ge(f_sem["h"], i + 1)
                    sl(0).then_inc(f_sem["sl"], 1)
                    act.wait_ge(f_sem["y"], i + 1)
                    yh(0, 0).then_inc(f_sem["ya"], 1)

            for n, t in enumerate(LAST_ORDER):
                w = width(t)
                act.wait_ge(s_var, n + 1)
                act.activation(small[0:w, 36:37], small[0:w, 35:36], ACT.Sqrt, bias=eps_t[0:w, 0:1]).then_inc(s_sd, 1)
                dst = o_yp[0, t * P:(t + 1) * P, :] if t < 4 else o_ys[:, 0, :]
                act.wait_ge(s_res, n + 1)
                act.dma_start(dst, base[0:w, t, :]).then_inc(s_final, 16)

        @block.vector
        def _(dve):
            count = [0]

            def chain(ins):
                count[0] += 1
                ins.then_inc(s_v, 1)
                return count[0]

            def link(ins):
                dve.wait_ge(s_v, chain(ins))

            for c in range(1, KC, 2):
                wait_full(dve, f"x{c}")
                dve.tensor_copy(xT[:, c, :], bank(f"x{c}")[:, 0:T]).then_inc(s_emV, 1)
            wait_full(dve, "par")
            link(dve.tensor_copy(par[:, :], bank("par")[:, 0:NPAR]))
            dve.tensor_copy(wcb[:, :], bank("par")[:, 512:512 + WB * RC]).then_inc(s_emV, 1)
            wait_full(dve, "st")
            link(dve.tensor_copy(h0t[:, :, :], bank("st")[:, 0:32].rearrange("p (c b) -> p c b", c=RC)))
            dve.tensor_copy(caT, bank("st")[:, 32:128].rearrange("p (c b) -> p c b", c=RC)).then_inc(s_emV, 1)
            wait_full(dve, "cb")
            chain(dve.tensor_copy(cbT[:, 0:2, :], bank("cb")[:, 0:480].rearrange("p (c b) -> p c b", c=2)))
            dve.tensor_copy(cbT[:, 2:4, :], bank("cb")[:, 512:992].rearrange("p (c b) -> p c b", c=2)).then_inc(s_emV, 1)
            lam = par[:, PAR_AT["rg_lambda"]:PAR_AT["rg_lambda"] + RC]
            dve.wait_ge(s_c8e, 1)
            y, s, s2, acc = c8[:, 1, :], c8[:, 2, :], c8[:, 3, :], c8[:, 4, :]
            link(dve.tensor_scalar(s, y, 2.0, None, ALU.add))
            link(dve.reciprocal(s2, s))
            link(dve.tensor_tensor(s, y, s2, ALU.mult))
            link(dve.tensor_tensor(s2, s, s, ALU.mult))
            terms = 9
            link(dve.tensor_scalar(acc, s2, 1.0 / (2 * terms + 1), 1.0 / (2 * terms - 1), ALU.mult, ALU.add))
            for n in range(terms - 2, -1, -1):
                link(dve.tensor_tensor(acc, acc, s2, ALU.mult))
                link(dve.tensor_scalar(acc, acc, 1.0 / (2 * n + 1), None, ALU.add))
            link(dve.tensor_tensor(acc, acc, s, ALU.mult))
            link(dve.tensor_scalar(c8[:, 5, :], lam, -1.0, 0.0, ALU.mult, ALU.max))
            link(dve.scalar_tensor_tensor(c8[:, 6, :], acc, 2.0, c8[:, 5, :], ALU.mult, ALU.add))
            dve.tensor_scalar(c8[:, 7, :], c8[:, 6, :], -RG_C / 2, None, ALU.mult).then_inc(s_c8, 1)

            def mult_add(out, in0, w, in1):
                return dve.scalar_tensor_tensor(out, in0, w, in1, ALU.mult, ALU.add)

            def conv_sample(x, state, out, taps, wtap, wrow, bias, c):
                link(dve.tensor_scalar(out[:, c, SEQ:T], x[:, c, SEQ:T], wtap(taps - 1), bias, ALU.mult, ALU.add))
                pr = cprod[:, :, 0:taps - 1]
                link(dve.tensor_tensor(pr, state[:, c, :].rearrange("p (b j) -> p b j", b=NS), wrow, ALU.mult))
                link(dve.tensor_reduce(csum, pr, AX.X, ALU.add))
                return dve.tensor_tensor(out[:, c, SEQ:T], out[:, c, SEQ:T], csum, ALU.add)

            def conv_prompt(x, out, taps, wtap, bias, chunks):
                done = {}
                for c in chunks:
                    done[c] = chain(dve.tensor_scalar(out[:, c, 0:SEQ], x[:, c, 0:SEQ], wtap(c, taps - 1), bias(c),
                                                      ALU.mult, ALU.add))
                for s in range(1, taps):
                    for c in chunks:
                        dve.wait_ge(s_v, done[c])
                        done[c] = chain(mult_add(out[:, c, s:SEQ], x[:, c, 0:SEQ - s], wtap(c, taps - 1 - s),
                                                 out[:, c, s:SEQ]))
                dve.wait_ge(s_v, count[0])

            def wa_tap(c, j):
                return col("w_conv_a", j * RC + c)

            def wb_row(c):
                return wcb[:, c:(WB - 1) * RC:RC].unsqueeze(1).broadcast_to([P, NS, WB - 1])

            def wa_row(c):
                a = PAR_AT["w_conv_a"]
                return par[:, a + c:a + (WA - 1) * RC:RC].unsqueeze(1).broadcast_to([P, NS, WA - 1])

            wait_out(dve, "cb")
            for c in range(RC):
                wait_out(dve, f"zs{c}")
                dve.tensor_tensor(gluT[:, c, :], gluT[:, c, :], rT[:, c, :], ALU.mult).then_inc(s_glu, 1)
            dve.wait_ge(s_glu, RC)
            for c in range(RC):
                link(conv_sample(gluT, cbT, cT, WB, lambda j: wb_tap(c, j), wb_row(c), col("b_conv_b", c), c))
            conv_prompt(gluT, cT, WB, wb_tap, lambda c: col("b_conv_b", c), range(0, 2))
            for c in range(RC):
                wait_out(dve, f"zu{c}")
            for c in range(RC):
                link(conv_sample(uT, caT, ucT, WA, lambda j: wa_tap(c, j), wa_row(c), col("b_conv_a", c), c))
            conv_prompt(uT, ucT, WA, wa_tap, lambda c: col("b_conv_a", c), range(RC))
            dve.tensor_copy(csum[:, 0:1], csum[:, 0:1]).then_inc(s_uc, 1)
            conv_prompt(gluT, cT, WB, wb_tap, lambda c: col("b_conv_b", c), range(2, 3))
            dve.tensor_copy(csum[:, 0:1], csum[:, 0:1]).then_inc(s_convb, 1)

            done = {}
            th, a, b, d = ([m[:, c, :] for c in range(RC)] for m in (thT, rT, uT, ucT))
            for c in range(RC):
                wait_out(dve, f"ri{c}")
                done[c] = chain(dve.tensor_tensor(b[c], b[c], d[c], ALU.mult))

            def per_chunk(op):
                for c in range(RC):
                    dve.wait_ge(s_v, done[c])
                    done[c] = chain(op(c))

            for c in range(RC):
                dve.wait_ge(s_v, done[c])
                dve.wait_ge(s_tanh, c + 1)
                done[c] = chain(dve.tensor_scalar(d[c], th[c], -1.0, 1.0, ALU.mult, ALU.add))
            per_chunk(lambda c: dve.reciprocal(d[c], d[c]))
            per_chunk(lambda c: dve.scalar_tensor_tensor(a[c], th[c], 1.0, d[c], ALU.add, ALU.mult))
            per_chunk(lambda c: dve.tensor_tensor(th[c], th[c], d[c], ALU.mult))
            for c in range(RC):
                dve.wait_ge(s_v, done[c])
                dve.scalar_tensor_tensor(th[c], a[c], 1.0, th[c], ALU.add, ALU.mult).then_inc(s_srt, 1)

            def norm_mean(mean, x, n):
                wait_full(dve, mean)
                for k in range(n):
                    ins = dve.tensor_tensor(halves(x[:, k, :]), halves(x[:, k, :]), two(bank(mean)), ALU.subtract)
                    if k < n - 1:
                        ins.then_inc(s_sub, 1)
                    else:
                        ins.then_inc(s_emV, 1)
                        emptied(dve, GID[mean])
                        dve.sem_inc(s_sub, 1)

            def norm_scale(var, x, n):
                wait_out(dve, var)
                link(dve.reciprocal(rstd[:, :], rstd[:, :]))
                for k in range(n):
                    dve.tensor_tensor(x[:, k, :], x[:, k, :], rstd[:, :], ALU.mult).then_inc(s_nrm, 1)

            norm_mean("cmean", cT, RC)
            for c in range(RC):
                dve.wait_ge(s_root, c + 1)
                done[c] = chain(dve.tensor_tensor(b[c], b[c], th[c], ALU.mult))
            h = d
            per_chunk(lambda c: dve.tensor_tensor_scan(h[c][:, 0:SEQ], a[c][:, 0:SEQ], b[c][:, 0:SEQ], 0.0, ALU.mult, ALU.add))
            per_chunk(lambda c: dve.tensor_tensor(h[c][:, SEQ:T], a[c][:, SEQ:T], h0t[:, c, :], ALU.mult))
            for c in range(RC):
                dve.wait_ge(s_v, done[c])
                dve.tensor_tensor(h[c][:, SEQ:T], h[c][:, SEQ:T], b[c][:, SEQ:T], ALU.add).then_inc(s_h, 1)
            for c in range(RC):
                dve.wait_ge(s_h, c + 1)
                wait_out(dve, f"zg{c}")
                dve.tensor_tensor(gT[:, c, :], gT[:, c, :], h[c], ALU.mult).then_inc(s_ya, 1)
            norm_scale("cvar", cT, RC)
            wait_full(dve, "hlast")
            dve.wait_ge(s_tailout, 16 * 4)
            dve.tensor_copy(tail[0:9, 0, :], bank("hlast")[0:9, 0:512]).then_inc(s_emV, 1)

            def residual(name, k):
                wait_full(dve, name)
                dve.scalar_tensor_tensor(halves(xT[:, k, :]), halves(xT[:, k, :]), ALPHA, two(bank(name)),
                                         ALU.mult, ALU.add).then_inc(s_emV, 1)
                wait_out(dve, name)
                if k > 0:
                    first = xT[:, 0, :] if k == 1 else xsum[:, 0, :]
                    ins = dve.tensor_tensor(xsum[:, 0, :], first, xT[:, k, :], ALU.add)
                    if k < KC - 1:
                        link(ins)
                    else:
                        ins.then_inc(s_xsum, 1)

            for k in range(KC):
                residual(f"wo{k}", k)
            norm_mean("mean1", xT, KC)
            norm_scale("var1", xT, KC)

            def softmax_max(t):
                o = 8 * (t % 2)
                wait_full(dve, f"sc{t}")
                link(dve.tensor_reduce(small[:, o:o + 4], bank(f"sc{t}").rearrange("p (h m) -> p h m", h=XH), AX.X, ALU.max))
                dve.tensor_scalar(small[:, o + 4:o + 8], small[:, o:o + 4], -XD ** -0.5, None, ALU.mult).then_inc(s_smax, 1)

            def softmax_scale(t):
                so = 16 + 4 * (t % 2)
                wait_out(dve, f"sc{t}")
                dve.wait_ge(s_ssum, (XH - 1) * (t + 1))
                if t > 0:
                    dve.wait_ge(s_v, count[0])
                    dve.wait_ge(s_prob, t)
                link(dve.reciprocal(small[:, 27:31], small[:, so:so + 4]))
                for h in range(XH):
                    pr = probs[:, t % 2, h, :]
                    ins = dve.tensor_scalar(pr, pr, small[:, 27 + h:28 + h], None, ALU.mult)
                    if h < XH - 1:
                        chain(ins)
                ins.then_inc(s_prob, 1)

            def sample_scores(b):
                if b % 4 == 0:
                    dve.wait_ge(s_load[6 + b // 4], 16 * 4)
                if b % 2 == 0:
                    dve.wait_ge(s_qall[b // 2], 16 * 2)
                kc = cache(1 + b // 4, b % 4)
                for m in range(2):
                    for h in range(XH):
                        ins = dve.tensor_tensor_reduce(junk, kc[:, m, XD * h:XD * h + XD], q_all[:, b, XD * h:XD * h + XD],
                                                       1.0, 0.0, ALU.mult, ALU.add, ss[:, m, 4 * b + h:4 * b + h + 1])
                        if (m, h) != (1, XH - 1):
                            link(ins)
                ins.then_inc(s_ss, 1)
                dve.wait_ge(s_ss, b + 1)

            softmax_max(0)
            softmax_max(1)
            softmax_scale(0)
            softmax_max(2)
            softmax_scale(1)
            softmax_max(3)
            softmax_scale(2)
            softmax_scale(3)
            for b in range(NS):
                sample_scores(b)

            def half(ap, h):
                return ap[:, HALF * h:HALF * h + HALF]

            def half_residual(name, h):
                k = int(name[2])
                wait_full(dve, name)
                x = half(xT[:, k, :], h)
                dve.scalar_tensor_tensor(x, x, ALPHA, bank(name)[:, 0:HALF], ALU.mult, ALU.add).then_inc(s_emV, 1)
                wait_out(dve, name)
                if k > 0:
                    total = half(xsum[:, 0, :], h)
                    ins = dve.tensor_tensor(total, half(xT[:, 0, :], h) if k == 1 else total, x, ALU.add)
                    if k < KC - 1:
                        link(ins)
                    else:
                        ins.then_inc(s_xsum, 1)

            def half_center(name, h):
                wait_full(dve, name)
                for k in range(KC):
                    x = half(xT[:, k, :], h)
                    ins = dve.tensor_tensor(x, x, bank(name)[:, 0:HALF], ALU.subtract)
                    if k < KC - 1:
                        ins.then_inc(s_sub, 1)
                    else:
                        ins.then_inc(s_emV, 1)
                        wait_out(dve, name)
                        dve.sem_inc(s_sub, 1)

            def half_scale(name, h):
                wait_out(dve, name)
                link(dve.reciprocal(half(rstd[:, :], h), half(rstd[:, :], h)))
                for k in range(KC):
                    x = half(xT[:, k, :], h)
                    dve.tensor_tensor(x, x, half(rstd[:, :], h), ALU.mult).then_inc(s_nrm, 1)

            def gated(name, h):
                j = "ab".index(name[2])
                wait_full(dve, name)
                wait_out(dve, "h1" + name[2:])
                dve.tensor_tensor(half(shT[:, j, :], h), half(sh1[:, j, :], h), bank(name)[:, 0:HALF], ALU.mult).then_inc(s_emV, 1)

            half_residual("xa0", 0)
            half_residual("xa1", 0)
            wait_full(dve, "ssT")
            link(dve.tensor_reduce(small[0:32, 24:25], bank("ssT")[0:32, 0:N_MEM], AX.X, ALU.max))
            dve.tensor_scalar(small[0:32, 25:26], small[0:32, 24:25], -XD ** -0.5, None, ALU.mult).then_inc(s_smax, 1)
            wait_out(dve, "ssT")
            link(dve.reciprocal(small[0:32, 31:32], small[0:32, 26:27]))
            dve.tensor_scalar(sp, sp, small[0:32, 31:32], None, ALU.mult).then_inc(s_prob, 1)

            def weigh_values(b):
                dve.wait_ge(s_pv0, b + 1)
                v = value_cache(b)
                for h in range(XH):
                    at = 4 * b + h
                    ins = mult_add(v[:, 0, XD * h:XD * h + XD], v[:, 1, XD * h:XD * h + XD], sample_p[:, 1, at:at + 1],
                                   v[:, 0, XD * h:XD * h + XD])
                    if h < XH - 1:
                        chain(ins)
                ins.then_inc(s_pv, 1)

            half_residual("xa2", 0)
            half_residual("xa3", 0)
            for c in range(4, KC):
                weigh_values(c - 4)
                half_residual(f"xa{c}", 0)
            half_center("mean2a", 0)
            for b in range(4, NS):
                weigh_values(b)
            half_scale("var2a", 0)
            for c in range(KC):
                half_residual(f"xb{c}", 1)
            half_center("mean2b", 1)
            gated("h3a0", 0)
            half_scale("var2b", 1)

            dve.memset(R[0], 0.0).then_inc(s_rz, 1)
            dve.memset(place, -1.0).then_inc(s_late2, 1)
            dve.wait_ge(s_late2, 1)
            dve.wait_ge(s_rt, 16)
            dve.wait_ge(s_late, 9)
            wait_out(dve, "rtT")
            dve.wait_ge(s_ssum, (XH - 1) * 4 + 1)
            score, biased, sel, tmp, left = R[0], R[1], R[2], R[3], R[4]
            link(dve.tensor_tensor(biased, score, rbias.unsqueeze(1).broadcast_to([P, TT, E]), ALU.add))
            for t in range(TT):
                for g in range(8):
                    n = chain(dve.max(rmax[:, t, g, :], biased[:, t, 8 * g:8 * g + 8]))
            dve.wait_ge(s_v, n)
            link(dve.tensor_tensor(gscore, rmax[:, :, :, 0], rmax[:, :, :, 1], ALU.add))
            mine = gscore.unsqueeze(3).broadcast_to([P, TT, 8, 8])
            other = gscore.unsqueeze(2).broadcast_to([P, TT, 8, 8])
            link(dve.tensor_tensor(pair, other, mine, ALU.is_equal))
            link(dve.tensor_tensor(pair, pair, tri8.unsqueeze(1).broadcast_to([P, TT, 8, 8]), ALU.mult))
            link(dve.tensor_tensor(pair2, other, mine, ALU.is_gt))
            link(dve.tensor_tensor(pair, pair, pair2, ALU.add))
            link(dve.tensor_reduce(grank, pair, AX.X, ALU.add))
            link(dve.tensor_scalar(grank, grank, 4.0, None, ALU.is_lt))
            gated("h3b0", 0)
            gm = grank.unsqueeze(3).broadcast_to([P, TT, 8, 8])
            b4 = biased.rearrange("p t (g j) -> p t g j", g=8)
            t4 = tmp.rearrange("p t (g j) -> p t g j", g=8)
            link(dve.tensor_tensor(t4, b4, gm, ALU.mult))
            link(dve.tensor_scalar(grank, grank, 1.0, 1e30, ALU.subtract, ALU.mult))
            link(dve.tensor_tensor(t4, t4, gm, ALU.add))
            for t in range(TT):
                n = chain(dve.max(top8[:, t, :], tmp[:, t, :]))
            dve.wait_ge(s_v, n)
            for t in range(TT):
                n = chain(dve.match_replace(left[:, t, :], top8[:, t, :], tmp[:, t, :], -2e30))
            dve.wait_ge(s_v, n)
            link(dve.tensor_scalar(sel, left, -2e30, None, ALU.is_equal))
            link(dve.tensor_tensor(sel, sel, rmask.unsqueeze(2).broadcast_to([P, TT, E]), ALU.mult))
            dve.tensor_copy(sel_b, sel).then_inc(s_sel, 1)
            link(dve.tensor_tensor(tmp, score, sel, ALU.mult))
            link(dve.tensor_reduce(gsum, tmp, AX.X, ALU.add))
            link(dve.tensor_scalar(gsum, gsum, 1e-30, None, ALU.max))
            link(dve.reciprocal(gsum, gsum))
            link(dve.tensor_scalar(gsum, gsum, ROUTED_SCALE, None, ALU.mult))
            link(dve.tensor_tensor(tmp, tmp, gsum.unsqueeze(2).broadcast_to([P, TT, E]), ALU.mult))
            link(dve.tensor_copy(table[:, :, :, 3], tmp))
            link(dve.tensor_tensor(tmp, tmp, table[:, :, :, 3], ALU.subtract))
            link(dve.tensor_copy(table[:, :, :, 4], tmp))
            link(dve.tensor_tensor(table[:, :, :, 5], tmp, table[:, :, :, 4], ALU.subtract))
            link(dve.tensor_copy(table[:, :, :, 0], row8.unsqueeze(2).broadcast_to([P, TT, E])))
            link(dve.tensor_copy(table[:, :, :, 1], tile8.unsqueeze(2).broadcast_to([P, TT, E])))
            link(dve.memset(wsum, 1.0))
            for t in range(TT):
                n = chain(dve.tensor_tensor_scan(left[:, t, :], wsum, sel[:, t, :], 0.0, ALU.mult, ALU.add))
            dve.wait_ge(s_v, n)
            link(dve.tensor_scalar(table[:, :, :, 2], left, 1.0, None, ALU.subtract))

            gated("h3a1", 1)
            gated("h3b1", 1)
            wait_full(dve, "rank")
            link(dve.scalar_tensor_tensor(place[:, :, 0:E], bank("rank")[:, 0:TT * E].rearrange("p (t e) -> p t e", t=TT),
                                          1.0, sel, ALU.add, ALU.mult))
            dve.tensor_scalar(place[:, :, 0:E], place[:, :, 0:E], 1.0, None, ALU.subtract).then_inc(s_emV, 1)
            wait_full(dve, "count")
            dve.tensor_reduce(cmax, bank("count")[:, 0:E], AX.X, ALU.max).then_inc(s_emV, 1)
            wait_out(dve, "count")
            dve.tensor_copy(over[:, :], cmax).then_inc(s_over, 1)
            wait_out(dve, "rank")
            dve.sem_inc(s_table, 1)

            def shared_sum(t):
                w = width(t)
                wait_full(dve, f"so{t}")
                wait_out(dve, f"x2{t}")
                dve.wait_ge(s_x2out, 16 * TT)
                dve.scalar_tensor_tensor(base[0:w, t, :], base[0:w, t, :], ALPHA, bank(f"so{t}")[0:w, :],
                                         ALU.mult, ALU.add).then_inc(s_emV, 1)

            def oh(n, e, numbers):
                return dve.tensor_tensor(onehot[:, n % 2, :, :], place[:, :, bass.ds(e, 1)].broadcast_to([P, TT, CAP]),
                                         numbers.unsqueeze(1).broadcast_to([P, TT, CAP]), ALU.is_equal)

            def indices(n, s, base_count):
                at = 512 * (n % 2)
                dve.tensor_reduce(picked[0:CAP, n, :], psum[0:CAP, 3, at:at + 6].rearrange("p (v c) -> p v c", v=2), AX.X,
                                  ALU.add).then_inc(s, 1)
                dve.wait_ge(s, base_count + 1)
                dve.tensor_scalar(idx_y[0:CAP, n:n + 1], picked[0:CAP, n, 0:1], FAR, None, ALU.add).then_inc(s, 1)
                dve.wait_ge(s, base_count + 2)
                return dve.tensor_scalar(idx_x[0:CAP, n:n + 1], idx_y[0:CAP, n:n + 1], 3, None, ALU.logical_shift_right)

            def hd(b):
                return dve.tensor_tensor(hidT[:, b, :], silu[:, b, :], psum[:, 2, 512 * b + 2 * CAP:512 * b + 4 * CAP], ALU.mult)

            def yh(b, n):
                return dve.tensor_scalar(ys[0:CAP, b, 512:1024], psum[0:CAP, 0, 512:1024], picked[0:CAP, n, 1:2], None, ALU.mult)

            def oh_step(e, n):
                if at_least(e, 2):
                    dve.wait_ge(m_ip, e - 1)
                oh(n, e, slots).then_inc(m_oh, 1)

            def i_step(e, n, sc):
                dve.wait_ge(m_ip, e + 1)
                if sc is not None:
                    dve.wait_ge(m_s[n % 2], sc)
                indices(n, m_iv, 2 * e).then_inc(m_idx, 1)

            def c_step(e, n):
                dve.wait_ge(m_sl, e + 1)
                if at_least(e, 2):
                    dve.wait_ge(m_y, e - 1)
                hd(n % 2).then_inc(m_hd, 1)

            def y_step(e, n, sc):
                dve.wait_ge(m_y, e + 1)
                if sc is not None:
                    dve.wait_ge(m_s[n % 2], sc)
                yh(n % 2, n).then_inc(m_yv, 1)

            oh_step(0, 0)
            oh_step(1, 1)
            i_step(0, 0, None)
            oh_step(2, 2)
            i_step(1, 1, None)
            oh_step(3, 3)
            shared_sum(0)
            shared_sum(1)
            i_step(2, 2, None)
            oh_step(4, 4)
            shared_sum(2)
            i_step(3, 3, None)
            oh_step(5, 5)
            shared_sum(3)
            shared_sum(4)
            c_step(0, 0)

            def step(e, k, i, sc, si):
                c_step(e, k % NB)
                y_step(e - 1, (k - 1) % NB, sc)
                if exists(e + 3):
                    i_step(e + 3, (k + 3) % NB, si)
                if exists(e + 5):
                    oh_step(e + 5, (k + 5) % NB)

            LAST = E // NB - 1
            for k in range(1, NB + 1):
                step(k, k, 0, None if k <= 2 else 16 * ((k - 1) // 2), None if k < 5 else 16 * ((k - 5) // 2 + 1))
            with dve.Fori(1, LAST) as i:
                for k in range(1, NB + 1):
                    step(NB * i + k, k, i, 16 * (NB // 2) * i + 16 * ((k - 1) // 2),
                         16 * (NB // 2) * i + 16 * ((k - 5) // 2 + 1))
            for k in range(1, NB):
                e = NB * LAST + k
                step(e, k, LAST, 16 * ((e - 1) // 2), 16 * ((e - 5) // 2 + 1))
            y_step(E - 1, NB - 1, 16 * ((E - 1) // 2))

            dve.wait_ge(s_over, 1)
            n_max = dve.value_load(over[0:1, 0:1], min_val=0, max_val=T)
            with dve.If(n_max > CAP):
                dve.wait_ge(m_s[0], 16 * (E // 2))
                dve.wait_ge(m_s[1], 16 * (E // 2))
                dve.wait_ge(m_g[0], 16 * (E // 4))
                dve.wait_ge(m_ip, E)
                dve.wait_ge(s_late, 10)
                with dve.Fori(1, E * (ROUNDS - 1) + 1) as turn_i:
                    dve.wait_ge(f_sem["it"], turn_i)
                    i = turn_i - 1
                    link_r = dve.tensor_scalar(slots_r, slots, rounds_t[:, bass.ds(i // E, 1)], None, ALU.add)
                    link_r.then_inc(f_sem["iv"], 1)
                    dve.wait_ge(f_sem["iv"], 3 * i + 1)
                    oh(0, i % E, slots_r).then_inc(f_sem["oh"], 1)
                    dve.wait_ge(f_sem["ip"], i + 1)
                    indices(0, f_sem["iv"], 3 * i + 1).then_inc(f_sem["idx"], 1)
                    dve.wait_ge(f_sem["sl"], i + 1)
                    hd(0).then_inc(f_sem["hd"], 1)
                    dve.wait_ge(f_sem["y"], i + 1)
                    yh(0, 0).then_inc(f_sem["yv"], 1)

            dve.wait_ge(s_lnw, 32)
            for m, t in enumerate(LAST_ORDER):
                w = width(t)
                x = base[0:w, t, :]
                for q in range(len(PARTS)):
                    if q == 3 and w == P:
                        dve.wait_ge(s_ysum, m)
                        link(dve.tensor_tensor(x, x, psum[0:w, m % 4, :], ALU.add))
                    if q == 0:
                        dve.wait_ge(s_ypool, 2 * (m + 1))
                    else:
                        dve.wait_ge(s_yin[q][m % 3], 16 * (m // 3 + 1))
                    for j in (DVE_ROWS if w == P else SMALL_ROWS)[q]:
                        ins = dve.tensor_tensor(x, x, y_in[m % 3][0:w, j, :], ALU.add)
                        if j < TOPK - 1:
                            link(ins)
                ins.then_inc(s_rowv, 1)
                dve.wait_ge(s_rowv, m + 1)
                for n in range(2):
                    link(dve.bn_stats(st6[0:w, n, :], base[0:w, t, 512 * n:512 * n + 512]))
                dve.bn_aggr(small[0:w, 34:36], st6[0:w, :, :]).then_inc(s_var, 1)
                dve.wait_ge(s_var, m + 1)
                dve.wait_ge(s_sd, m + 1)
                link(dve.reciprocal(small[0:w, 37:38], small[0:w, 36:37]))
                link(dve.scalar_tensor_tensor(x, x, small[0:w, 34:35], ln3g[0:w, :], ALU.subtract, ALU.mult))
                dve.scalar_tensor_tensor(x, x, small[0:w, 37:38], ln3b[0:w, :], ALU.mult, ALU.add).then_inc(s_res, 1)


_INS = ['x_prompt', 'x_sample', 'mem_prompt', 'state_rglru_h', 'state_rglru_conv', 'state_dwconv', 'cache_mem_k',
        'cache_mem_v', 'w_in', 'b_in', 'w_conv_a', 'b_conv_a', 'w_rg_a', 'b_rg_a', 'w_rg_x', 'b_rg_x', 'rg_lambda',
        'w_conv_b', 'b_conv_b', 'ln_c_g', 'ln_c_b', 'w_out', 'ln1_g', 'ln1_b', 'w_q', 'w_k', 'w_v', 'w_o', 'ln2_g',
        'ln2_b', 'w_router', 'router_bias', 'w1_e', 'w3_e', 'w2_e', 'w1_s', 'w3_s', 'w2_s', 'ln3_g', 'ln3_b']
_OUTS = [(1, 512, 1024), (8, 1, 1024), (1, 1, 512), (1, 1, 3, 512), (1, 1, 30, 512), (1, 1, 256, 4, 256),
         (1, 1, 256, 4, 256), (1, 8, 512), (1, 8, 3, 512), (1, 8, 30, 512)]


def kernel(**inputs):
    import numpy as _np
    import concourse.bacc as _bacc
    from concourse import mybir as _mybir
    from concourse.bass_utils import run_bass_kernel_spmd as _run

    nc = _bacc.Bacc("TRN2", target_bir_lowering=False, num_devices=1)
    arrays, ins = {}, {}
    for name in _INS:
        a = _np.ascontiguousarray(inputs[name])
        arrays[f"in_{name}_dram"] = a
        ins[name] = nc.dram_tensor(f"in_{name}_dram", a.shape, _mybir.dt.from_np(a.dtype), kind="ExternalInput").ap()
    outs = [nc.dram_tensor(f"out_{i}_dram", shape, _mybir.dt.float32, kind="ExternalOutput").ap()
            for i, shape in enumerate(_OUTS)]
    decoder_step(nc, ins, outs)
    r = _run(nc, [arrays], core_ids=[0])
    return tuple(r.results[0][f"out_{i}_dram"] for i in range(len(_OUTS)))
```
